# Optimizing a Trainium2 kernel written in Bass

```python
import jax, jax.numpy as jnp
from jax import lax
import numpy as np
import math

D_MODEL = 1024
BATCH = 1
SEQ = 256
DEPTH = 2

N_A_LAYERS = DEPTH // 2
N_B_LAYERS = DEPTH - N_A_LAYERS
N_META = 16
EPS = 1e-6
NEG_INF = -1e30

D_FF = 2816

GLA_HEADS = 4
GLA_DK = D_MODEL // 2 // GLA_HEADS
GLA_DV = D_MODEL // GLA_HEADS
GLA_QK = GLA_HEADS * GLA_DK
GLA_V = GLA_HEADS * GLA_DV
GLA_RANK = 16
GLA_TAU = 16.0
GLA_IN = 2 * GLA_QK + 2 * GLA_V + GLA_RANK
CHUNK = 64

N_Q_HEADS = 16
N_KV_HEADS = 4
HEAD_DIM = 64
GROUP = N_Q_HEADS // N_KV_HEADS
WINDOW = 128
ROT_DIM = HEAD_DIM // 4
ROPE_THETA = 500000.0


def rmsnorm(x, g):
    xf = x.astype(jnp.float32)
    y = xf * lax.rsqrt(jnp.mean(xf * xf, axis=-1, keepdims=True) + EPS)
    return (y * g.astype(jnp.float32)).astype(x.dtype)

def swiglu(x, w_in, w_out):
    gate, up = jnp.split(x @ w_in, 2, axis=-1)
    return (jax.nn.silu(gate) * up) @ w_out

def rope_tables(length):
    inv_freq = ROPE_THETA ** (-jnp.arange(0, ROT_DIM, 2, dtype=jnp.float32) / ROT_DIM)
    ang = jnp.arange(length, dtype=jnp.float32)[:, None] * inv_freq[None, :]
    return jnp.cos(ang), jnp.sin(ang)

def apply_partial_rope(x, cos, sin):
    half = ROT_DIM // 2
    shape = (cos.shape[0],) + (1,) * (x.ndim - 3) + (half,)
    c, s = cos.reshape(shape), sin.reshape(shape)
    x1 = x[..., :half].astype(jnp.float32)
    x2 = x[..., half:ROT_DIM].astype(jnp.float32)
    return jnp.concatenate([(x1 * c - x2 * s).astype(x.dtype), (x2 * c + x1 * s).astype(x.dtype),
                            x[..., ROT_DIM:]], axis=-1)

def gla_mixer(hn, w_in, w_gate, b_gate, g_head, w_out):
    B, L, _ = hn.shape
    q, k, v, r, lr = jnp.split(hn @ w_in, [GLA_QK, 2 * GLA_QK, 2 * GLA_QK + GLA_V, 2 * GLA_QK + 2 * GLA_V], axis=-1)
    gk = jax.nn.log_sigmoid((lr @ w_gate + b_gate).astype(jnp.float32)) / GLA_TAU
    pad = CHUNK - N_META
    padf = lambda t: jnp.pad(t, ((0, 0), (pad, 0), (0, 0)))
    Lp = L + pad
    nC = Lp // CHUNK
    def chunks(t, d):
        return t.reshape(B, nC, CHUNK, GLA_HEADS, d).transpose(0, 3, 1, 2, 4)
    qf = chunks(padf(q).astype(jnp.float32), GLA_DK) * (GLA_DK ** -0.5)
    kf = chunks(padf(k).astype(jnp.float32), GLA_DK)
    vf = chunks(padf(v).astype(jnp.float32), GLA_DV)
    bcum = jnp.cumsum(chunks(padf(gk), GLA_DK), axis=3)
    q_dec = qf * jnp.exp(bcum)
    k_dec = kf * jnp.exp(-bcum)
    causal = jnp.tril(jnp.ones((CHUNK, CHUNK), dtype=bool))
    att = jnp.where(causal, jnp.einsum('bhncd,bhnsd->bhncs', q_dec, k_dec), 0.0)
    o_intra = jnp.einsum('bhncs,bhnsv->bhncv', att, vf)
    b_last = bcum[:, :, :, -1:, :]
    chunk_kv = jnp.einsum('bhnsd,bhnsv->bhndv', kf * jnp.exp(b_last - bcum), vf)
    decay = jnp.exp(b_last[:, :, :, 0, :])

    def step(S, inp):
        kv_c, dec_c = inp
        return dec_c[..., None] * S + kv_c, S
    S0 = jnp.zeros((B, GLA_HEADS, GLA_DK, GLA_DV), jnp.float32)
    _, states = lax.scan(step, S0, (jnp.moveaxis(chunk_kv, 2, 0), jnp.moveaxis(decay, 2, 0)))
    states = jnp.moveaxis(states, 0, 2)
    o = o_intra + jnp.einsum('bhncd,bhndv->bhncv', q_dec, states)
    o = o.reshape(B, GLA_HEADS, Lp, GLA_DV)[:, :, pad:].transpose(0, 2, 1, 3)
    o = rmsnorm(o, g_head) * jax.nn.silu(r.astype(jnp.float32)).reshape(B, L, GLA_HEADS, GLA_DV)
    return o.reshape(B, L, GLA_V).astype(hn.dtype) @ w_out

def shared_kv(h, g_kv, w_kv, cos, sin):
    B, L, _ = h.shape
    k, v = jnp.split(rmsnorm(h, g_kv) @ w_kv, 2, axis=-1)
    k = apply_partial_rope(k.reshape(B, L, N_KV_HEADS, HEAD_DIM), cos, sin)
    v = v.reshape(B, L, N_KV_HEADS, HEAD_DIM)
    return k.transpose(0, 2, 1, 3), v.transpose(0, 2, 1, 3)

def sink_softmax(s, mask, sink):
    s = jnp.where(mask, s.astype(jnp.float32), NEG_INF)
    m = jnp.maximum(jnp.max(s, axis=-1, keepdims=True), sink)
    p = jnp.exp(s - m)
    return p / (jnp.sum(p, axis=-1, keepdims=True) + jnp.exp(sink - m))

def swa_mixer(hn, w_q, sinks, w_out, k, v, cos, sin):
    B, L, _ = hn.shape
    S = L - N_META
    nB = S // WINDOW
    q = (hn @ w_q).reshape(B, L, N_KV_HEADS, GROUP, HEAD_DIM)
    q = (apply_partial_rope(q, cos, sin) * (HEAD_DIM ** -0.5)).transpose(0, 2, 3, 1, 4)
    sink_b = sinks.reshape(N_KV_HEADS, GROUP).astype(jnp.float32)
    k_meta, v_meta = k[:, :, :N_META], v[:, :, :N_META]
    s_meta = jnp.einsum('bkgqd,bkmd->bkgqm', q[:, :, :, :N_META], k_meta)
    p_meta = sink_softmax(s_meta, jnp.tril(jnp.ones((N_META, N_META), dtype=bool)), sink_b[None, :, :, None, None])
    o_meta = jnp.einsum('bkgqm,bkmd->bkgqd', p_meta.astype(v.dtype), v_meta)
    q_blk = q[:, :, :, N_META:].reshape(B, N_KV_HEADS, GROUP, nB, WINDOW, HEAD_DIM)
    def band(t):
        t_meta = t[:, :, :N_META]
        t_blk = t[:, :, N_META:].reshape(B, N_KV_HEADS, nB, WINDOW, HEAD_DIM)
        prev = jnp.concatenate([jnp.zeros_like(t_blk[:, :, :1]), t_blk[:, :, :-1]], axis=2)
        meta = jnp.broadcast_to(t_meta[:, :, None], (B, N_KV_HEADS, nB, N_META, HEAD_DIM))
        return jnp.concatenate([meta, prev, t_blk], axis=3)
    k_band, v_band = band(k), band(v)
    s = jnp.einsum('bkgnqd,bknsd->bkgnqs', q_blk, k_band)
    i = jnp.arange(WINDOW)[:, None]
    j = jnp.arange(WINDOW)[None, :]
    blk = jnp.arange(nB)[:, None, None]
    mask = jnp.concatenate([
        jnp.ones((nB, WINDOW, N_META), dtype=bool),
        (j > i)[None] & (blk > 0),
        jnp.broadcast_to((j <= i)[None], (nB, WINDOW, WINDOW)),
    ], axis=-1)
    p = sink_softmax(s, mask, sink_b[None, :, :, None, None, None])
    o_real = jnp.einsum('bkgnqs,bknsd->bkgnqd', p.astype(v.dtype), v_band).reshape(B, N_KV_HEADS, GROUP, S, HEAD_DIM)
    o = jnp.concatenate([o_meta, o_real], axis=3).transpose(0, 3, 1, 2, 4).reshape(B, L, N_Q_HEADS * HEAD_DIM)
    return o @ w_out

def first_inputs(seed: int = 0) -> dict:
    key = jax.random.key(seed)
    ks = jax.random.split(key, 16)
    nrm = lambda k, shape, fan_in: jax.random.normal(k, shape, jnp.float32) * (fan_in ** -0.5)
    return {
        "x": jax.random.normal(ks[0], (BATCH, SEQ, D_MODEL), jnp.float32),
        "meta_tokens": jax.random.normal(ks[1], (N_META, D_MODEL), jnp.float32),
        "norm_gains": 1.0 + 0.02 * jax.random.normal(ks[2], (DEPTH, 6, D_MODEL), jnp.float32),
        "w_ffn_in": nrm(ks[3], (DEPTH, 2, D_MODEL, 2 * D_FF), D_MODEL),
        "w_ffn_out": nrm(ks[4], (DEPTH, 2, D_FF, D_MODEL), D_FF),
        "gla_w_in": nrm(ks[5], (N_A_LAYERS, D_MODEL, GLA_IN), D_MODEL),
        "gla_w_gate": nrm(ks[6], (N_A_LAYERS, GLA_RANK, GLA_QK), GLA_RANK),
        "gla_b_gate": 0.1 * jax.random.normal(ks[7], (N_A_LAYERS, GLA_QK), jnp.float32),
        "gla_norm": 1.0 + 0.02 * jax.random.normal(ks[8], (N_A_LAYERS, GLA_DV), jnp.float32),
        "gla_w_out": nrm(ks[9], (N_A_LAYERS, GLA_V, D_MODEL), GLA_V),
        "kv_norm": 1.0 + 0.02 * jax.random.normal(ks[10], (D_MODEL,), jnp.float32),
        "w_kv": nrm(ks[11], (D_MODEL, 2 * N_KV_HEADS * HEAD_DIM), D_MODEL),
        "swa_w_q": nrm(ks[12], (N_B_LAYERS, D_MODEL, N_Q_HEADS * HEAD_DIM), D_MODEL),
        "swa_sinks": 0.5 * jax.random.normal(ks[13], (N_B_LAYERS, N_Q_HEADS), jnp.float32),
        "swa_w_out": nrm(ks[14], (N_B_LAYERS, N_Q_HEADS * HEAD_DIM, D_MODEL), N_Q_HEADS * HEAD_DIM),
    }

def first_block(x, meta_tokens, norm_gains, w_ffn_in, w_ffn_out, gla_w_in, gla_w_gate, gla_b_gate, gla_norm,
              gla_w_out, kv_norm, w_kv, swa_w_q, swa_sinks, swa_w_out):
    B = x.shape[0]
    meta = jnp.broadcast_to(meta_tokens.astype(x.dtype)[None], (B, N_META, D_MODEL))
    h = jnp.concatenate([meta, x], axis=1)
    cos, sin = rope_tables(h.shape[1])
    k_sh, v_sh = None, None
    for layer in range(DEPTH):
        g = norm_gains[layer]
        h = h + 0.5 * rmsnorm(swiglu(rmsnorm(h, g[0]), w_ffn_in[layer, 0], w_ffn_out[layer, 0]), g[1])
        hn = rmsnorm(h, g[2])
        if layer < N_A_LAYERS:
            a = layer
            mix = gla_mixer(hn, gla_w_in[a], gla_w_gate[a], gla_b_gate[a], gla_norm[a], gla_w_out[a])
        else:
            b = layer - N_A_LAYERS
            mix = swa_mixer(hn, swa_w_q[b], swa_sinks[b], swa_w_out[b], k_sh, v_sh, cos, sin)
        h = h + rmsnorm(mix, g[3])
        h = h + 0.5 * rmsnorm(swiglu(rmsnorm(h, g[4]), w_ffn_in[layer, 1], w_ffn_out[layer, 1]), g[5])
        if layer == N_A_LAYERS - 1:
            k_sh, v_sh = shared_kv(h, kv_norm, w_kv, cos, sin)
    return h[:, N_META:]


DEPTH_2 = 1

HG_HEADS = 4
HG_DK = 128
HG_DV = 128
HG_KEY_WIDTH = HG_HEADS * HG_DK
HG_WIDTH = HG_HEADS * HG_DV
HG_CHUNK = 64

MB_HEADS = 8
MB_DH = 64
MB_WIDTH = MB_HEADS * MB_DH
MB_BLOCK = 256
MB_TOPK = 3
MB_QCHUNK = 16

REL_BUCKETS = 32
REL_MAX_DIST = 128

N_GROUPS = 4
EXPERTS_PER_GROUP = 8
N_EXPERTS = N_GROUPS * EXPERTS_PER_GROUP
TOP_K = 2
EXPERT_HIDDEN = 512
MOE_BLOCK = 128

DN_ALPHA = (2.0 * DEPTH_2) ** 0.25
DN_BETA = (8.0 * DEPTH_2) ** -0.25
NORM_EPS = 1e-5

IN_SIZES = (HG_KEY_WIDTH, HG_KEY_WIDTH, HG_WIDTH, HG_WIDTH, MB_WIDTH, MB_WIDTH, MB_WIDTH, D_MODEL, D_MODEL)
IN_COLS = sum(IN_SIZES)


def layer_norm(x, g, b):
    xf = x.astype(jnp.float32)
    mu = jnp.mean(xf, axis=-1, keepdims=True)
    xc = xf - mu
    var = jnp.mean(xc * xc, axis=-1, keepdims=True)
    return (xc * lax.rsqrt(var + NORM_EPS) * g.astype(jnp.float32) + b.astype(jnp.float32)).astype(x.dtype)

def hgrn2_mixer(q, f_logit, i, g, lb, norm_g):
    B, S, _ = q.shape
    nc = S // HG_CHUNK
    f32 = jnp.float32
    lb = lb.astype(f32)
    z = f_logit.astype(f32)
    log_f = jnp.log(lb + (1.0 - lb) * jax.nn.sigmoid(z))
    k = (1.0 - lb) * jax.nn.sigmoid(-z)
    qf = jax.nn.silu(q.astype(f32))
    vf = i.astype(f32)

    def to_chunks(t, dh):
        return t.reshape(B, nc, HG_CHUNK, HG_HEADS, dh).transpose(1, 0, 3, 2, 4)

    causal = jnp.tril(jnp.ones((HG_CHUNK, HG_CHUNK), dtype=bool))

    def chunk_step(state, inp):
        qc, kc, vc, lfc = inp
        b = jnp.cumsum(lfc, axis=2)
        o_inter = jnp.einsum('bhtk,bhkv->bhtv', qc * jnp.exp(b), state)
        rel = b[:, :, :, None, :] - b[:, :, None, :, :]
        decay = jnp.exp(jnp.where(causal[:, :, None], rel, -jnp.inf))
        scores = jnp.einsum('bhtk,bhtsk,bhsk->bhts', qc, decay, kc)
        o_intra = jnp.einsum('bhts,bhsv->bhtv', scores, vc)
        b_end = b[:, :, -1:, :]
        state = (jnp.exp(b_end[:, :, 0, :])[..., None] * state
                 + jnp.einsum('bhsk,bhsv->bhkv', kc * jnp.exp(b_end - b), vc))
        return state, o_inter + o_intra

    s0 = jnp.zeros((B, HG_HEADS, HG_DK, HG_DV), f32)
    _, o = lax.scan(chunk_step, s0, (to_chunks(qf, HG_DK), to_chunks(k, HG_DK),
                                     to_chunks(vf, HG_DV), to_chunks(log_f, HG_DK)))
    o = o.transpose(1, 0, 3, 2, 4).reshape(B, S, HG_HEADS, HG_DV)
    o = o * lax.rsqrt(jnp.mean(o * o, axis=-1, keepdims=True) + NORM_EPS)
    o = o.reshape(B, S, HG_WIDTH) * norm_g.astype(f32) * jax.nn.silu(g.astype(f32))
    return o.astype(q.dtype)

def t5_bucket(dist):
    max_exact = REL_BUCKETS // 2
    d = jnp.maximum(dist, 1).astype(jnp.float32)
    log_part = max_exact + (jnp.log(d / max_exact) / math.log(REL_MAX_DIST / max_exact)
                            * (REL_BUCKETS - max_exact)).astype(jnp.int32)
    return jnp.where(dist < max_exact, dist, jnp.minimum(log_part, REL_BUCKETS - 1))

def moba_mixer(q, k, v, rel_bias):
    B, S, _ = q.shape
    f32 = jnp.float32
    nb = -(-S // MB_BLOCK)
    s_pad = nb * MB_BLOCK
    k_sel = min(MB_TOPK, nb)
    scale = MB_DH ** -0.5

    def to_heads(t):
        t = jnp.pad(t, ((0, 0), (0, s_pad - S), (0, 0)))
        return t.reshape(B, s_pad, MB_HEADS, MB_DH).transpose(0, 2, 1, 3)

    qh, kh, vh = to_heads(q), to_heads(k), to_heads(v)
    kb = kh.reshape(B, MB_HEADS, nb, MB_BLOCK, MB_DH)
    vb = vh.reshape(B, MB_HEADS, nb, MB_BLOCK, MB_DH)
    k_mean = jnp.mean(kb, axis=3)
    gate = jnp.einsum('bhsd,bhnd->bhsn', qh, k_mean).astype(f32)
    pos = jnp.arange(s_pad)
    fully_past = jnp.arange(nb)[None, :] < (pos // MB_BLOCK)[:, None]
    gate = jnp.where(fully_past, gate, -jnp.inf)
    top_val, top_idx = lax.top_k(gate, k_sel)
    top_ok = jnp.isfinite(top_val)

    rb = rel_bias.astype(f32).T
    b_ix = jnp.arange(B)[:, None, None, None]
    h_ix = jnp.arange(MB_HEADS)[None, :, None, None]

    def attend(c):
        t0 = c * MB_QCHUNK
        tq = t0 + jnp.arange(MB_QCHUNK)
        qc = lax.dynamic_slice_in_dim(qh, t0, MB_QCHUNK, axis=2)
        idx = lax.dynamic_slice_in_dim(top_idx, t0, MB_QCHUNK, axis=2)
        ok = lax.dynamic_slice_in_dim(top_ok, t0, MB_QCHUNK, axis=2)
        kg = kb[b_ix, h_ix, idx]
        vg = vb[b_ix, h_ix, idx]
        kpos = idx[..., None] * MB_BLOCK + jnp.arange(MB_BLOCK)
        bucket = t5_bucket(tq[None, None, :, None, None] - kpos)
        s_past = (jnp.einsum('bhqd,bhqjkd->bhqjk', qc, kg).astype(f32) * scale
                  + rb[h_ix[..., None], bucket])
        s_past = jnp.where(ok[..., None], s_past, -jnp.inf).reshape(B, MB_HEADS, MB_QCHUNK, k_sel * MB_BLOCK)
        j0 = (t0 // MB_BLOCK) * MB_BLOCK
        k_own = lax.dynamic_slice_in_dim(kh, j0, MB_BLOCK, axis=2)
        v_own = lax.dynamic_slice_in_dim(vh, j0, MB_BLOCK, axis=2)
        dist_own = tq[:, None] - (j0 + jnp.arange(MB_BLOCK))[None, :]
        s_own = (jnp.einsum('bhqd,bhkd->bhqk', qc, k_own).astype(f32) * scale
                 + rb[:, t5_bucket(jnp.maximum(dist_own, 0))])
        s_own = jnp.where(dist_own >= 0, s_own, -jnp.inf)
        p = jax.nn.softmax(jnp.concatenate([s_past, s_own], axis=-1), axis=-1)
        p_past = p[..., :k_sel * MB_BLOCK].reshape(B, MB_HEADS, MB_QCHUNK, k_sel, MB_BLOCK).astype(vg.dtype)
        p_own = p[..., k_sel * MB_BLOCK:].astype(v_own.dtype)
        return (jnp.einsum('bhqjk,bhqjkd->bhqd', p_past, vg)
                + jnp.einsum('bhqk,bhkd->bhqd', p_own, v_own))

    o = lax.map(attend, jnp.arange(s_pad // MB_QCHUNK))
    o = o.transpose(1, 0, 3, 2, 4).reshape(B, s_pad, MB_WIDTH)[:, :S]
    return o

def hier_moe(x, w_group, b_group, w_expert, b_expert, w_gate_up, w_down):
    B, S, D = x.shape
    n_tok = B * S
    n_asg = n_tok * TOP_K
    f32 = jnp.float32
    xt = x.reshape(n_tok, D)
    g_logits = (xt @ w_group + b_group).astype(f32)
    grp = jnp.argmax(g_logits, axis=-1)
    p_grp = jnp.take_along_axis(jax.nn.softmax(g_logits, axis=-1), grp[:, None], axis=1)
    e_logits = (xt @ w_expert + b_expert).astype(f32).reshape(n_tok, N_GROUPS, EXPERTS_PER_GROUP)
    e_in_grp = jnp.take_along_axis(e_logits, grp[:, None, None], axis=1)[:, 0]
    top_v, top_i = lax.top_k(e_in_grp, TOP_K)
    weights = (jax.nn.softmax(top_v, axis=-1) * p_grp).reshape(n_asg)
    expert = (grp[:, None] * EXPERTS_PER_GROUP + top_i).reshape(n_asg)
    token = jnp.repeat(jnp.arange(n_tok), TOP_K)
    order = jnp.argsort(expert)
    e_s, tok_s, w_s = expert[order], token[order], weights[order]
    counts = jax.ops.segment_sum(jnp.ones((n_asg,), jnp.int32), expert, num_segments=N_EXPERTS)
    starts = jnp.cumsum(counts) - counts
    padded = (counts + MOE_BLOCK - 1) // MOE_BLOCK * MOE_BLOCK
    pad_end = jnp.cumsum(padded)
    pad_start = pad_end - padded
    dest = pad_start[e_s] + jnp.arange(n_asg) - starts[e_s]
    n_blk = -(-n_asg // MOE_BLOCK) + N_EXPERTS
    n_rows = n_blk * MOE_BLOCK
    x_buf = jnp.zeros((n_rows, D), x.dtype).at[dest].set(xt[tok_s])
    blk_expert = jnp.minimum(jnp.searchsorted(pad_end, jnp.arange(n_blk) * MOE_BLOCK, side='right'),
                             N_EXPERTS - 1)

    def expert_block(args):
        xb, e = args
        gate, up = jnp.split(xb @ w_gate_up[e], 2, axis=-1)
        return (jax.nn.silu(gate) * up) @ w_down[e]

    y_buf = lax.map(expert_block, (x_buf.reshape(n_blk, MOE_BLOCK, D), blk_expert)).reshape(n_rows, D)
    y = jnp.zeros((n_tok, D), x.dtype).at[tok_s].add(y_buf[dest] * w_s[:, None].astype(x.dtype))
    return y.reshape(B, S, D)

def second_inputs(seed: int = 0) -> dict:
    key = jax.random.key(seed)
    ks = jax.random.split(key, 20)
    f32 = jnp.float32
    L = DEPTH_2

    def normal(k, shape, std):
        return jax.random.normal(k, shape, f32) * std

    col_scale = jnp.concatenate([jnp.full((n,), s, f32) for n, s in
                                 zip(IN_SIZES, (1.0, 1.0, DN_BETA, 1.0, 1.0, 1.0, DN_BETA, 1.0, 1.0))])
    return {
        'x': normal(ks[0], (BATCH, SEQ, D_MODEL), 1.0),
        'w_in': normal(ks[1], (L, D_MODEL, IN_COLS), D_MODEL ** -0.5) * col_scale,
        'b_in': normal(ks[2], (L, IN_COLS), 0.02),
        'lb_logits': normal(ks[3], (L + 1, HG_KEY_WIDTH), 0.5),
        'hg_norm_g': 1.0 + normal(ks[4], (L, HG_WIDTH), 0.1),
        'rel_bias': normal(ks[5], (REL_BUCKETS, MB_HEADS), 0.5),
        'w_proj_a': normal(ks[6], (L, HG_WIDTH, D_MODEL), DN_BETA * HG_WIDTH ** -0.5),
        'w_proj_b': normal(ks[7], (L, MB_WIDTH, D_MODEL), DN_BETA * MB_WIDTH ** -0.5),
        'w_out': normal(ks[8], (L, D_MODEL, D_MODEL), DN_BETA * D_MODEL ** -0.5),
        'ln1_g': 1.0 + normal(ks[9], (L, D_MODEL), 0.1),
        'ln1_b': normal(ks[10], (L, D_MODEL), 0.02),
        'w_group': normal(ks[11], (L, D_MODEL, N_GROUPS), D_MODEL ** -0.5),
        'b_group': normal(ks[12], (L, N_GROUPS), 0.01),
        'w_expert': normal(ks[13], (L, D_MODEL, N_EXPERTS), D_MODEL ** -0.5),
        'b_expert': normal(ks[14], (L, N_EXPERTS), 0.01),
        'w_gate_up': normal(ks[15], (L, N_EXPERTS, D_MODEL, 2 * EXPERT_HIDDEN), D_MODEL ** -0.5),
        'w_down': normal(ks[16], (L, N_EXPERTS, EXPERT_HIDDEN, D_MODEL), DN_BETA * EXPERT_HIDDEN ** -0.5),
        'ln2_g': 1.0 + normal(ks[17], (L, D_MODEL), 0.1),
        'ln2_b': normal(ks[18], (L, D_MODEL), 0.02),
    }

def second_block(x, w_in, b_in, lb_logits, hg_norm_g, rel_bias, w_proj_a, w_proj_b, w_out, ln1_g, ln1_b,
              w_group, b_group, w_expert, b_expert, w_gate_up, w_down, ln2_g, ln2_b):
    split_at = [int(s) for s in np.cumsum(IN_SIZES)[:-1]]
    lower_bounds = jnp.cumsum(jax.nn.softmax(lb_logits.astype(jnp.float32), axis=0), axis=0)
    for l in range(DEPTH_2):
        h = x
        proj = h @ w_in[l] + b_in[l]
        hg_q, hg_f, hg_i, hg_g, mb_q, mb_k, mb_v, gate_a, gate_b = jnp.split(proj, split_at, axis=-1)
        y_a = hgrn2_mixer(hg_q, hg_f, hg_i, hg_g, lower_bounds[l], hg_norm_g[l]) @ w_proj_a[l]
        y_b = moba_mixer(mb_q, mb_k, mb_v, rel_bias) @ w_proj_b[l]
        mixed = (jax.nn.sigmoid(gate_a) * y_a + jax.nn.sigmoid(gate_b) * y_b) @ w_out[l]
        x = layer_norm(DN_ALPHA * h + mixed, ln1_g[l], ln1_b[l])
        ffn = hier_moe(x, w_group[l], b_group[l], w_expert[l], b_expert[l], w_gate_up[l], w_down[l])
        x = layer_norm(DN_ALPHA * x + ffn, ln2_g[l], ln2_b[l])
    return x


def setup_inputs(seed=0):
    out = dict(first_inputs(seed))
    for name, value in second_inputs(seed + 1).items():
        if name != "x":
            out[name + "_2"] = value
    return out


def reference(
    x, meta_tokens, norm_gains, w_ffn_in, w_ffn_out, gla_w_in, gla_w_gate, gla_b_gate, gla_norm,
    gla_w_out, kv_norm, w_kv, swa_w_q, swa_sinks, swa_w_out, w_in_2, b_in_2, lb_logits_2,
    hg_norm_g_2, rel_bias_2, w_proj_a_2, w_proj_b_2, w_out_2, ln1_g_2, ln1_b_2, w_group_2,
    b_group_2, w_expert_2, b_expert_2, w_gate_up_2, w_down_2, ln2_g_2, ln2_b_2,
):
    x = first_block(
        x, meta_tokens, norm_gains, w_ffn_in, w_ffn_out, gla_w_in, gla_w_gate, gla_b_gate,
        gla_norm, gla_w_out, kv_norm, w_kv, swa_w_q, swa_sinks, swa_w_out,
    )
    return second_block(
        x, w_in_2, b_in_2, lb_logits_2, hg_norm_g_2, rel_bias_2, w_proj_a_2, w_proj_b_2,
        w_out_2, ln1_g_2, ln1_b_2, w_group_2, b_group_2, w_expert_2, b_expert_2, w_gate_up_2,
        w_down_2, ln2_g_2, ln2_b_2,
    )


_drawn_inputs = setup_inputs


def setup_inputs(seed=0):
    import zlib

    import numpy as np

    out = dict(_drawn_inputs(seed))
    spreads = {}
    factors = {'gla_norm': 2.706,
     'kv_norm': 3.182,
     'swa_sinks': 8.0,
     'b_in_2': 8.0,
     'lb_logits_2': 7.995,
     'hg_norm_g_2': 3.565,
     'rel_bias_2': 3.22,
     'b_group_2': 38.335,
     'b_expert_2': 24.197,
     'ln2_b_2': 2.809}
    for name, (base, spread) in spreads.items():
        noise = np.random.default_rng([zlib.crc32(name.encode()), seed]).standard_normal(out[name].shape)
        drawn = base * np.exp(spread * noise) if base else spread * noise
        out[name] = __import__('jax').numpy.asarray(drawn.astype(out[name].dtype))
    for name, factor in factors.items():
        out[name] = (out[name] * factor).astype(out[name].dtype)
    return out
```

```python
from contextlib import ExitStack

import numpy as np

import concourse.bass as bass
from concourse import mybir

F32 = mybir.dt.float32
I32 = mybir.dt.int32
U32 = mybir.dt.uint32
ALU = mybir.AluOpType
ACT = mybir.ActivationFunctionType
AX = mybir.AxisListType.X

P = 128
D = 1024
KT = D // P
SEQ = 256
META = 16
TA = SEQ + META
FF = 2816
FT = FF // P
EPS = 1e-6
LN_EPS = 1e-5
GH, GDK, GDV, CH = 4, 128, 256, 64
RANK = 16
NEG = -1e30
ALPHA = float(2.0 ** 0.25)
NE, EH = 32, 512
SLOTS = 64
MAXB = NE + 2 * SEQ // SLOTS
RING = 4
UNIT = 2 * KT * P
OUT_UNIT = FT * P
EXP_UNITS = 6

C_COLS = {}
for _name, _n in (("ident", P), ("ones", P), ("rot", P), ("pairmask", P), ("upper", P), ("iota", SLOTS),
                  ("iota32", 32), ("iotab", MAXB), ("reset_g", TA), ("reset_h", SEQ), ("cos", TA), ("sin", TA),
                  ("swa0", P + META), ("swa1", SEQ + META), ("ninf", SEQ), ("onehot", 384)):
    C_COLS[_name] = (sum(n for _, n in C_COLS.values()), _n)
NC_COLS = sum(n for _, n in C_COLS.values())
LEVELS = [64, 32, 16, 8, 4, 2, 1, 0]

P_COLS = {}
for _name, _n in (("gains", 96), ("kv_norm", KT), ("b_gate", GH), ("gla_norm", 2), ("w_lr", KT * RANK),
                  ("w_gate", GH * GDK), ("b_in", 44), ("lb_logits", 8), ("hg_norm", 4), ("ln1_g", KT), ("ln1_b", KT),
                  ("w_route", KT * 36), ("b_route", 36), ("rel_bias", 8), ("sinks", 32)):
    P_COLS[_name] = (sum(n for _, n in P_COLS.values()), _n)
NP_COLS = sum(n for _, n in P_COLS.values())


def constants():
    c = {k: np.zeros((P, n), np.float32) for k, (_, n) in C_COLS.items()}
    i = np.arange(P)
    c["ident"][i, i] = 1
    c["ones"][:] = 1
    d = i % 64
    part = np.where(d < 8, i + 8, i - 8)
    m = i[d < 16]
    c["rot"][part[m], m] = 1
    s, t = i[:, None], i[None, :]
    c["pairmask"][:] = (s // CH == t // CH) & (s <= t)
    c["upper"][:] = s < t
    c["iota"][:] = np.arange(SLOTS)
    c["iota32"][:] = np.arange(32)
    c["iotab"][:] = np.arange(MAXB)
    col = np.arange(TA)
    c["reset_g"][:] = col % CH != 0
    c["reset_h"][:] = np.arange(SEQ) % P != 0
    inv = np.float32(500000.0) ** (-np.arange(0, 16, 2, dtype=np.float32) / np.float32(16))
    pos = np.where(col < SEQ, col + META, col - SEQ).astype(np.float32)
    ang = pos[None, :] * inv[d % 8][:, None]
    c["cos"][:] = np.where((d < 16)[:, None], np.cos(ang), 1)
    c["sin"][:] = np.where((d < 8)[:, None], -np.sin(ang), np.where((d < 16)[:, None], np.sin(ang), 0))
    own = np.where(t <= s, 0, NEG)
    c["swa0"][:, :P] = own
    c["swa1"][:, :P] = np.where(t > s, 0, NEG)
    c["swa1"][:, P:2 * P] = own
    c["ninf"][:, :] = np.where(np.arange(SEQ)[None, :] <= P + s, 0, NEG)
    dist = 255 - np.arange(384)
    dd = np.maximum(dist, 1).astype(np.float32)
    log_part = 16 + (np.log(dd / np.float32(16)) / np.float32(np.log(8.0)) * np.float32(16)).astype(np.int32)
    bucket = np.where(dist < 16, dist, np.minimum(log_part, 31))
    c["onehot"][:32] = (bucket[None, :] == np.arange(32)[:, None]) & (dist >= 0)[None, :]
    table = np.concatenate([c[k] for k in C_COLS], axis=1)
    levels = np.zeros((P, len(LEVELS), P), np.float32)
    for n, h in enumerate(LEVELS):
        if h:
            levels[:, n] = (s // (2 * h) == t // (2 * h)) & (s % (2 * h) < h) & (t % (2 * h) >= h)
        else:
            levels[:, n] = s == t
    return table, levels.reshape(P, -1)


class Stream:

    def __init__(self):
        self.n = 0

    def take(self, n):
        first, self.n = self.n, self.n + n
        return first


class Tiles:

    def __init__(self, uses, banks, n):
        self.banks, self.base = banks, {b: uses[b] for b in banks}
        for i in range(n):
            uses[banks[i % len(banks)]] += 1

    def at(self, i, it=0, body=0):
        b = self.banks[i % len(self.banks)]
        return b, self.base[b] + i // len(self.banks) + it * (body // len(self.banks))


def two_blocks(nc, xT, w_units, w_out_units, w_gate_up, w_down, table, levels, params, rows, out):
    ctx = ExitStack()
    with ctx:
        def sb(name, shape, dt=F32):
            return ctx.enter_context(nc.sbuf_tensor(name, shape, dt))

        def sem(name):
            return ctx.enter_context(nc.semaphore(name))

        ring = sb("ring", [P, EXP_UNITS * UNIT])
        h = sb("h", [P, KT * TA])
        hn = sb("hn", [P, KT * TA])
        zg = sb("zg", [P, KT * TA])
        sq = sb("sq", [P, 2, TA])
        acc = sb("acc", [P, TA])
        var = sb("var", [P, TA])
        std = sb("std", [P, TA])
        rs = sb("rs", [P, TA])
        kT = sb("kT", [P, 2, TA])
        vs = sb("vs", [P, 3, 256])
        small = sb("small", [P, 320])
        cst = sb("cst", [P, NC_COLS])
        par = sb("par", [P, NP_COLS])
        halfg = sb("halfg", [P, 96])
        arena = sb("arena", [P, 25400])
        meta_i = sb("meta_i", [1, MAXB + 8], I32)
        ps = [ctx.enter_context(nc.psum_tensor(f"ps{b}", [P, 512], F32)) for b in range(8)]
        bias_rows = nc.dram_tensor("bias_rows", [8, P * 384], F32, kind="Internal").ap()

        def C(name, a=0, b=None, parts=slice(0, P)):
            at, n = C_COLS[name]
            return cst[parts, at + a:at + (n if b is None else b)]

        def W(name, a=0, b=None, parts=slice(0, P)):
            at, n = P_COLS[name]
            return par[parts, at + a:at + (n if b is None else b)]

        def gain(g, m, table=par):
            at = P_COLS["gains"][0] if table is par else 0
            return table[:, at + g * KT + m:at + g * KT + m + 1]

        place = [0]

        def room(n):
            at = place[0]
            place[0] += n
            assert place[0] <= 25400, place[0]
            return arena[:, at:at + n]

        def tile(buf, m, t, w=TA):
            return buf[:, m * w:m * w + t]

        hid = room(FT * TA)
        sg = room(2 * TA)
        hk = room(KT * TA)
        s_kraw = hid[:, 0:2 * TA]
        s_krot = hid[:, 2 * TA:4 * TA]
        place[0] = 0
        g_v = room(2 * D)
        g_vm = room(D)
        g_r = room(KT * TA)
        g_b = room(GH * TA)
        g_e = [room(GH * TA) for _ in range(3)]
        g_q, g_k, g_kw = room(GH * TA), room(GH * TA), room(GH * TA)
        g_att = room(GH * TA)
        g_kwT = room(GH * 384)
        g_s = room(GH * 4 * GDV)
        g_o = room(KT * TA)
        g_lr = room(TA)
        g_sq = arena[:, 3 * D + KT * TA + 2 * GH * TA:3 * D + KT * TA + 4 * GH * TA]
        place[0] = 0
        s_q = room(KT * SEQ)
        s_t = room(2 * SEQ)
        s_o = room(KT * SEQ)
        a_p = room(2 * 4 * TA)
        a_pT = room(4 * 384)
        place[0] = 0
        b_sga, b_sgb = hn, room(KT * SEQ)
        b_sg = room(4 * SEQ)
        b_kf, b_q, b_b, b_e, b_qk = (room(4 * SEQ) for _ in range(5))
        b_v, b_mv = room(2 * 512), room(2 * 512)
        b_mq, b_mk = room(4 * SEQ), room(4 * SEQ)
        b_bias = room(8 * SEQ)
        b_att = room(3 * 512)
        b_a, b_bo = room(4 * SEQ), room(4 * SEQ)
        b_sq = room(4 * SEQ)
        b_p, b_pT = room(2 * 4 * TA), room(4 * 384)
        b_lv = room(len(LEVELS) * P)
        b_rows = room(2 * 512)
        place[0] = 0
        m_x = room(2 * D)
        m_g, m_b = room(D), room(D)
        m_r = room(2200)
        r_, at_ = {}, 64
        for name, n in (("lg", 72), ("gl", 8), ("gt", 8), ("g1", 8), ("ge", 8), ("em", 64), ("tmp", 64), ("o1", 64),
                        ("o2", 64), ("gtop", 2), ("top1", 2), ("top2", 2), ("place", 2), ("ev", 2), ("pg", 2),
                        ("w1", 2), ("w2", 2), ("dest", 4), ("cnt", 32), ("nb", 32), ("end", 32), ("beg", 32),
                        ("eb", MAXB), ("cmp", MAXB * 32)):
            r_[name] = m_r[:, at_:at_ + n]
            at_ += n
        assert at_ <= 2200, at_
        m_P = room(2 * 64)
        m_PW = room(2 * P)
        m_t = room(6 * 64)
        m_zero = room(P)
        m_xT = room(512)
        m_h = room(256)
        m_sg = room(256)
        m_turn = room(512)
        m_hT, m_pwT = m_turn[:, 0:2 * P], m_turn[:, 2 * P:4 * P]
        m_y = room(512)
        m_o = room(2 * D)
        b_br = hid[:, 0:8 * 384]

        consts_in, params_in, x_in, levels_in, rows_in, ln2_in = (
            sem(n) for n in ("consts_in", "params_in", "x_in", "levels_in", "rows_in", "ln2_in"))
        bias_out, bias_in, out_stored = sem("bias_out"), sem("bias_in"), sem("out_stored")
        full = [sem(f"full{b}") for b in range(8)]
        evac = [sem(f"evac{b}") for b in range(8)]
        landed = [sem(f"landed{s}") for s in range(RING)]
        e_landed = [sem(f"e_landed{s}") for s in range(EXP_UNITS)]
        unit_begun = sem("unit_begun")
        sq_made, sq_used, std_made = sem("sq_made"), sem("sq_used"), sem("std_made")
        hn_ready, h_ready = sem("hn_ready"), sem("h_ready")
        act_chain, dve_chain = sem("act_chain"), sem("dve_chain")
        soft_made, decay_in, decay_made, gated = (sem(n) for n in ("soft_made", "decay_in", "decay_made", "gated"))
        q_roped, neg_max, exp_made, p_ready = (sem(n) for n in ("q_roped", "neg_max", "exp_made", "p_ready"))
        lb_in, lb_exp = sem("lb_in"), sem("lb_exp")
        hg_arg, hg_ln, lvl_in, lvl_exp, lvl_ready = (
            sem(n) for n in ("hg_arg", "hg_ln", "lvl_in", "lvl_exp", "lvl_ready"))
        hgo_ready, mixed = sem("hgo_ready"), sem("mixed")
        ln_in, centred, ln_squared, x2_ready = (sem(n) for n in ("ln_in", "centred", "ln_squared", "x2_ready"))
        route_in, route_exp, m_ready, table_ready = (
            sem(n) for n in ("route_in", "route_exp", "m_ready", "table_ready"))
        p_made, pw_made, pw_turned, parts_made, moved = (
            sem(n) for n in ("p_made", "pw_made", "pw_turned", "parts_made", "moved"))
        y_zeroed, silu_made, y_done = (sem(n) for n in ("y_zeroed", "silu_made", "y_done"))
        fin_centred, fin_squared, fin_var, fin_std, out_ready = (
            sem(n) for n in ("fin_centred", "fin_squared", "fin_var", "fin_std", "out_ready"))

        units, uses = Stream(), [0] * 8
        MAIN = [0, 1, 2, 3]
        plan = {}

        def ffn_plan(n):
            plan[f"in{n}"] = (units.take(FT), Tiles(uses, MAIN, 2 * FT))
            plan[f"out{n}"] = (units.take(KT), Tiles(uses, MAIN, KT))

        def tiles(name, banks, n):
            plan[name] = Tiles(uses, banks, n)

        tiles("bias", [4, 5, 6, 7], 8)
        tiles("stat0", [7], 1)
        ffn_plan(0)
        tiles("stat1", [7], 1)
        tiles("stat2", [7], 1)
        tiles("lr", [4], 1)
        plan["r"] = (units.take(4), Tiles(uses, MAIN, 8))
        tiles("gate", [4, 5, 6, 7], 4)
        plan["v"] = (units.take(4), Tiles(uses, MAIN, 12))
        plan["k"] = (units.take(2), Tiles(uses, MAIN, 4))
        plan["q"] = (units.take(2), Tiles(uses, MAIN, 4))
        tiles("att", [0, 1, 2, 3], 4)
        tiles("kwT", [4, 5, 6, 7], 4)
        tiles("kv", list(range(8)), 12)
        tiles("o", list(range(8)), 8)
        tiles("gst", MAIN, 4)
        plan["gout"] = (units.take(4), Tiles(uses, MAIN, 8))
        tiles("stat3", [7], 1)
        tiles("stat4", [7], 1)
        ffn_plan(1)
        tiles("stat5", [7], 1)
        tiles("stat6", [7], 1)
        plan["ks"] = (units.take(1), Tiles(uses, MAIN, 2))
        tiles("krot", [4, 5], 2)
        plan["vs"] = (units.take(1), Tiles(uses, MAIN, 3))
        ffn_plan(2)
        tiles("stat7", [7], 1)
        tiles("stat8", [7], 1)
        plan["sq"] = (units.take(4), Tiles(uses, MAIN, 8))
        tiles("qrot", [4, 5], 8)
        tiles("ss", MAIN, 32)
        tiles("sT", [4, 5, 6], 32)
        tiles("sv", [7], 8)
        plan["sout"] = (units.take(4), Tiles(uses, MAIN, 8))
        tiles("stat9", [7], 1)
        tiles("stat10", [7], 1)
        ffn_plan(3)
        tiles("stat11", [7], 1)
        SECTIONS = ["z", "hq", "ga", "gb", "hgate", "mq", "mk", "hi", "mv"]
        for name in SECTIONS:
            n_units = 4 if name in ("ga", "gb") else 2
            plan[name] = (units.take(n_units), Tiles(uses, MAIN, 2 * n_units))
        tiles("lvl", [4, 5, 6, 7], 16)
        tiles("cross", [4], 1)
        tiles("ho", [0, 1, 2, 3], 4)
        tiles("hst", [4, 5, 6, 7], 4)
        tiles("bs", MAIN, 16)
        tiles("bT", [4, 5, 6], 16)
        tiles("bv", [7], 4)
        plan["pa"] = (units.take(2), Tiles(uses, MAIN, 8))
        plan["pb"] = (units.take(2), Tiles(uses, MAIN, 8))
        plan["wo"] = (units.take(4), Tiles(uses, MAIN, 8))
        tiles("mean", [7], 1)
        tiles("lnvar", [7], 1)
        tiles("xtok", [0, 1, 2, 3], 4)
        tiles("route", [4], 1)
        tiles("pos", [5], 1)
        tiles("cnt", [6], 1)
        N_UNITS = units.n
        tiles("e_gather", [4], 1)
        E_BASE = {b: uses[b] for b in range(4, 8)}


        block = ctx.enter_context(nc.Block())

        runs = []
        u, row, orow = 0, 0, 0
        for key, val in plan.items():
            if not isinstance(val, tuple):
                continue
            n = {"out": KT, "in": FT}.get(key.rstrip("0123"), None)
            first = val[0]
            nxt = min([v[0] for v in plan.values() if isinstance(v, tuple) and v[0] > first] + [N_UNITS])
            n = nxt - first
            if key.startswith("out"):
                runs.append((1, orow, first, n))
                orow += n
            elif runs and runs[-1][0] == 0 and runs[-1][2] + runs[-1][3] == first:
                runs[-1] = (0, runs[-1][1], runs[-1][2], runs[-1][3] + n)
                row += n
            else:
                runs.append((0, row, first, n))
                row += n

        def slot(u, n=UNIT):
            s = u % RING
            return ring[:, s * OUT_UNIT:s * OUT_UNIT + n]

        @block.sync
        def _(sp):
            sp.dma_start(cst[:, :], table).then_inc(consts_in, 16)
            sp.dma_start(h[:, :], xT).then_inc(x_in, 16)
            sp.dma_start(par[:, :], params).then_inc(params_in, 16)

            def load(kind, row, u, it=0):
                n = OUT_UNIT if kind else UNIT
                src = (w_out_units if kind else w_units)[bass.ds(row + RING * it, 1), :, :]
                if not isinstance(it, int) or u + RING * it >= RING:
                    sp.wait_ge(unit_begun, u - RING + 2 + RING * it)
                sp.dma_start(slot(u, n), src.rearrange("a p n -> (a p) n")).then_inc(landed[u % RING], 16)

            for kind, row, first, n in runs:
                head = RING if first == 0 else 0
                for j in range(head):
                    load(kind, row + j, first + j)
                row, first, n = row + head, first + head, n - head
                if n // RING > 1:
                    with sp.Fori(0, n // RING) as it:
                        for j in range(RING):
                            load(kind, row + j, first + j, it)
                    done = n // RING * RING
                else:
                    done = 0
                for j in range(done, n):
                    load(kind, row + j, first + j)

            sp.wait_ge(unit_begun, N_UNITS)
            sp.wait_ge(y_zeroed, 1)
            sp.wait_ge(table_ready, 1)
            n_blocks = sp.value_load(meta_i[0:1, MAXB:MAXB + 1], min_val=1, max_val=MAXB)
            with sp.Fori(0, n_blocks) as b:
                e = sp.value_load(meta_i[0:1, bass.ds(b, 1)], min_val=0, max_val=NE - 1)
                for i in range(EXP_UNITS):
                    sp.wait_ge(unit_begun, N_UNITS + b * EXP_UNITS + i - EXP_UNITS + 2)
                    if i < 4:
                        src = w_gate_up[bass.ds(e, 1), 2 * P * i:2 * P * (i + 1), :]
                    else:
                        src = w_down[bass.ds(e, 1), 2 * P * (i - 4):2 * P * (i - 3), :]
                    sp.dma_start(ring[:, i * UNIT:(i + 1) * UNIT].rearrange("p (k n) -> p k n", k=2),
                                 src.rearrange("a (k p) n -> p (a k) n", p=P)).then_inc(e_landed[i], 16)

        @block.gpsimd
        def _(pool):
            pool.wait_ge(evac[plan["bias"].at(7)[0]], plan["bias"].at(7)[1] + 1)
            for i in range(8):
                pool.dma_start(bias_rows[i, :].rearrange("(p n) -> p n", p=P),
                               b_br[:, i * 384:(i + 1) * 384]).then_inc(bias_out, 16)
            pool.wait_ge(bias_out, 8 * 16)
            t = plan["stat11"].at(0)
            pool.wait_ge(full[t[0]], t[1] + 1)
            for i in range(8):
                src = bias_rows[i, 127:127 + P * 383].rearrange("(p n) -> p n", p=P)[:, 0:SEQ]
                pool.dma_start(b_bias[:, i * SEQ:(i + 1) * SEQ], src).then_inc(bias_in, 16)
            pool.dma_start(b_lv, levels).then_inc(levels_in, 16)
            pool.dma_start(b_rows, rows[:, 0:1024]).then_inc(rows_in, 16)
            t = plan["lnvar"].at(0)
            pool.wait_ge(full[t[0]], t[1] + 1)
            pool.dma_start(m_g, rows[:, 1024:2048]).then_inc(ln2_in, 16)
            pool.dma_start(m_b, rows[:, 2048:3072]).then_inc(ln2_in, 16)

        @block.tensor
        def _(pe):
            def mm(out_ap, lhsT, rhs, start, stop):
                return nc.tensor.matmul(out_ap, lhsT, rhs, start=start, stop=stop, skip_group_check=True)

            def turn(out_ap, in_ap):
                k = in_ap.shape[0]
                return nc.tensor.transpose(out_ap, in_ap, C("ident", 0, k, slice(0, k)))

            def free(t):
                if not isinstance(t[1], int) or t[1] > 0:
                    pe.wait_ge(evac[t[0]], t[1])
                return ps[t[0]]

            def taken(t):
                pe.wait_ge(evac[t[0]], t[1] + 1)

            def unit(u, it=0):
                pe.wait_ge(landed[u % RING], 16 * (u // RING + 1) + 16 * it)

            def project(u, T, i, src, w, it=0, body=0, kt=KT, n_tiles=2, pitch=TA):
                unit(u, it)
                wt = slot(u)
                for j in range(n_tiles):
                    t = T.at(i + j, it, body)
                    bank = free(t)
                    for k in range(kt):
                        m = mm(bank[:, 0:w], wt[:, (j * kt + k) * P:(j * kt + k + 1) * P],
                               src[:, k * pitch:k * pitch + w], k == 0, k == kt - 1)
                        if j == 0 and k == 0:
                            m.then_inc(unit_begun, 1)
                    m.then_inc(full[t[0]], 1)

            def project_tokens(u, T, i, src, spans, pitch=TA):
                unit(u)
                wt = slot(u)
                for j, (a, n) in enumerate(spans):
                    t = T.at(i + j)
                    bank = free(t)
                    for k in range(KT):
                        m = mm(bank[0:n, 0:256], src[:, k * pitch + a:k * pitch + a + n],
                               wt[:, k * 256:(k + 1) * 256], k == 0, k == KT - 1)
                        if j == 0 and k == 0:
                            m.then_inc(unit_begun, 1)
                    m.then_inc(full[t[0]], 1)

            def stat(n, w):
                t = plan[f"stat{n}"].at(0)
                pe.wait_ge(sq_used, 8 * (n + 1))
                bank = free(t)
                mm(bank[:, 0:w], C("ones"), acc[:, 0:w], True, True).then_inc(full[t[0]], 1)

            def ffn(n, hn_count, w):
                pe.wait_ge(hn_ready, hn_count)
                u0, T = plan[f"in{n}"]
                rounds = FT // RING
                with pe.Fori(0, rounds) as it:
                    for j in range(RING):
                        project(u0 + j, T, 2 * j, hn, w, it, 2 * RING)
                for j in range(rounds * RING, FT):
                    project(u0 + j, T, 2 * j, hn, w)
                last = T.at(2 * FT - 1)
                u1, T = plan[f"out{n}"]
                before = plan[f"in{n}"][1].at(2 * FT - 3)
                with pe.Fori(0, KT // RING) as it:
                    for j in range(RING):
                        t = T.at(j, it, RING)
                        unit(u1 + j, it)
                        bank = free(t)
                        if j == 0:
                            taken(before)
                        for k in range(FT):
                            if j == 0 and k == FT - 1:
                                taken(last)
                            m = mm(bank[:, 0:w], slot(u1 + j, OUT_UNIT)[:, k * P:(k + 1) * P],
                                   hid[:, k * TA:k * TA + w], k == 0, k == FT - 1)
                            if k == 0:
                                m.then_inc(unit_begun, 1)
                        m.then_inc(full[t[0]], 1)

            pe.wait_ge(consts_in, 16)
            pe.wait_ge(params_in, 16)
            for i in range(8):
                t = plan["bias"].at(i)
                bank = free(t)
                mm(bank[:, 0:384], W("rel_bias", i, i + 1, slice(0, 32)).to_broadcast([32, P]),
                   C("onehot", 0, 384, slice(0, 32)), True, True).then_inc(full[t[0]], 1)
            stat(0, TA)
            ffn(0, 8, TA)
            stat(1, TA)
            stat(2, TA)

            pe.wait_ge(hn_ready, 16)
            t = plan["lr"].at(0)
            bank = free(t)
            for k in range(KT):
                m = mm(bank[0:RANK, 0:TA], W("w_lr", k * RANK, (k + 1) * RANK), hn[:, k * TA:(k + 1) * TA],
                       k == 0, k == KT - 1)
            m.then_inc(full[t[0]], 1)
            u0, T = plan["r"]
            project(u0, T, 0, hn, TA)
            taken(plan["lr"].at(0))
            for i in range(GH):
                t = plan["gate"].at(i)
                bank = free(t)
                mm(bank[:, 0:TA], W("w_gate", i * GDK, (i + 1) * GDK, slice(0, RANK)), g_lr[0:RANK, :],
                   True, True).then_inc(full[t[0]], 1)
            for j in range(1, 4):
                project(u0 + j, T, 2 * j, hn, TA)
            u0, T = plan["v"]
            for j in range(4):
                project_tokens(u0 + j, T, 3 * j, hn, ((0, P), (P, P), (SEQ, META)))
            for name in ("k", "q"):
                u0, T = plan[name]
                for j in range(2):
                    project(u0 + j, T, 2 * j, hn, TA)
            for i in range(GH):
                t = plan["att"].at(i)
                bank = free(t)
                taken(plan["q"][1].at(i))
                for a, n in ((0, P), (P, P), (SEQ, META)):
                    m = mm(bank[0:n, a:a + n], g_k[:, i * TA + a:i * TA + a + n], g_q[:, i * TA + a:i * TA + a + n],
                           True, True)
                m.then_inc(full[t[0]], 1)
            for i in range(GH):
                t = plan["kwT"].at(i)
                bank = free(t)
                turn(bank[:, 0:P], g_kw[:, i * TA:i * TA + P])
                turn(bank[:, P:2 * P], g_kw[:, i * TA + P:i * TA + 2 * P])
                turn(bank[0:META, 256:384], g_kw[:, i * TA + SEQ:(i + 1) * TA]).then_inc(full[t[0]], 1)
            for i in range(GH):
                taken(plan["kwT"].at(i))
                T = plan["kv"]
                kw = g_kwT[:, i * 384:(i + 1) * 384]
                v0, v1 = (g_v[:, t * D + i * GDV:t * D + (i + 1) * GDV] for t in (0, 1))
                bank = free(T.at(3 * i))
                mm(bank[:, 0:256], kw[0:META, 256:384], g_vm[0:META, i * GDV:(i + 1) * GDV], True, True)
                mm(bank[:, 256:512], kw[0:64, 0:128], v0[0:64, :], True, True).then_inc(full[T.at(3 * i)[0]], 1)
                bank = free(T.at(3 * i + 1))
                mm(bank[:, 0:256], kw[64:128, 0:128], v0[64:128, :], True, True).then_inc(full[T.at(3 * i + 1)[0]], 1)
                bank = free(T.at(3 * i + 2))
                mm(bank[:, 0:256], kw[0:64, 128:256], v1[0:64, :], True, True).then_inc(full[T.at(3 * i + 2)[0]], 1)
            for i in range(GH):
                taken(plan["att"].at(i))
                taken(plan["kv"].at(3 * i + 2))
                for half in range(2):
                    t = plan["o"].at(2 * i + half)
                    bank = free(t)
                    c0 = i * GDV + half * P
                    mm(bank[:, 0:P], g_v[:, c0:c0 + P], g_att[:, i * TA:i * TA + P], True, False)
                    mm(bank[:, P:2 * P], g_v[:, D + c0:D + c0 + P], g_att[:, i * TA + P:i * TA + 2 * P], False, False)
                    mm(bank[:, SEQ:TA], g_vm[0:META, c0:c0 + P], g_att[0:META, i * TA + SEQ:(i + 1) * TA], False, False)
                    for c in range(4):
                        st = g_s[:, (i * 4 + c) * GDV + half * P:(i * 4 + c) * GDV + (half + 1) * P]
                        m = mm(bank[:, c * CH:(c + 1) * CH], st, g_q[:, i * TA + c * CH:i * TA + (c + 1) * CH],
                               False, c == 3)
                    m.then_inc(full[t[0]], 1)
            for i in range(GH):
                taken(plan["o"].at(2 * i + 1))
                t = plan["gst"].at(i)
                bank = free(t)
                mm(bank[:, 0:TA], C("ones"), tile(g_sq, 2 * i, TA), True, False)
                mm(bank[:, 0:TA], C("ones"), tile(g_sq, 2 * i + 1, TA), False, True).then_inc(full[t[0]], 1)
            pe.wait_ge(gated, 8)
            u0, T = plan["gout"]
            for j in range(4):
                project(u0 + j, T, 2 * j, g_o, TA)
            stat(3, TA)
            stat(4, TA)
            ffn(1, 24, TA)
            stat(5, TA)
            stat(6, TA)

            pe.wait_ge(hn_ready, 32)
            u0, T = plan["ks"]
            project(u0, T, 0, hk, TA)
            for i in range(2):
                taken(plan["ks"][1].at(i))
                t = plan["krot"].at(i)
                bank = free(t)
                mm(bank[:, 0:TA], C("rot"), tile(s_kraw, i, TA), True, True).then_inc(full[t[0]], 1)
            u0, T = plan["vs"]
            project_tokens(u0, T, 0, hk, ((0, P), (P, P), (SEQ, META)))
            ffn(2, 40, SEQ)
            stat(7, SEQ)
            stat(8, SEQ)

            pe.wait_ge(hn_ready, 48)
            u0, T = plan["sq"]
            for j in range(4):
                project(u0 + j, T, 2 * j, hn, SEQ)
                for i in (2 * j, 2 * j + 1):
                    taken(T.at(i))
                    t = plan["qrot"].at(i)
                    bank = free(t)
                    mm(bank[:, 0:SEQ], C("rot"), s_q[:, i * SEQ:(i + 1) * SEQ], True, True).then_inc(full[t[0]], 1)

            def attend(names, groups, first, pb, pT, q_of, k_of, v_of, segs, done):
                S, TT, V = (plan[x] for x in names)

                def scores(g):
                    done(g)
                    for u in range(4):
                        n, b = divmod(u, 2)
                        t = S.at(4 * g + u)
                        bank = free(t)
                        hs = slice(64 * b, 64 * b + 64)
                        for at, size, key in segs(n):
                            m = mm(bank[:, at:at + size], q_of(g, hs, n), k_of(g, hs, key, size), True, True)
                        m.then_inc(full[t[0]], 1)

                scores(0)
                for g in range(groups):
                    if g + 1 < groups:
                        scores(g + 1)
                    for u in range(4):
                        n, b = divmod(u, 2)
                        t = TT.at(4 * g + u)
                        bank = free(t)
                        pe.wait_ge(p_ready, first + 4 * g + u + 1)
                        for s, (at, size, key) in enumerate(segs(n)):
                            p = pb[:, ((g % 2) * 4 + u) * TA + at:((g % 2) * 4 + u) * TA + at + size]
                            m = turn(bank[0:size, s * P:(s + 1) * P], p)
                        m.then_inc(full[t[0]], 1)
                    t = V.at(g)
                    bank = free(t)
                    for u in range(4):
                        n, b = divmod(u, 2)
                        taken(TT.at(4 * g + u))
                        ss = segs(n)
                        for s, (at, size, key) in enumerate(ss):
                            m = mm(bank[64 * b:64 * b + 64, n * P:(n + 1) * P], v_of(g, b, key, size),
                                   pT[0:size, u * 384 + s * P:u * 384 + (s + 1) * P], s == 0, s == len(ss) - 1)
                    m.then_inc(full[t[0]], 1)
            swa_segs = (((0, P, 0), (P, META, SEQ)), ((0, P, 0), (P, P, P), (SEQ, META, SEQ)))
            attend(("ss", "sT", "sv"), 8, 0, a_p, a_pT,
                   lambda g, hs, n: s_q[hs, g * SEQ + n * P:g * SEQ + (n + 1) * P],
                   lambda g, hs, key, size: kT[hs, g // 4, key:key + size],
                   lambda g, b, key, size: vs[0:size, key // P, (2 * (g // 4) + b) * 64:(2 * (g // 4) + b) * 64 + 64],
                   lambda n: swa_segs[n],
                   lambda g: pe.wait_ge(q_roped, g + 1))
            taken(plan["sv"].at(7))
            u0, T = plan["sout"]
            for j in range(4):
                project(u0 + j, T, 2 * j, s_o, SEQ, pitch=SEQ)
            stat(9, SEQ)
            stat(10, SEQ)
            ffn(3, 56, SEQ)
            stat(11, SEQ)

            pe.wait_ge(h_ready, 48)

            def level(n):
                if n == 0:
                    taken(plan["hq"][1].at(3))
                if LEVELS[n]:
                    pe.wait_ge(lvl_ready, n + 1)
                for p in range(2):
                    t = plan["lvl"].at(2 * n + p)
                    bank = free(t)
                    for i in range(4):
                        a = i * SEQ + p * P
                        left, right = (b_qk, b_qk) if LEVELS[n] else (b_kf, b_q)
                        m = mm(bank[:, i * P:(i + 1) * P], left[:, a:a + P], right[:, a:a + P], True, True)
                    m.then_inc(full[t[0]], 1)

            def section(name, js=None):
                u0, T = plan[name]
                for j in js if js is not None else range(4 if name in ("ga", "gb") else 2):
                    project(u0 + j, T, 2 * j, h, SEQ)

            section("z")
            section("hq")
            for j in range(4):
                section("ga", [j])
                if j >= 2:
                    level(j - 2)
            for j in range(4):
                section("gb", [j])
                level(j + 2)
            for j in range(2):
                section("hgate", [j])
                level(j + 6)
            section("mq")
            section("mk")
            pe.wait_ge(lvl_ready, len(LEVELS))
            t = plan["cross"].at(0)
            bank = free(t)
            for i in range(4):
                m = mm(bank[:, i * P:(i + 1) * P], b_qk[:, i * SEQ:i * SEQ + P], b_qk[:, i * SEQ + P:(i + 1) * SEQ], True, True)
            m.then_inc(full[t[0]], 1)
            for name in ("hi", "mv"):
                u0, T = plan[name]
                for j in range(2):
                    project_tokens(u0 + j, T, 2 * j, h, ((0, P), (P, P)))
            taken(plan["cross"].at(0))
            taken(plan["hi"][1].at(3))
            for i in range(4):
                t = plan["ho"].at(i)
                bank = free(t)
                v0, v1 = b_v[:, i * P:(i + 1) * P], b_v[:, 512 + i * P:512 + (i + 1) * P]
                mm(bank[:, 0:P], v0, b_att[:, i * P:(i + 1) * P], True, False)
                mm(bank[:, P:SEQ], v1, b_att[:, 512 + i * P:512 + (i + 1) * P], False, False)
                mm(bank[:, P:SEQ], v0, b_att[:, 1024 + i * P:1024 + (i + 1) * P], False, True).then_inc(full[t[0]], 1)
            for i in range(4):
                taken(plan["ho"].at(i))
                t = plan["hst"].at(i)
                bank = free(t)
                mm(bank[:, 0:SEQ], C("ones"), b_sq[:, i * SEQ:(i + 1) * SEQ], True, True).then_inc(full[t[0]], 1)
            moba_segs = (((0, P, 0),), ((0, P, 0), (P, P, P)))

            def moba_ready(g):
                if g == 0:
                    taken(plan["mk"][1].at(3))
                    taken(plan["mv"][1].at(3))

            attend(("bs", "bT", "bv"), 4, 32, b_p, b_pT,
                   lambda g, hs, n: b_mq[hs, g * SEQ + n * P:g * SEQ + (n + 1) * P],
                   lambda g, hs, key, size: b_mk[hs, g * SEQ + key:g * SEQ + key + size],
                   lambda g, b, key, size: b_mv[0:size, key // P * 512 + (2 * g + b) * 64:key // P * 512 + (2 * g + b) * 64 + 64],
                   lambda n: moba_segs[n], moba_ready)
            pe.wait_ge(hgo_ready, 4)
            for name, src in (("pa", b_a), ("pb", b_bo)):
                if name == "pb":
                    taken(plan["bv"].at(3))
                u0, T = plan[name]
                for j in range(2):
                    project(u0 + j, T, 4 * j, src, SEQ, kt=4, n_tiles=4, pitch=SEQ)
            pe.wait_ge(mixed, 8)
            u0, T = plan["wo"]
            for j in range(4):
                project(u0 + j, T, 2 * j, zg, SEQ)
            for name, k in (("mean", 1), ("lnvar", 2)):
                t = plan[name].at(0)
                pe.wait_ge(ln_in, k)
                bank = free(t)
                m = mm(bank[:, 0:SEQ], C("ones"), acc[:, 0:SEQ], True, True)
                m.then_inc(full[t[0]], 1)

            pe.wait_ge(x2_ready, 8)
            t = plan["route"].at(0)
            bank = free(t)
            for p in range(2):
                for k in range(KT):
                    m = mm(bank[:, p * 64:p * 64 + 36], h[:, k * TA + p * P:k * TA + (p + 1) * P],
                           W("w_route", k * 36, (k + 1) * 36), k == 0, k == KT - 1)
            m.then_inc(full[t[0]], 1)
            for i in range(4):
                t = plan["xtok"].at(i)
                bank = free(t)
                for k in range(4):
                    a = ((i % 2) * 4 + k) * TA + i // 2 * P
                    m = turn(bank[:, k * P:(k + 1) * P], h[:, a:a + P])
                m.then_inc(full[t[0]], 1)
            pe.wait_ge(m_ready, 1)
            t = plan["pos"].at(0)
            bank = free(t)
            M0, M1 = m_r[:, 0:32], m_r[:, 32:64]
            mm(bank[:, 0:32], C("upper"), M0, True, True)
            mm(bank[:, 32:64], C("upper"), M1, True, False)
            mm(bank[:, 32:64], C("ones"), M0, False, True).then_inc(full[t[0]], 1)
            t = plan["cnt"].at(0)
            bank = free(t)
            mm(bank[:, 0:32], C("ones"), M0, True, False)
            mm(bank[:, 0:32], C("ones"), M1, False, True).then_inc(full[t[0]], 1)

            pe.wait_ge(table_ready, 1)
            for i in range(4):
                taken(plan["xtok"].at(i))
                m = mm(ps[i][:, :], m_zero, m_x[:, 0:512], True, False)
            m.then_inc(y_zeroed, 1)
            n_blocks = pe.value_load(meta_i[0:1, MAXB:MAXB + 1], min_val=1, max_val=MAXB)
            taken(plan["cnt"].at(0))

            def gather():
                bank = ps[4]
                for kt in range(KT):
                    for p in range(2):
                        m = mm(bank[:, kt * 64:(kt + 1) * 64], m_x[:, p * D + kt * P:p * D + (kt + 1) * P],
                               m_P[:, p * 64:(p + 1) * 64], p == 0, p == 1)
                m.then_inc(full[4], 1)

            def combine():
                for p in range(2):
                    for n in range(2):
                        hs = slice(64 * n, 64 * n + 64)
                        m = mm(ps[2 * p + n][:, :], m_pwT[hs, p * P:(p + 1) * P], m_y[hs, :], False, False)
                return m

            pe.wait_ge(p_made, 1)
            t = plan["e_gather"].at(0)
            free(t)
            gather()
            with pe.Fori(0, n_blocks) as b:
                pe.wait_ge(evac[4], E_BASE[4] + b)
                pe.wait_ge(evac[5], E_BASE[5] + b)
                for i in range(4):
                    pe.wait_ge(e_landed[i], 16 * b + 16)
                    for kk in range(2):
                        k = 2 * i + kk
                        for j in range(2):
                            wt = ring[:, i * UNIT + kk * D:i * UNIT + (kk + 1) * D].rearrange(
                                "p (g n) -> p g n", g=2)[:, :, 256 * j:256 * j + 256]
                            m = mm(ps[5][64 * j:64 * j + 64, :].rearrange("p (g n) -> p g n", g=2),
                                   m_xT[:, k * 64:(k + 1) * 64], wt, k == 0, k == KT - 1)
                            if kk == 0 and j == 0:
                                m.then_inc(unit_begun, 1)
                m.then_inc(full[5], 1)
                pe.wait_ge(evac[7], E_BASE[7] + b)
                combine()
                pe.wait_ge(evac[6], E_BASE[6] + b)
                pe.wait_ge(pw_made, b + 1)
                for p in range(2):
                    m = turn(ps[6][:, 256 + p * P:256 + (p + 1) * P], m_PW[:, p * P:(p + 1) * P])
                m.then_inc(pw_turned, 1)
                pe.wait_ge(p_made, b + 2)
                gather()
                pe.wait_ge(evac[5], E_BASE[5] + b + 1)
                for c in range(2):
                    m = turn(ps[6][:, c * P:(c + 1) * P], m_h[:, c * P:(c + 1) * P])
                m.then_inc(full[6], 1)
                pe.wait_ge(evac[6], E_BASE[6] + b + 1)
                for i in range(2):
                    pe.wait_ge(e_landed[4 + i], 16 * b + 16)
                    for kk in range(2):
                        k = 2 * i + kk
                        for n in range(2):
                            m = mm(ps[7][64 * n:64 * n + 64, :], m_hT[:, kk * P + 64 * i:kk * P + 64 * i + 64],
                                   ring[:, (4 + i) * UNIT + kk * D + n * 512:(4 + i) * UNIT + kk * D + (n + 1) * 512],
                                   k == 0, k == 3)
                            if kk == 0 and n == 0:
                                m.then_inc(unit_begun, 1)
                m.then_inc(full[7], 1)
            pe.wait_ge(evac[7], E_BASE[7] + n_blocks)
            combine().then_inc(y_done, 1)

        @block.scalar
        def _(act):
            chain = [0]
            stds = [0]

            def did(ins):
                ins.then_inc(act_chain, 1)
                chain[0] += 1

            def own():
                act.wait_ge(act_chain, chain[0])

            def filled(t):
                act.wait_ge(full[t[0]], t[1] + 1)
                return ps[t[0]]

            def square(q, src, w):
                if q >= 2:
                    act.wait_ge(sq_used, q - 1)
                nc.scalar.activation(sq[:, q % 2, 0:w], src, ACT.Square).then_inc(sq_made, 1)

            def squares_of_h(n, w):
                for m in range(KT):
                    if n:
                        act.wait_ge(h_ready, 8 * ((n - 1) // 2) + m + 1)
                    square(8 * n + m, tile(h, m, w), w)

            def root(t, src, dst):
                act.wait_ge(evac[t[0]], t[1] + 1)
                nc.scalar.activation(dst, src, ACT.Sqrt).then_inc(std_made, 1)

            def root_stat(n, w):
                root(plan[f"stat{n}"].at(0), var[:, 0:w], std[:, 0:w])

            def branch_out(T, n, g, table, w):
                for m in range(KT):
                    t = T.at(m)
                    bank = filled(t)
                    square(8 * n + m, bank[:, 0:w], w)
                    nc.scalar.activation(tile(zg, m, w), bank[:, 0:w], ACT.Copy,
                                         scale=gain(g, m, table)).then_inc(evac[t[0]], 1)
                root_stat(n, w)

            def ffn(n, g, w):
                T = plan[f"in{n}"][1]
                with act.Fori(0, FT // 2) as it:
                    for j in range(2):
                        tg, tu = T.at(2 * j, it, 4), T.at(2 * j + 1, it, 4)
                        act.wait_ge(full[tg[0]], tg[1] + 1)
                        act.wait_ge(evac[tu[0]], tu[1])
                        nc.scalar.activation(tile(sg, j, w), ps[tg[0]][:, 0:w], ACT.Silu).then_inc(evac[tg[0]], 1)
                branch_out(plan[f"out{n}"][1], 2 * g_index[n] + 1, g, halfg, w)

            g_index = {0: 0, 1: 2, 2: 3, 3: 5}

            act.wait_ge(consts_in, 16)
            act.wait_ge(params_in, 16)
            act.wait_ge(lb_in, 1)
            nc.scalar.activation(small[:, 0:8], small[:, 0:8], ACT.Exp).then_inc(lb_exp, 1)
            for i in range(8):
                t = plan["bias"].at(i)
                nc.scalar.activation(b_br[:, i * 384:(i + 1) * 384], filled(t)[:, 0:384], ACT.Copy)\
                    .then_inc(evac[t[0]], 1)
            act.wait_ge(x_in, 16)
            squares_of_h(0, TA)
            root_stat(0, TA)
            act.wait_ge(lb_in, 2)
            ffn(0, 1, TA)
            squares_of_h(2, TA)
            root_stat(2, TA)

            t = plan["lr"].at(0)
            nc.scalar.activation(g_lr[0:RANK, :], filled(t)[0:RANK, 0:TA], ACT.Copy).then_inc(evac[t[0]], 1)
            for i in range(8):
                t = plan["r"][1].at(i)
                nc.scalar.activation(tile(g_r, i, TA), filled(t)[:, 0:TA], ACT.Silu).then_inc(evac[t[0]], 1)
            t = plan["gate"].at(3)
            act.wait_ge(evac[t[0]], t[1] + 1)
            did(nc.scalar.activation(g_e[0], g_b, ACT.Abs))
            own()
            did(nc.scalar.activation(g_e[1], g_e[0], ACT.Exp, scale=-1.0))
            own()
            nc.scalar.activation(g_e[2], g_e[1], ACT.Ln, bias=C("ones", 0, 1)).then_inc(soft_made, 1)
            act.wait_ge(decay_in, 1)
            nc.scalar.activation(g_e[0], g_b, ACT.Exp, scale=1.0 / 16).then_inc(decay_made, 1)
            nc.scalar.activation(g_e[1], g_b, ACT.Exp, scale=-1.0 / 16).then_inc(decay_made, 1)
            act.wait_ge(decay_in, 2)
            nc.scalar.activation(g_e[2], g_e[2], ACT.Exp, scale=1.0 / 16).then_inc(decay_made, 1)
            for i in range(GH):
                t = plan["kwT"].at(i)
                bank = filled(t)
                nc.scalar.activation(g_kwT[:, i * 384:i * 384 + 256], bank[:, 0:256], ACT.Copy)
                nc.scalar.activation(g_kwT[0:META, i * 384 + 256:(i + 1) * 384], bank[0:META, 256:384], ACT.Copy)\
                    .then_inc(evac[t[0]], 1)
            for i in range(8):
                t = plan["o"].at(i)
                bank = filled(t)
                nc.scalar.activation(tile(g_sq, i, TA), bank[:, 0:TA], ACT.Square)
                nc.scalar.activation(tile(g_o, i, TA), bank[:, 0:TA], ACT.Copy).then_inc(evac[t[0]], 1)
            for i in range(GH):
                root(plan["gst"].at(i), tile(g_kw, i, TA), tile(g_kw, i, TA))
            branch_out(plan["gout"][1], 3, 3, par, TA)
            squares_of_h(4, TA)
            root_stat(4, TA)
            ffn(1, 5, TA)
            squares_of_h(6, TA)
            root_stat(6, TA)

            for i in range(2):
                t = plan["ks"][1].at(i)
                nc.scalar.activation(tile(s_kraw, i, TA), filled(t)[:, 0:TA], ACT.Copy).then_inc(evac[t[0]], 1)
            for i, n in enumerate((P, P, META)):
                t = plan["vs"][1].at(i)
                nc.scalar.activation(vs[0:n, i, :], filled(t)[0:n, 0:256], ACT.Copy).then_inc(evac[t[0]], 1)
            ffn(2, 7, SEQ)
            squares_of_h(8, SEQ)
            root_stat(8, SEQ)

            for i in range(8):
                t = plan["sq"][1].at(i)
                nc.scalar.activation(s_q[:, i * SEQ:(i + 1) * SEQ], filled(t)[:, 0:SEQ], ACT.Copy).then_inc(evac[t[0]], 1)

            def attend(names, groups, first, pb, pT, widths, n_full, meta, o, sinks):
                S, TT, V = (plan[x] for x in names)
                for g in range(groups):
                    at = 16 + (g % 2) * 16
                    act.wait_ge(neg_max, first + g + 1)
                    if sinks:
                        nc.scalar.activation(small[:, at + 4:at + 8], small[:, at + 4:at + 8], ACT.Exp)
                    for u in range(4):
                        p = pb[:, ((g % 2) * 4 + u) * TA:((g % 2) * 4 + u) * TA + widths[u // 2]]
                        e = nc.scalar.activation(p, p, ACT.Exp, bias=small[:, at + u:at + u + 1],
                                                 accum_out=small[:, at + 8 + u:at + 9 + u])
                        if u == 3:
                            e.then_inc(exp_made, 1)
                    for u in range(4):
                        t = TT.at(4 * g + u)
                        bank = filled(t)
                        if g:
                            act.wait_ge(full[V.at(g - 1)[0]], V.at(g - 1)[1] + 1)
                        n = n_full[u // 2] * P
                        c = nc.scalar.activation(pT[:, u * 384:u * 384 + n], bank[:, 0:n], ACT.Copy)
                        if meta:
                            c = nc.scalar.activation(pT[0:META, u * 384 + n:u * 384 + n + P], bank[0:META, n:n + P], ACT.Copy)
                        c.then_inc(evac[t[0]], 1)
                    t = V.at(g)
                    nc.scalar.activation(o[:, g * SEQ:(g + 1) * SEQ], filled(t)[:, 0:SEQ], ACT.Copy).then_inc(evac[t[0]], 1)

            attend(("ss", "sT", "sv"), 8, 0, a_p, a_pT, (P + META, SEQ + META), (1, 2), True, s_o, True)
            branch_out(plan["sout"][1], 9, 9, par, SEQ)
            squares_of_h(10, SEQ)
            root_stat(10, SEQ)
            ffn(3, 11, SEQ)

            def b_in(i):
                return W("b_in", i, i + 1)

            def sect(name, i, dst, func, col):
                t = plan[name][1].at(i)
                nc.scalar.activation(dst, filled(t)[:, 0:SEQ], func, bias=b_in(col)).then_inc(evac[t[0]], 1)

            for i in range(4):
                t = plan["z"][1].at(i)
                bank = filled(t)
                nc.scalar.activation(b_e[:, i * SEQ:(i + 1) * SEQ], bank[:, 0:SEQ], ACT.Sigmoid, bias=b_in(4 + i))
                nc.scalar.activation(b_kf[:, i * SEQ:(i + 1) * SEQ], bank[:, 0:SEQ], ACT.Sigmoid, scale=-1.0,
                                     bias=small[:, 12 + i:13 + i]).then_inc(evac[t[0]], 1)
            for i in range(4):
                sect("hq", i, b_q[:, i * SEQ:(i + 1) * SEQ], ACT.Silu, i)
            act.wait_ge(hg_arg, 1)
            nc.scalar.activation(b_b, b_e, ACT.Ln).then_inc(hg_ln, 1)
            for j in range(8):
                for i in range(2):
                    name, m = ("ga", 2 * j + i) if j < 4 else ("gb", 2 * (j - 4) + i)
                    buf = b_sga if j < 4 else b_sgb
                    sect(name, m, buf[:, m * SEQ:(m + 1) * SEQ], ACT.Sigmoid, (28 if j < 4 else 36) + m)
                act.wait_ge(lvl_in, j + 1)
                nc.scalar.activation(b_e, b_e, ACT.Exp).then_inc(lvl_exp, 1)
            for i in range(4):
                sect("hgate", i, b_sg[:, i * SEQ:(i + 1) * SEQ], ACT.Silu, 12 + i)
            for i in range(4):
                sect("mq", i, b_mq[:, i * SEQ:(i + 1) * SEQ], ACT.Identity, 16 + i)
            for i in range(4):
                sect("mk", i, b_mk[:, i * SEQ:(i + 1) * SEQ], ACT.Identity, 20 + i)
            for i in range(4):
                t = plan["ho"].at(i)
                bank = filled(t)
                nc.scalar.activation(b_sq[:, i * SEQ:(i + 1) * SEQ], bank[:, 0:SEQ], ACT.Square)
                nc.scalar.activation(b_a[:, i * SEQ:(i + 1) * SEQ], bank[:, 0:SEQ], ACT.Copy).then_inc(evac[t[0]], 1)
            for i in range(4):
                root(plan["hst"].at(i), b_e[:, i * SEQ:(i + 1) * SEQ], b_e[:, i * SEQ:(i + 1) * SEQ])
            attend(("bs", "bT", "bv"), 4, 8, b_p, b_pT, (P, SEQ), (1, 2), False, b_bo, False)
            h3 = h[:, :].rearrange("p (m t) -> p m t", m=KT)[:, :, 0:SEQ]
            z3 = zg[:, :].rearrange("p (m t) -> p m t", m=KT)[:, :, 0:SEQ]
            act.wait_ge(centred, 1)
            nc.scalar.activation(z3, h3, ACT.Square).then_inc(ln_squared, 1)
            root(plan["lnvar"].at(0), var[:, 0:SEQ], std[:, 0:SEQ])
            for i in range(4):
                t = plan["xtok"].at(i)
                nc.scalar.activation(m_x[:, (i // 2) * D + (i % 2) * 512:(i // 2) * D + (i % 2) * 512 + 512],
                                     filled(t)[:, :], ACT.Copy).then_inc(evac[t[0]], 1)
            act.wait_ge(route_in, 1)
            nc.scalar.activation(r_["ge"], r_["ge"], ACT.Exp).then_inc(route_exp, 1)
            act.wait_ge(route_in, 2)
            nc.scalar.activation(r_["ev"], r_["ev"], ACT.Exp).then_inc(route_exp, 1)

            act.wait_ge(table_ready, 1)
            n_blocks = act.value_load(meta_i[0:1, MAXB:MAXB + 1], min_val=1, max_val=MAXB)
            t = plan["e_gather"].at(0)
            nc.scalar.activation(m_xT, filled(t)[:, :], ACT.Copy).then_inc(evac[4], 1)
            with act.Fori(0, n_blocks) as b:
                act.wait_ge(full[5], E_BASE[5] + b + 1)
                act.wait_ge(evac[5], E_BASE[5] + b)
                nc.scalar.activation(m_sg, ps[5][:, 0:256], ACT.Silu).then_inc(silu_made, 1)
                act.wait_ge(full[4], E_BASE[4] + b + 1)
                nc.scalar.activation(m_xT, ps[4][:, :], ACT.Copy).then_inc(evac[4], 1)
                act.wait_ge(full[6], E_BASE[6] + b + 1)
                nc.scalar.activation(m_turn, ps[6][:, :], ACT.Copy).then_inc(evac[6], 1)

            for p in range(2):
                act.wait_ge(fin_centred, p + 1)
                nc.scalar.activation(zg[:, p * D:(p + 1) * D], m_o[:, p * D:(p + 1) * D], ACT.Square,
                                     accum_out=small[:, 100 + p:101 + p]).then_inc(fin_squared, 1)
            act.wait_ge(fin_var, 1)
            nc.scalar.activation(small[:, 104:106], small[:, 102:104], ACT.Sqrt).then_inc(fin_std, 1)
            for p in range(2):
                act.wait_ge(out_ready, p + 1)
                act.dma_start(out[0, p * P:(p + 1) * P, :], m_o[:, p * D:(p + 1) * D]).then_inc(out_stored, 16)
            act.wait_ge(out_stored, 32)

        @block.vector
        def _(dve):
            chain = [0]
            stds = [0]
            v = nc.vector

            def did(ins):
                ins.then_inc(dve_chain, 1)
                chain[0] += 1
                return chain[0]

            def own(c=None):
                dve.wait_ge(dve_chain, chain[0] if c is None else c)

            def then(ins):
                did(ins)
                own()

            def filled(t):
                dve.wait_ge(full[t[0]], t[1] + 1)
                return ps[t[0]]

            def mine(t):
                dve.wait_ge(evac[t[0]], t[1] + 1)

            def add_square(n, m, w):
                q = 8 * n + m
                dve.wait_ge(sq_made, q + 1)
                if m == 0:
                    v.tensor_copy(acc[:, 0:w], sq[:, q % 2, 0:w]).then_inc(sq_used, 1)
                else:
                    dve.wait_ge(sq_used, q)
                    v.tensor_tensor(acc[:, 0:w], acc[:, 0:w], sq[:, q % 2, 0:w], ALU.add).then_inc(sq_used, 1)

            def inverse_root(t, w, mean_of, eps, mid, root, dst):
                bank = filled(t)
                v.tensor_scalar(mid, bank[:, 0:w], 1.0 / mean_of, eps, ALU.mult, ALU.add).then_inc(evac[t[0]], 1)
                stds[0] += 1
                dve.wait_ge(std_made, stds[0])
                then(v.reciprocal(dst, root))

            def inverse_rms(n, w):
                inverse_root(plan[f"stat{n}"].at(0), w, D, EPS, var[:, 0:w], std[:, 0:w], rs[:, 0:w])

            def normalise(g, dst, w, col=None):
                for m in range(KT):
                    gm = gain(g, m) if col is None else W(col, m, m + 1)
                    v.scalar_tensor_tensor(tile(dst, m, w), tile(h, m, w), gm, rs[:, 0:w],
                                           ALU.mult, ALU.mult).then_inc(hn_ready, 1)

            def residual(T, n, w, follow=True):
                for m in range(KT):
                    add_square(n, m, w)
                inverse_rms(n, w)
                for m in range(KT):
                    mine(T.at(m))
                steps = [did(v.tensor_tensor(tile(zg, 0, w), tile(zg, 0, w), rs[:, 0:w], ALU.mult))]
                for m in range(KT):
                    if m + 1 < KT:
                        z = tile(zg, m + 1, w)
                        steps.append(did(v.tensor_tensor(z, z, rs[:, 0:w], ALU.mult)))
                    own(steps[m])
                    v.tensor_tensor(tile(h, m, w), tile(h, m, w), tile(zg, m, w), ALU.add).then_inc(h_ready, 1)
                    if follow and m:
                        add_square(n + 1, m - 1, w)
                if follow:
                    add_square(n + 1, KT - 1, w)
                    inverse_rms(n + 1, w)

            def ffn_in(n, w):
                T = plan[f"in{n}"][1]
                with dve.Fori(0, FT // 2) as it:
                    for j in range(2):
                        tg, tu = T.at(2 * j, it, 4), T.at(2 * j + 1, it, 4)
                        dve.wait_ge(full[tu[0]], tu[1] + 1)
                        dve.wait_ge(evac[tg[0]], tg[1] + 1)
                        v.tensor_tensor(hid[:, bass.ds(it * (2 * TA) + j * TA, w)], ps[tu[0]][:, 0:w],
                                        tile(sg, j, w), ALU.mult).then_inc(evac[tu[0]], 1)

            dve.wait_ge(params_in, 16)
            l0, l1 = W("lb_logits", 0, 4), W("lb_logits", 4, 8)
            then(v.tensor_tensor(small[:, 8:12], l0, l1, ALU.max))
            did(v.tensor_tensor(small[:, 0:4], l0, small[:, 8:12], ALU.subtract))
            v.tensor_tensor(small[:, 4:8], l1, small[:, 8:12], ALU.subtract).then_inc(lb_in, 1)
            v.tensor_scalar(halfg[:, :], W("gains"), 0.5, None, ALU.mult).then_inc(lb_in, 1)
            then(v.tensor_scalar(small[:, 12:16], W("b_in", 4, 8), -1.0, None, ALU.mult))
            dve.wait_ge(lb_exp, 1)
            then(v.tensor_tensor(small[:, 8:12], small[:, 0:4], small[:, 4:8], ALU.add))
            then(v.reciprocal(small[:, 8:12], small[:, 8:12]))
            LB, LB1 = slice(240, 244), slice(244, 248)
            then(v.tensor_tensor(small[:, LB], small[:, 0:4], small[:, 8:12], ALU.mult))
            then(v.tensor_scalar(small[:, LB1], small[:, LB], -1.0, 1.0, ALU.mult, ALU.add))

            for m in range(KT):
                add_square(0, m, TA)
            inverse_rms(0, TA)
            dve.wait_ge(x_in, 16)
            normalise(0, hn, TA)
            dve.wait_ge(bias_out, 8 * 16)
            ffn_in(0, TA)
            residual(plan["out0"][1], 1, TA)
            normalise(2, hn, TA)

            for i in range(GH):
                t = plan["gate"].at(i)
                v.tensor_scalar(tile(g_b, i, TA), filled(t)[:, 0:TA], W("b_gate", i, i + 1), None, ALU.add)\
                    .then_inc(evac[t[0]], 1)
            mine(plan["gate"].at(3))
            dve.wait_ge(soft_made, 1)
            then(v.tensor_scalar(g_b, g_b, 0.0, None, ALU.min))
            then(v.tensor_tensor(g_e[2], g_b, g_e[2], ALU.subtract))
            for i in range(GH):
                s = v.tensor_tensor_scan(tile(g_b, i, TA), C("reset_g"), tile(g_e[2], i, TA), 0.0, ALU.mult, ALU.add)
            s.then_inc(decay_in, 1)
            dve.wait_ge(decay_in, 1)
            b4 = g_b.rearrange("p (h t) -> p h t", h=GH)
            e4 = g_e[2].rearrange("p (h t) -> p h t", h=GH)
            for i in range(GH):
                bx = g_b[:, i * TA:i * TA + SEQ].rearrange("p (c s) -> p c s", s=CH)
                ex = g_e[2][:, i * TA:i * TA + SEQ].rearrange("p (c s) -> p c s", s=CH)
                v.tensor_tensor(ex, bx[:, :, CH - 1:CH].to_broadcast([P, 4, CH]), bx, ALU.subtract)
            v.tensor_tensor(e4[:, :, SEQ:TA], b4[:, :, TA - 1:TA].to_broadcast([P, GH, META]), b4[:, :, SEQ:TA],
                            ALU.subtract).then_inc(decay_in, 1)
            for j in range(4):
                for s, n in enumerate((P, P, META)):
                    t = plan["v"][1].at(3 * j + s)
                    dst = g_vm[0:n, j * 256:(j + 1) * 256] if s == 2 else g_v[:, s * D + j * 256:s * D + (j + 1) * 256]
                    v.tensor_copy(dst, filled(t)[0:n, 0:256]).then_inc(evac[t[0]], 1)
            dve.wait_ge(decay_made, 3)
            for i in range(GH):
                t = plan["k"][1].at(i)
                bank = filled(t)
                v.tensor_tensor(tile(g_k, i, TA), bank[:, 0:TA], tile(g_e[1], i, TA), ALU.mult)
                v.tensor_tensor(tile(g_kw, i, TA), bank[:, 0:TA], tile(g_e[2], i, TA), ALU.mult).then_inc(evac[t[0]], 1)
            for i in range(GH):
                t = plan["q"][1].at(i)
                v.scalar_tensor_tensor(tile(g_q, i, TA), filled(t)[:, 0:TA], float(GDK) ** -0.5, tile(g_e[0], i, TA),
                                       ALU.mult, ALU.mult).then_inc(evac[t[0]], 1)
            for i in range(GH):
                t = plan["att"].at(i)
                bank = filled(t)
                v.tensor_tensor(g_att[:, i * TA:i * TA + SEQ].rearrange("p (a b) -> p a b", a=2),
                                bank[:, 0:SEQ].rearrange("p (a b) -> p a b", a=2),
                                C("pairmask").rearrange("p (a b) -> p a b", a=1).to_broadcast([P, 2, P]), ALU.mult)
                v.tensor_tensor(g_att[0:META, i * TA + SEQ:(i + 1) * TA], bank[0:META, SEQ:TA],
                                C("pairmask", 0, META, slice(0, META)), ALU.mult).then_inc(evac[t[0]], 1)
            for i in range(GH):
                def state(c):
                    return g_s[:, (i * 4 + c) * GDV:(i * 4 + c + 1) * GDV]

                def decay(c):
                    return g_e[0][:, i * TA + c * CH + CH - 1:i * TA + c * CH + CH]

                ta, tb, tc = (plan["kv"].at(3 * i + c) for c in range(3))
                bank = filled(ta)
                then(v.tensor_copy(state(0), bank[:, 0:256]))
                v.scalar_tensor_tensor(state(1), state(0), decay(0), bank[:, 256:512], ALU.mult, ALU.add)\
                    .then_inc(evac[ta[0]], 1)
                mine(ta)
                v.scalar_tensor_tensor(state(2), state(1), decay(1), filled(tb)[:, 0:256], ALU.mult, ALU.add)\
                    .then_inc(evac[tb[0]], 1)
                mine(tb)
                v.scalar_tensor_tensor(state(3), state(2), decay(2), filled(tc)[:, 0:256], ALU.mult, ALU.add)\
                    .then_inc(evac[tc[0]], 1)
            for i in range(GH):
                r = tile(g_kw, i, TA)
                inverse_root(plan["gst"].at(i), TA, GDV, EPS, r, r, r)
                for half in range(2):
                    o = tile(g_o, 2 * i + half, TA)
                    then(v.scalar_tensor_tensor(o, o, W("gla_norm", half, half + 1), r, ALU.mult, ALU.mult))
                    v.tensor_tensor(o, o, tile(g_r, 2 * i + half, TA), ALU.mult).then_inc(gated, 1)
            residual(plan["gout"][1], 3, TA)
            normalise(4, hn, TA)
            ffn_in(1, TA)
            residual(plan["out1"][1], 5, TA)
            normalise(None, hk, TA, "kv_norm")
            normalise(6, hn, TA)

            for i in range(2):
                t = plan["krot"].at(i)
                bank = filled(t)
                v.tensor_tensor(tile(s_krot, i, TA), bank[:, 0:TA], C("sin"), ALU.mult).then_inc(evac[t[0]], 1)
                mine(plan["ks"][1].at(i))
                then(v.tensor_tensor(kT[:, i, :], tile(s_kraw, i, TA), C("cos"), ALU.mult))
                then(v.tensor_tensor(kT[:, i, :], kT[:, i, :], tile(s_krot, i, TA), ALU.add))
            ffn_in(2, SEQ)
            residual(plan["out2"][1], 7, SEQ)
            normalise(8, hn, SEQ)

            for i in range(8):
                t = plan["qrot"].at(i)
                bank = filled(t)
                mine(plan["sq"][1].at(i))
                q = s_q[:, i * SEQ:(i + 1) * SEQ]
                x = s_t[:, (i % 2) * SEQ:(i % 2 + 1) * SEQ]
                did(v.tensor_tensor(q, q, C("cos", 0, SEQ), ALU.mult))
                v.tensor_tensor(x, bank[:, 0:SEQ], C("sin", 0, SEQ), ALU.mult).then_inc(evac[t[0]], 1)
                own()
                mine(t)
                v.tensor_tensor(q, q, x, ALU.add).then_inc(q_roped, 1)

            def attend(names, groups, first, pb, widths, mask_of, sinks):
                S = plan[names[0]]

                def maxima(g):
                    at = 16 + (g % 2) * 16
                    for u in range(4):
                        w = widths[u // 2]
                        t = S.at(4 * g + u)
                        p = pb[:, ((g % 2) * 4 + u) * TA:((g % 2) * 4 + u) * TA + w]
                        v.scalar_tensor_tensor(p, filled(t)[:, 0:w], 0.125, mask_of(g, u), ALU.mult, ALU.add)\
                            .then_inc(evac[t[0]], 1)
                    mine(t)
                    p4 = pb[:, (g % 2) * 4 * TA:(g % 2 + 1) * 4 * TA].rearrange("p (u t) -> p u t", u=4)
                    did(v.tensor_reduce(small[:, at:at + 2], p4[:, 0:2, 0:widths[0]], AX, ALU.max))
                    then(v.tensor_reduce(small[:, at + 2:at + 4], p4[:, 2:4, 0:widths[1]], AX, ALU.max))
                    if sinks:
                        sk = W("sinks", 4 * g, 4 * g + 4)
                        then(v.tensor_tensor(small[:, at:at + 4], small[:, at:at + 4], sk, ALU.max))
                        then(v.tensor_scalar(small[:, at:at + 4], small[:, at:at + 4], -1.0, None, ALU.mult))
                        v.tensor_tensor(small[:, at + 4:at + 8], small[:, at:at + 4], sk, ALU.add).then_inc(neg_max, 1)
                    else:
                        v.tensor_scalar(small[:, at:at + 4], small[:, at:at + 4], -1.0, None, ALU.mult)\
                            .then_inc(neg_max, 1)

                maxima(0)
                for g in range(groups):
                    if g + 1 < groups:
                        maxima(g + 1)
                    at = 16 + (g % 2) * 16
                    dve.wait_ge(exp_made, first + g + 1)
                    if sinks:
                        then(v.tensor_tensor(small[:, at + 8:at + 12], small[:, at + 8:at + 12],
                                             small[:, at + 4:at + 8], ALU.add))
                    then(v.reciprocal(small[:, at + 12:at + 16], small[:, at + 8:at + 12]))
                    for u in range(4):
                        p = pb[:, ((g % 2) * 4 + u) * TA:((g % 2) * 4 + u) * TA + widths[u // 2]]
                        v.tensor_scalar(p, p, small[:, at + 12 + u:at + 13 + u], None, ALU.mult).then_inc(p_ready, 1)

            attend(("ss",), 8, 0, a_p, (P + META, SEQ + META), lambda g, u: C("swa0") if u < 2 else C("swa1"), True)
            residual(plan["sout"][1], 9, SEQ)
            normalise(10, hn, SEQ)
            ffn_in(3, SEQ)
            residual(plan["out3"][1], 11, SEQ, follow=False)

            dve.wait_ge(bias_in, 8 * 16)
            for i in range(8):
                last = v.tensor_tensor(b_bias[:, i * SEQ:(i + 1) * SEQ], b_bias[:, i * SEQ:(i + 1) * SEQ], C("ninf"), ALU.add)
            did(last)
            did(v.memset(b_att[:, 0:1024], 0.0))
            for i in range(4):
                t = plan["z"][1].at(i)
                mine(t)
                e = b_e[:, i * SEQ:(i + 1) * SEQ]
                k = b_kf[:, i * SEQ:(i + 1) * SEQ]
                did(v.tensor_scalar(k, k, small[:, 244 + i:245 + i], None, ALU.mult))
                a = v.tensor_scalar(e, e, small[:, 244 + i:245 + i], small[:, 240 + i:241 + i], ALU.mult, ALU.add)
            a.then_inc(hg_arg, 1)
            dve.wait_ge(hg_ln, 1)
            then(v.tensor_copy(b_e, b_b))
            for i in range(4):
                did(v.tensor_tensor_scan(b_b[:, i * SEQ:(i + 1) * SEQ], C("reset_h"), b_e[:, i * SEQ:(i + 1) * SEQ],
                                         0.0, ALU.mult, ALU.add))
            own()
            dve.wait_ge(levels_in, 16)

            def merge(n):
                for p in range(2):
                    t = plan["lvl"].at(2 * n + p)
                    bank = filled(t)
                    mask = b_lv[:, n * P:(n + 1) * P].bitcast(U32).rearrange("p (a s) -> p a s", a=1).to_broadcast([P, 4, P])
                    v.copy_predicated(b_att[:, p * 512:(p + 1) * 512].rearrange("p (a s) -> p a s", a=4), mask,
                                      bank[:, :].rearrange("p (a s) -> p a s", a=4)).then_inc(evac[t[0]], 1)

            for n in range(8):
                half = LEVELS[n] if n < 7 else P
                b3 = b_b.rearrange("p (g e s) -> p g e s", e=2, s=half)
                d3 = b_e.rearrange("p (g e s) -> p g e s", e=2, s=half)
                G = 4 * SEQ // (2 * half)
                ref = b3[:, :, 0, half - 1:half].to_broadcast([P, G, half])
                did(v.tensor_tensor(d3[:, :, 0, :], ref, b3[:, :, 0, :], ALU.subtract))
                if n < 7:
                    last = v.tensor_tensor(d3[:, :, 1, :], b3[:, :, 1, :], ref, ALU.subtract)
                else:
                    last = v.tensor_copy(d3[:, :, 1, :], b3[:, :, 1, :])
                last.then_inc(lvl_in, 1)
                if n:
                    t = plan["lvl"].at(2 * (n - 1) + 1)
                    filled(t)
                dve.wait_ge(lvl_exp, n + 1)
                q3, k3, w3 = (x.rearrange("p (g e s) -> p g e s", e=2, s=half) for x in (b_q, b_kf, b_qk))
                if n == 0:
                    mine(plan["hq"][1].at(3))
                did(v.tensor_tensor(w3[:, :, 0, :], k3[:, :, 0, :], d3[:, :, 0, :], ALU.mult))
                v.tensor_tensor(w3[:, :, 1, :], q3[:, :, 1, :], d3[:, :, 1, :], ALU.mult).then_inc(lvl_ready, 1)
                dve.wait_ge(lvl_ready, n + 1)
                if n:
                    merge(n - 1)
                    mine(plan["lvl"].at(2 * (n - 1) + 1))
            merge(7)
            t = plan["cross"].at(0)
            v.tensor_copy(b_att[:, 1024:1536], filled(t)[:, :]).then_inc(evac[t[0]], 1)
            dve.wait_ge(rows_in, 16)
            for name, dst, at in (("hi", b_v, 0), ("mv", b_mv, 512)):
                for j in range(2):
                    for p in range(2):
                        t = plan[name][1].at(2 * j + p)
                        v.tensor_tensor(dst[:, p * 512 + j * 256:p * 512 + (j + 1) * 256], filled(t)[:, 0:256],
                                        b_rows[:, at + j * 256:at + (j + 1) * 256], ALU.add).then_inc(evac[t[0]], 1)
            for i in range(4):
                r = b_e[:, i * SEQ:(i + 1) * SEQ]
                inverse_root(plan["hst"].at(i), SEQ, P, LN_EPS, r, r, r)
                mine(plan["hgate"][1].at(i))
                o = b_a[:, i * SEQ:(i + 1) * SEQ]
                then(v.scalar_tensor_tensor(o, o, W("hg_norm", i, i + 1), r, ALU.mult, ALU.mult))
                v.tensor_tensor(o, o, b_sg[:, i * SEQ:(i + 1) * SEQ], ALU.mult).then_inc(hgo_ready, 1)

            def moba_bias(g, u):
                head = 2 * g + u % 2
                return b_bias[:, head * SEQ + P:(head + 1) * SEQ] if u < 2 else b_bias[:, head * SEQ:(head + 1) * SEQ]

            attend(("bs",), 4, 8, b_p, (P, SEQ), moba_bias, False)

            for i in range(KT):
                t = plan["pa"][1].at(i)
                v.tensor_tensor(tile(zg, i, SEQ), filled(t)[:, 0:SEQ], b_sga[:, i * SEQ:(i + 1) * SEQ], ALU.mult)\
                    .then_inc(evac[t[0]], 1)
            for i in range(KT):
                t = plan["pb"][1].at(i)
                gate = b_sgb[:, i * SEQ:(i + 1) * SEQ]
                v.tensor_tensor(gate, filled(t)[:, 0:SEQ], gate, ALU.mult).then_inc(evac[t[0]], 1)
                mine(t)
                v.tensor_tensor(tile(zg, i, SEQ), tile(zg, i, SEQ), gate, ALU.add).then_inc(mixed, 1)
            for i in range(KT):
                t = plan["wo"][1].at(i)
                v.scalar_tensor_tensor(tile(h, i, SEQ), tile(h, i, SEQ), ALPHA, filled(t)[:, 0:SEQ], ALU.mult, ALU.add)\
                    .then_inc(evac[t[0]], 1)
            mine(t)
            h3 = h[:, :].rearrange("p (m t) -> p m t", m=KT)[:, :, 0:SEQ]
            ht = h[:, :].rearrange("p (m t) -> p t m", m=KT)[:, 0:SEQ, :]
            zt = zg[:, :].rearrange("p (m t) -> p t m", m=KT)[:, 0:SEQ, :]

            def over_tiles(x):
                return x.rearrange("p (a t) -> p a t", a=1).to_broadcast([P, KT, SEQ])

            v.tensor_reduce(acc[:, 0:SEQ], ht, AX, ALU.add).then_inc(ln_in, 1)
            t = plan["mean"].at(0)
            v.tensor_scalar(var[:, 0:SEQ], filled(t)[:, 0:SEQ], 1.0 / D, None, ALU.mult).then_inc(evac[t[0]], 1)
            mine(t)
            v.tensor_tensor(h3, h3, over_tiles(var[:, 0:SEQ]), ALU.subtract).then_inc(centred, 1)
            dve.wait_ge(centred, 1)
            dve.wait_ge(ln_squared, 1)
            v.tensor_reduce(acc[:, 0:SEQ], zt, AX, ALU.add).then_inc(ln_in, 1)
            inverse_root(plan["lnvar"].at(0), SEQ, D, LN_EPS, var[:, 0:SEQ], std[:, 0:SEQ], rs[:, 0:SEQ])
            then(v.tensor_tensor(h3, h3, over_tiles(rs[:, 0:SEQ]), ALU.mult))
            for m in range(KT):
                v.tensor_scalar(tile(h, m, SEQ), tile(h, m, SEQ), W("ln1_g", m, m + 1), W("ln1_b", m, m + 1),
                                ALU.mult, ALU.add).then_inc(x2_ready, 1)

            def two(x):
                return x.rearrange("p (a n) -> p a n", a=2)

            def spread(col, n):
                return col.rearrange("p (a n) -> p a n", n=1).to_broadcast([P, 2, n])

            def first_max(x, n, top, tmp, one):
                then(v.tensor_reduce(top, two(x), AX, ALU.max))
                then(v.tensor_tensor(two(tmp), two(x), spread(top, n), ALU.is_equal))
                places = C("iota32", 0, n).rearrange("p (a n) -> p a n", a=1).to_broadcast([P, 2, n])
                then(v.scalar_tensor_tensor(two(tmp), two(tmp), -64.0, places, ALU.mult, ALU.add))
                then(v.tensor_reduce(r_["place"], two(tmp), AX, ALU.min))
                then(v.tensor_tensor(two(one), two(tmp), spread(r_["place"], n), ALU.is_equal))

            t = plan["route"].at(0)
            bank = filled(t)
            lg = r_["lg"]
            v.tensor_tensor(two(lg), bank[:, 0:128].rearrange("p (a n) -> p a n", a=2)[:, :, 0:36],
                            W("b_route").rearrange("p (a n) -> p a n", a=1).to_broadcast([P, 2, 36]), ALU.add)\
                .then_inc(evac[t[0]], 1)
            mine(t)
            did(v.tensor_copy(two(r_["gl"]), two(lg)[:, :, 0:4]))
            then(v.tensor_copy(two(r_["em"]), two(lg)[:, :, 4:36]))
            first_max(r_["gl"], 4, r_["gtop"], r_["gt"], r_["g1"])
            v.tensor_tensor(two(r_["ge"]), two(r_["gl"]), spread(r_["gtop"], 4), ALU.subtract).then_inc(route_in, 1)
            then(v.tensor_scalar(r_["g1"], r_["g1"], -NEG, NEG, ALU.mult, ALU.add))
            e3 = r_["em"].rearrange("p (a n) -> p a n", n=8)
            then(v.tensor_tensor(e3, e3, r_["g1"].rearrange("p (a n) -> p a n", n=1).to_broadcast([P, 8, 8]), ALU.add))
            first_max(r_["em"], 32, r_["top1"], r_["tmp"], r_["o1"])
            then(v.scalar_tensor_tensor(r_["em"], r_["o1"], 3 * NEG, r_["em"], ALU.mult, ALU.add))
            first_max(r_["em"], 32, r_["top2"], r_["tmp"], r_["o2"])
            v.tensor_tensor(m_r[:, 0:64], r_["o1"], r_["o2"], ALU.add).then_inc(m_ready, 1)
            v.tensor_tensor(r_["ev"], r_["top2"], r_["top1"], ALU.subtract).then_inc(route_in, 1)
            dve.wait_ge(route_exp, 1)
            then(v.tensor_reduce(r_["pg"], two(r_["ge"]), AX, ALU.add))
            then(v.reciprocal(r_["pg"], r_["pg"]))
            dve.wait_ge(route_exp, 2)
            then(v.tensor_scalar(r_["w1"], r_["ev"], 1.0, None, ALU.add))
            then(v.reciprocal(r_["w1"], r_["w1"]))
            then(v.tensor_tensor(r_["w1"], r_["w1"], r_["pg"], ALU.mult))
            then(v.tensor_tensor(r_["w2"], r_["w1"], r_["ev"], ALU.mult))
            t = plan["cnt"].at(0)
            v.tensor_copy(r_["cnt"], filled(t)[:, 0:32]).then_inc(evac[t[0]], 1)
            mine(t)
            then(v.tensor_scalar(r_["nb"], r_["cnt"], 0.0, None, ALU.is_gt))
            for j in range(1, SEQ // SLOTS):
                then(v.scalar_tensor_tensor(r_["nb"], r_["cnt"], float(SLOTS * j), r_["nb"], ALU.is_gt, ALU.add))
            then(v.tensor_tensor_scan(r_["end"], C("ones", 0, 32), r_["nb"], 0.0, ALU.mult, ALU.add))
            then(v.tensor_tensor(r_["beg"], r_["end"], r_["nb"], ALU.subtract))
            then(v.tensor_scalar(r_["beg"], r_["beg"], float(SLOTS), None, ALU.mult))
            cmp3 = r_["cmp"][0:1, :].rearrange("p (b e) -> p b e", e=32)
            then(v.tensor_tensor(cmp3, r_["end"][0:1, :].rearrange("p (a e) -> p a e", a=1).to_broadcast([1, MAXB, 32]),
                                 C("iotab", 0, MAXB, slice(0, 1)).rearrange("p (b a) -> p b a", a=1).to_broadcast([1, MAXB, 32]),
                                 ALU.is_le))
            then(v.tensor_reduce(r_["eb"][0:1, :], cmp3, AX, ALU.add))
            then(v.tensor_scalar(meta_i[0:1, 0:MAXB], r_["eb"][0:1, :], float(NE - 1), None, ALU.min))
            then(v.tensor_copy(meta_i[0:1, MAXB:MAXB + 1], r_["end"][0:1, 31:32]))
            t = plan["pos"].at(0)
            bank = filled(t)
            v.tensor_tensor(two(r_["em"]), two(bank[:, 0:64]),
                            r_["beg"].rearrange("p (a n) -> p a n", a=1).to_broadcast([P, 2, 32]), ALU.add)\
                .then_inc(evac[t[0]], 1)
            mine(t)
            for k, one in ((0, "o1"), (1, "o2")):
                then(v.tensor_tensor(r_["tmp"], r_["em"], r_[one], ALU.mult))
                then(v.tensor_reduce(r_["dest"][:, 2 * k:2 * k + 2], two(r_["tmp"]), AX, ALU.add))
            did(v.memset(m_zero, 0.0))
            did(v.memset(m_y, 0.0))
            v.memset(m_turn, 0.0).then_inc(table_ready, 1)

            def col(x, i):
                return r_[x][:, i:i + 1]

            def choose():
                for p in range(2):
                    e = v.tensor_scalar(m_t[:, p * 64:(p + 1) * 64], C("iota"), col("dest", p), None, ALU.is_equal)
                return e

            def choose_2():
                for p in range(2):
                    e = v.scalar_tensor_tensor(m_P[:, p * 64:(p + 1) * 64], C("iota"), col("dest", 2 + p),
                                               m_t[:, p * 64:(p + 1) * 64], ALU.is_equal, ALU.add)
                return e

            def weigh():
                for p in range(2):
                    v.tensor_scalar(m_t[:, 128 + p * 64:192 + p * 64], C("iota"), col("dest", p), col("w1", p),
                                    ALU.is_equal, ALU.mult)
                    e = v.tensor_scalar(m_t[:, 256 + p * 64:320 + p * 64], C("iota"), col("dest", 2 + p), col("w2", p),
                                        ALU.is_equal, ALU.mult)
                return e

            def weigh_2():
                for p in range(2):
                    a, b = (m_t[:, x + p * 64:x + 64 + p * 64].rearrange("p (a s) -> p a s", a=1).to_broadcast([P, 2, 64])
                            for x in (128, 256))
                    e = v.tensor_tensor(m_PW[:, p * P:(p + 1) * P].rearrange("p (a s) -> p a s", a=2), a, b, ALU.add)
                return e

            def move_on():
                return v.tensor_scalar(r_["dest"], r_["dest"], -float(SLOTS), None, ALU.add)

            choose().then_inc(parts_made, 1)
            dve.wait_ge(parts_made, 1)
            choose_2().then_inc(p_made, 1)
            weigh().then_inc(parts_made, 1)
            dve.wait_ge(parts_made, 2)
            weigh_2().then_inc(pw_made, 1)
            dve.wait_ge(pw_made, 1)
            move_on().then_inc(moved, 1)
            n_blocks = dve.value_load(meta_i[0:1, MAXB:MAXB + 1], min_val=1, max_val=MAXB)
            with dve.Fori(0, n_blocks) as b:
                dve.wait_ge(moved, b + 1)
                choose().then_inc(parts_made, 1)
                dve.wait_ge(parts_made, 2 * b + 3)
                dve.wait_ge(full[4], E_BASE[4] + b)
                choose_2().then_inc(p_made, 1)
                dve.wait_ge(silu_made, b + 1)
                v.tensor_tensor(m_h, ps[5][:, 256:512], m_sg, ALU.mult).then_inc(evac[5], 1)
                weigh().then_inc(parts_made, 1)
                dve.wait_ge(parts_made, 2 * b + 4)
                dve.wait_ge(pw_turned, b + 1)
                weigh_2().then_inc(pw_made, 1)
                dve.wait_ge(pw_made, b + 2)
                move_on().then_inc(moved, 1)
                dve.wait_ge(full[7], E_BASE[7] + b + 1)
                v.tensor_copy(m_y, ps[7][:, :]).then_inc(evac[7], 1)

            dve.wait_ge(y_done, 1)
            for p in range(2):
                for n in range(2):
                    o = m_o[:, p * D + n * 512:p * D + (n + 1) * 512]
                    did(v.scalar_tensor_tensor(o, m_x[:, p * D + n * 512:p * D + (n + 1) * 512], ALPHA,
                                               ps[2 * p + n][:, :], ALU.mult, ALU.add))
            own()
            then(v.tensor_reduce(small[:, 96:98], two(m_o), AX, ALU.add))
            then(v.tensor_scalar(small[:, 96:98], small[:, 96:98], -1.0 / D, None, ALU.mult))
            for p in range(2):
                o = m_o[:, p * D:(p + 1) * D]
                v.tensor_scalar(o, o, small[:, 96 + p:97 + p], None, ALU.add).then_inc(fin_centred, 1)
            dve.wait_ge(fin_squared, 2)
            v.tensor_scalar(small[:, 102:104], small[:, 100:102], 1.0 / D, LN_EPS, ALU.mult, ALU.add).then_inc(fin_var, 1)
            dve.wait_ge(fin_std, 1)
            then(v.reciprocal(small[:, 106:108], small[:, 104:106]))
            dve.wait_ge(ln2_in, 32)
            dve.wait_ge(fin_centred, 2)
            for p in range(2):
                o = m_o[:, p * D:(p + 1) * D]
                then(v.scalar_tensor_tensor(o, o, small[:, 106 + p:107 + p], m_g, ALU.mult, ALU.mult))
                v.tensor_tensor(o, o, m_b, ALU.add).then_inc(out_ready, 1)


def kernel(x, meta_tokens, norm_gains, w_ffn_in, w_ffn_out, gla_w_in, gla_w_gate, gla_b_gate, gla_norm, gla_w_out,
           kv_norm, w_kv, swa_w_q, swa_sinks, swa_w_out, w_in_2, b_in_2, lb_logits_2, hg_norm_g_2, rel_bias_2,
           w_proj_a_2, w_proj_b_2, w_out_2, ln1_g_2, ln1_b_2, w_group_2, b_group_2, w_expert_2, b_expert_2,
           w_gate_up_2, w_down_2, ln2_g_2, ln2_b_2):
    import concourse.bacc as bacc
    from concourse.bass_utils import run_bass_kernel_spmd

    f = np.float32
    a = {k: np.asarray(v) for k, v in locals().items() if k not in ("bacc", "run_bass_kernel_spmd", "f")}

    def by_feature(w):
        n = w.shape[1] // 256
        return w.reshape(KT, P, n, 2, P).transpose(2, 1, 3, 0, 4).reshape(n, P, UNIT)

    def by_token(w):
        n = w.shape[1] // 256
        return w.reshape(KT, P, n, 256).transpose(2, 1, 0, 3).reshape(n, P, UNIT)

    def short(w):
        return w.reshape(4, P, 2, 4, P).transpose(2, 1, 3, 0, 4).reshape(2, P, UNIT)

    def ffn_in(w):
        return by_feature(np.stack([w[:, :FF].reshape(D, FT, P), w[:, FF:].reshape(D, FT, P)], axis=2).reshape(D, 2 * FF))

    order = np.array([(t * 8 + half * 4 + i) * 64 + d for t in range(2) for i in range(4) for half in range(2)
                      for d in range(64)])
    g = a["gla_w_in"][0]
    w2 = a["w_in_2"][0]
    kv = a["w_kv"]
    fi = a["w_ffn_in"]
    cut = {"q": (0, 512), "z": (512, 1024), "i": (1024, 1536), "g": (1536, 2048), "mq": (2048, 2560),
           "mk": (2560, 3072), "mv": (3072, 3584), "ga": (3584, 4608), "gb": (4608, 5632)}
    sec = {k: w2[:, s:e] for k, (s, e) in cut.items()}
    w_units = np.concatenate([
        ffn_in(fi[0, 0]), by_feature(g[:, 2048:3072]), by_token(g[:, 1024:2048]), by_feature(g[:, 512:1024]),
        by_feature(g[:, 0:512]), by_feature(a["gla_w_out"][0]), ffn_in(fi[0, 1]), by_feature(kv[:, :256]),
        by_token(kv[:, 256:]), ffn_in(fi[1, 0]), by_feature(a["swa_w_q"][0][:, order]),
        by_feature(a["swa_w_out"][0][order]), ffn_in(fi[1, 1]),
        by_feature(sec["z"]), by_feature(sec["q"]), by_feature(sec["ga"]), by_feature(sec["gb"]), by_feature(sec["g"]),
        by_feature(sec["mq"]), by_feature(sec["mk"]), by_token(sec["i"]), by_token(sec["mv"]),
        short(a["w_proj_a_2"][0]), short(a["w_proj_b_2"][0]), by_feature(a["w_out_2"][0])])
    w_out_units = a["w_ffn_out"].reshape(4, FT, P, KT, P).transpose(0, 3, 2, 1, 4).reshape(4 * KT, P, OUT_UNIT)
    tokens = np.concatenate([a["x"][0], a["meta_tokens"]])
    xT = tokens.reshape(TA, KT, P).transpose(2, 1, 0).reshape(P, KT * TA)

    def cols(vec):
        return vec.reshape(-1, P).T

    table, levels = constants()
    par = {k: np.zeros((P, n), f) for k, (_, n) in P_COLS.items()}
    par["gains"][:] = cols(a["norm_gains"].reshape(-1))
    par["kv_norm"][:] = cols(a["kv_norm"])
    par["b_gate"][:] = cols(a["gla_b_gate"][0])
    par["gla_norm"][:] = cols(a["gla_norm"][0])
    par["w_lr"][:] = g[:, 3072:].reshape(KT, P, RANK).transpose(1, 0, 2).reshape(P, -1)
    par["w_gate"][:RANK] = a["gla_w_gate"][0]
    par["b_in"][:] = cols(a["b_in_2"][0])
    par["lb_logits"][:] = cols(a["lb_logits_2"].reshape(-1))
    par["hg_norm"][:] = cols(a["hg_norm_g_2"][0])
    par["ln1_g"][:] = cols(a["ln1_g_2"][0])
    par["ln1_b"][:] = cols(a["ln1_b_2"][0])
    wr = np.concatenate([a["w_group_2"][0], a["w_expert_2"][0]], axis=1)
    par["w_route"][:] = wr.reshape(KT, P, 36).transpose(1, 0, 2).reshape(P, -1)
    par["b_route"][:] = np.concatenate([a["b_group_2"][0], a["b_expert_2"][0]])[None]
    par["rel_bias"][:32] = a["rel_bias_2"]
    heads = [t * 8 + half * 4 + i for t in range(2) for i in range(4) for _ in range(2) for half in range(2)]
    par["sinks"][:] = a["swa_sinks"][0][heads][None]
    params = np.concatenate([par[k] for k in P_COLS], axis=1)
    b2 = a["b_in_2"][0]
    rows = np.ascontiguousarray(np.broadcast_to(
        np.concatenate([b2[1024:1536], b2[3072:3584], a["ln2_g_2"][0], a["ln2_b_2"][0]]), (P, 3072)))

    nc = bacc.Bacc("TRN2", target_bir_lowering=False, num_devices=1)
    arrays = {"xT": xT, "w_units": w_units, "w_out_units": w_out_units, "w_gate_up": a["w_gate_up_2"][0],
              "w_down": a["w_down_2"][0], "table": table, "levels": levels, "params": params, "rows": rows}
    arrays = {k: np.ascontiguousarray(v) for k, v in arrays.items()}
    aps = [nc.dram_tensor(k, v.shape, mybir.dt.from_np(v.dtype), kind="ExternalInput").ap() for k, v in arrays.items()]
    out = nc.dram_tensor("out", (1, SEQ, D), F32, kind="ExternalOutput").ap()
    two_blocks(nc, *aps, out)
    r = run_bass_kernel_spmd(nc, [arrays], core_ids=[0])
    return r.results[0]["out"]
```

```python
from contextlib import ExitStack

import numpy as np

import concourse.bass as bass
from concourse import mybir

F32 = mybir.dt.float32
F32R = mybir.dt.float32r
I32 = mybir.dt.int32
U32 = mybir.dt.uint32
ALU = mybir.AluOpType
ACT = mybir.ActivationFunctionType
AX = mybir.AxisListType.X

P = 128
D = 1024
KT = D // P
SEQ = 256
META = 16
TA = SEQ + META
FF = 2816
FT = FF // P
EPS = 1e-6
LN_EPS = 1e-5
GH, GDK, GDV, CH = 4, 128, 256, 64
RANK = 16
NEG = -1e30
ALPHA = float(2.0 ** 0.25)
NE, EH = 32, 512
ARENA = 19008
SLOTS = 64
MAXB = NE + 2 * SEQ // SLOTS
RAW = 2
PARTS = 4
UNIT = 2 * KT * P
OUT_UNIT = FT * P
HALF = OUT_UNIT // 2
EXP_UNITS = 6

C_COLS = {}
for _name, _n in (("ident", P), ("ones", P), ("rot", P), ("pairmask", P), ("upper", P), ("iota", SLOTS),
                  ("iota32", 32), ("iotab", MAXB), ("reset_g", TA), ("reset_h", SEQ), ("cos", TA), ("sin", TA),
                  ("swa0", P + META), ("swa1", SEQ + META), ("ninf", SEQ), ("onehot", 384)):
    C_COLS[_name] = (sum(n for _, n in C_COLS.values()), _n)
NC_COLS = sum(n for _, n in C_COLS.values())
LEVELS = [64, 32, 16, 8, 4, 2, 1, 0]

P_COLS = {}
for _name, _n in (("gains", 96), ("kv_norm", KT), ("b_gate", GH), ("gla_norm", 2), ("w_lr", KT * RANK),
                  ("w_gate", GH * GDK), ("b_in", 44), ("lb_logits", 8), ("hg_norm", 4), ("ln1_g", KT), ("ln1_b", KT),
                  ("w_route", KT * 36), ("b_route", 36), ("rel_bias", 8), ("sinks", 32)):
    P_COLS[_name] = (sum(n for _, n in P_COLS.values()), _n)
NP_COLS = sum(n for _, n in P_COLS.values())


def constants():
    c = {k: np.zeros((P, n), np.float32) for k, (_, n) in C_COLS.items()}
    i = np.arange(P)
    c["ident"][i, i] = 1
    c["ones"][:] = 1
    d = i % 64
    part = np.where(d < 8, i + 8, i - 8)
    m = i[d < 16]
    c["rot"][part[m], m] = 1
    s, t = i[:, None], i[None, :]
    c["pairmask"][:] = (s // CH == t // CH) & (s <= t)
    c["upper"][:] = s < t
    c["iota"][:] = np.arange(SLOTS)
    c["iota32"][:] = np.arange(32)
    c["iotab"][:] = np.arange(MAXB)
    col = np.arange(TA)
    c["reset_g"][:] = col % CH != 0
    c["reset_h"][:] = np.arange(SEQ) % P != 0
    inv = np.float32(500000.0) ** (-np.arange(0, 16, 2, dtype=np.float32) / np.float32(16))
    pos = np.where(col < SEQ, col + META, col - SEQ).astype(np.float32)
    ang = pos[None, :] * inv[d % 8][:, None]
    c["cos"][:] = np.where((d < 16)[:, None], np.cos(ang), 1)
    c["sin"][:] = np.where((d < 8)[:, None], -np.sin(ang), np.where((d < 16)[:, None], np.sin(ang), 0))
    own = np.where(t <= s, 0, NEG)
    c["swa0"][:, :P] = own
    c["swa1"][:, :P] = np.where(t > s, 0, NEG)
    c["swa1"][:, P:2 * P] = own
    c["ninf"][:, :] = np.where(np.arange(SEQ)[None, :] <= P + s, 0, NEG)
    dist = 255 - np.arange(384)
    dd = np.maximum(dist, 1).astype(np.float32)
    log_part = 16 + (np.log(dd / np.float32(16)) / np.float32(np.log(8.0)) * np.float32(16)).astype(np.int32)
    bucket = np.where(dist < 16, dist, np.minimum(log_part, 31))
    c["onehot"][:32] = (bucket[None, :] == np.arange(32)[:, None]) & (dist >= 0)[None, :]
    table = np.concatenate([c[k] for k in C_COLS], axis=1)
    levels = np.zeros((P, len(LEVELS), P), np.float32)
    for n, h in enumerate(LEVELS):
        if h:
            levels[:, n] = (s // (2 * h) == t // (2 * h)) & (s % (2 * h) < h) & (t % (2 * h) >= h)
        else:
            levels[:, n] = s == t
    return table, levels.reshape(P, -1)


class Stream:

    def __init__(self):
        self.n = 0

    def take(self, n):
        first, self.n = self.n, self.n + n
        return first


class Tiles:

    def __init__(self, uses, banks, n):
        self.banks, self.base = banks, {b: uses[b] for b in banks}
        for i in range(n):
            uses[banks[i % len(banks)]] += 1

    def at(self, i, it=0, body=0):
        b = self.banks[i % len(self.banks)]
        return b, self.base[b] + i // len(self.banks) + it * (body // len(self.banks))


def two_blocks(nc, xT, w_units, w_out_units, w_gate_up, w_down, table, levels, params, rows, out):
    ctx = ExitStack()
    with ctx:
        def sb(name, shape, dt=F32):
            return ctx.enter_context(nc.sbuf_tensor(name, shape, dt))

        def sem(name):
            return ctx.enter_context(nc.semaphore(name))

        h = sb("h", [P, KT * TA])
        x_hi = sb("x_hi", [P, KT * TA], F32R)
        x_lo = sb("x_lo", [P, KT * TA], F32R)
        zg = sb("zg", [P, KT * TA])
        sq = sb("sq", [P, 2, TA])
        acc = sb("acc", [P, TA])
        var = sb("var", [P, TA])
        std = sb("std", [P, TA])
        rs = sb("rs", [P, TA])
        kT = sb("kT", [P, 2, TA])
        vs = sb("vs", [P, 3, 256])
        small = sb("small", [P, 320])
        cst = sb("cst", [P, NC_COLS])
        par = sb("par", [P, NP_COLS])
        halfg = sb("halfg", [P, 96])
        sg = sb("sg", [P, 2 * TA])
        hw = sb("hw", [P, 2 * TA])
        with ExitStack() as early:
            def eb(name, shape, dt=F32):
                return early.enter_context(nc.sbuf_tensor(name, shape, dt))

            raw = eb("raw", [P, RAW * OUT_UNIT])
            w_hi = eb("w_hi", [P, PARTS * HALF], F32R)
            w_lo = eb("w_lo", [P, PARTS * HALF], F32R)
        ring = sb("ring", [P, EXP_UNITS * UNIT])
        sb("behind_ring", [P, RAW * OUT_UNIT + 2 * PARTS * HALF - EXP_UNITS * UNIT])
        with ExitStack() as early:
            hid_hi = eb("hid_hi", [P, FT * TA], F32R)
            hid_lo = eb("hid_lo", [P, FT * TA], F32R)
        arena = sb("arena", [P, ARENA])
        meta_i = sb("meta_i", [1, MAXB + 8], I32)
        ps = [ctx.enter_context(nc.psum_tensor(f"ps{b}", [P, 512], F32)) for b in range(8)]
        bias_rows = nc.dram_tensor("bias_rows", [8, P * 384], F32, kind="Internal").ap()

        def C(name, a=0, b=None, parts=slice(0, P)):
            at, n = C_COLS[name]
            return cst[parts, at + a:at + (n if b is None else b)]

        def W(name, a=0, b=None, parts=slice(0, P)):
            at, n = P_COLS[name]
            return par[parts, at + a:at + (n if b is None else b)]

        def gain(g, m, table=par):
            at = P_COLS["gains"][0] if table is par else 0
            return table[:, at + g * KT + m:at + g * KT + m + 1]

        place = [0]

        def room(n):
            at = place[0]
            place[0] += n
            assert place[0] <= ARENA, place[0]
            return arena[:, at:at + n]

        def tile(buf, m, t, w=TA):
            return buf[:, m * w:m * w + t]

        s_kraw = arena[:, 2 * FT * TA:2 * FT * TA + 2 * TA]
        s_krot = arena[:, 2 * FT * TA + 2 * TA:2 * FT * TA + 4 * TA]
        g_v = room(2 * D)
        g_vm = room(D)
        g_r = zg
        g_b = room(GH * TA)
        g_att = g_b
        g_sq = room(2 * GH * TA)
        g_e1, g_e2 = g_sq[:, 0:GH * TA], g_sq[:, GH * TA:2 * GH * TA]
        g_o = room(KT * TA)
        g_e0, g_k = g_o[:, 0:GH * TA], g_o[:, GH * TA:2 * GH * TA]
        g_kw, g_q = room(GH * TA), room(GH * TA)
        g_kwT = room(GH * 384)
        g_s = room(GH * 4 * GDV)
        g_dec = room(GH * 4)
        g_lr = room(TA)
        place[0] = 0
        s_q = room(KT * SEQ)
        s_t = room(2 * SEQ)
        s_o = room(KT * SEQ)
        a_p = room(2 * 4 * TA)
        a_pT = room(4 * 384)
        place[0] = 0
        b_sga, b_sgb = zg, room(KT * SEQ)
        b_sg = room(4 * SEQ)
        b_p = room(8 * SEQ)
        b_kf, b_q = b_p[:, 0:4 * SEQ], b_p[:, 4 * SEQ:8 * SEQ]
        b_b, b_e, b_qk = (room(4 * SEQ) for _ in range(3))
        b_bo, b_sq = b_b, b_qk
        b_v, b_mv = room(2 * 512), room(2 * 512)
        b_mq, b_mk = room(4 * SEQ), room(4 * SEQ)
        b_bias = room(8 * SEQ)
        b_att = room(3 * 512)
        b_a = room(4 * SEQ)
        b_lv = room(len(LEVELS) * P)
        b_rows = room(2 * 512)
        b_pT = arena[:, place[0] - 2 * 1024:place[0] - 2 * 1024 + 4 * 384]
        place[0] = 0
        m_x = room(2 * D)
        m_g, m_b = room(D), room(D)
        m_r = room(2200)
        r_, at_ = {}, 64
        for name, n in (("lg", 72), ("gl", 8), ("gt", 8), ("g1", 8), ("ge", 8), ("em", 64), ("tmp", 64), ("o1", 64),
                        ("o2", 64), ("gtop", 2), ("top1", 2), ("top2", 2), ("place", 2), ("ev", 2), ("pg", 2),
                        ("w1", 2), ("w2", 2), ("dest", 4), ("cnt", 32), ("nb", 32), ("end", 32), ("beg", 32),
                        ("eb", MAXB), ("cmp", MAXB * 32)):
            r_[name] = m_r[:, at_:at_ + n]
            at_ += n
        assert at_ <= 2200, at_
        m_P = room(2 * 64)
        m_PW = room(2 * P)
        m_t = room(6 * 64)
        m_zero = room(P)
        m_xT = room(512)
        m_h = room(256)
        m_sg = room(256)
        m_turn = room(512)
        m_hT, m_pwT = m_turn[:, 0:2 * P], m_turn[:, 2 * P:4 * P]
        m_y = room(512)
        m_o = room(2 * D)
        b_br = arena[:, 0:8 * 384]

        consts_in, params_in, x_in, levels_in, rows_in, ln2_in = (
            sem(n) for n in ("consts_in", "params_in", "x_in", "levels_in", "rows_in", "ln2_in"))
        bias_out, bias_in, out_stored = sem("bias_out"), sem("bias_in"), sem("out_stored")
        full = [sem(f"full{b}") for b in range(8)]
        evac = [sem(f"evac{b}") for b in range(8)]
        landed = [sem(f"landed{s}") for s in range(RAW)]
        hi_made, lo_made, hw_made = sem("hi_made"), sem("lo_made"), sem("hw_made")
        e_landed = [sem(f"e_landed{s}") for s in range(EXP_UNITS)]
        half_begun = sem("half_begun")
        exp_begun = sem("exp_begun")
        sq_made, sq_used, std_made = sem("sq_made"), sem("sq_used"), sem("std_made")
        x_ready, h_ready = sem("x_ready"), sem("h_ready")
        act_chain, dve_chain = sem("act_chain"), sem("dve_chain")
        soft_made, decay_in, decay_made = (sem(n) for n in ("soft_made", "decay_in", "decay_made"))
        q_roped, neg_max, exp_made, p_ready = (sem(n) for n in ("q_roped", "neg_max", "exp_made", "p_ready"))
        lb_in, lb_exp = sem("lb_in"), sem("lb_exp")
        hg_arg, hg_ln, lvl_in, lvl_exp, lvl_ready = (
            sem(n) for n in ("hg_arg", "hg_ln", "lvl_in", "lvl_exp", "lvl_ready"))
        ln_in, centred, ln_squared, x2_ready = (sem(n) for n in ("ln_in", "centred", "ln_squared", "x2_ready"))
        route_in, route_exp, m_ready, table_ready = (
            sem(n) for n in ("route_in", "route_exp", "m_ready", "table_ready"))
        p_made, pw_made, pw_turned, parts_made, moved = (
            sem(n) for n in ("p_made", "pw_made", "pw_turned", "parts_made", "moved"))
        y_zeroed, silu_made, y_done = (sem(n) for n in ("y_zeroed", "silu_made", "y_done"))
        fin_centred, fin_squared, fin_var, fin_std, out_ready = (
            sem(n) for n in ("fin_centred", "fin_squared", "fin_var", "fin_std", "out_ready"))

        units, uses = Stream(), [0] * 8
        MAIN = [0, 1, 2, 3]
        plan = {}

        def ffn_plan(n):
            plan[f"in{n}"] = (units.take(FT), Tiles(uses, MAIN, 2 * FT))
            plan[f"out{n}"] = (units.take(KT), Tiles(uses, MAIN, KT))

        def tiles(name, banks, n):
            plan[name] = Tiles(uses, banks, n)

        tiles("bias", [4, 5, 6, 7], 8)
        tiles("stat0", [7], 1)
        ffn_plan(0)
        tiles("stat1", [7], 1)
        tiles("stat2", [7], 1)
        tiles("lr", [4], 1)
        plan["r"] = (units.take(4), Tiles(uses, MAIN, 8))
        tiles("gate", [4, 5, 6, 7], 4)
        plan["v"] = (units.take(4), Tiles(uses, MAIN, 12))
        plan["k"] = (units.take(2), Tiles(uses, MAIN, 4))
        plan["q"] = (units.take(2), Tiles(uses, MAIN, 4))
        tiles("att", [0, 1, 2, 3], 4)
        tiles("kwT", [4, 5, 6, 7], 4)
        tiles("kv", list(range(8)), 12)
        tiles("o", list(range(8)), 8)
        tiles("gst", MAIN, 4)
        plan["gout"] = (units.take(4), Tiles(uses, MAIN, 8))
        tiles("stat3", [7], 1)
        tiles("stat4", [7], 1)
        ffn_plan(1)
        tiles("stat5", [7], 1)
        tiles("stat6", [7], 1)
        plan["ks"] = (units.take(1), Tiles(uses, MAIN, 2))
        tiles("krot", [4, 5], 2)
        plan["vs"] = (units.take(1), Tiles(uses, MAIN, 3))
        ffn_plan(2)
        tiles("stat7", [7], 1)
        tiles("stat8", [7], 1)
        plan["sq"] = (units.take(4), Tiles(uses, MAIN, 8))
        tiles("qrot", [4, 5], 8)
        tiles("ss", MAIN, 32)
        tiles("sT", [4, 5, 6], 32)
        tiles("sv", [7], 8)
        plan["sout"] = (units.take(4), Tiles(uses, MAIN, 8))
        tiles("stat9", [7], 1)
        tiles("stat10", [7], 1)
        ffn_plan(3)
        tiles("stat11", [7], 1)
        SECTIONS = ["z", "hq", "ga", "gb", "hgate", "mq", "mk", "hi", "mv"]
        for name in SECTIONS:
            n_units = 4 if name in ("ga", "gb") else 2
            plan[name] = (units.take(n_units), Tiles(uses, MAIN, 2 * n_units))
        tiles("lvl", [4, 5, 6, 7], 16)
        tiles("cross", [4], 1)
        tiles("ho", [0, 1, 2, 3], 4)
        tiles("hst", [4, 5, 6, 7], 4)
        tiles("bs", MAIN, 16)
        tiles("bT", [4, 5, 6], 16)
        tiles("bv", [7], 4)
        plan["pa"] = (units.take(2), Tiles(uses, MAIN, 8))
        plan["pb"] = (units.take(2), Tiles(uses, MAIN, 8))
        plan["wo"] = (units.take(4), Tiles(uses, MAIN, 8))
        tiles("mean", [7], 1)
        tiles("lnvar", [7], 1)
        tiles("xtok", [0, 1, 2, 3], 4)
        tiles("route", [4], 1)
        tiles("pos", [5], 1)
        tiles("cnt", [6], 1)
        N_UNITS = units.n
        tiles("e_gather", [4], 1)
        E_BASE = {b: uses[b] for b in range(4, 8)}


        block = ctx.enter_context(nc.Block())

        runs = []
        u, row, orow = 0, 0, 0
        for key, val in plan.items():
            if not isinstance(val, tuple):
                continue
            n = {"out": KT, "in": FT}.get(key.rstrip("0123"), None)
            first = val[0]
            nxt = min([v[0] for v in plan.values() if isinstance(v, tuple) and v[0] > first] + [N_UNITS])
            n = nxt - first
            if key.startswith("out"):
                runs.append((1, orow, first, n))
                orow += n
            elif runs and runs[-1][0] == 0 and runs[-1][2] + runs[-1][3] == first:
                runs[-1] = (0, runs[-1][1], runs[-1][2], runs[-1][3] + n)
                row += n
            else:
                runs.append((0, row, first, n))
                row += n

        is_out = [False] * N_UNITS
        for kind, _, first, n in runs:
            for u in range(first, first + n):
                is_out[u] = bool(kind)

        def half_size(u):
            return HALF if is_out[u] else UNIT // 2

        def raw_slot(u, a, n):
            return raw[:, (u % RAW) * OUT_UNIT + a:(u % RAW) * OUT_UNIT + a + n]

        def part(w, c, a, n):
            return w[:, (c % PARTS) * HALF + a:(c % PARTS) * HALF + a + n]

        @block.sync
        def _(sp):
            sp.dma_start(cst[:, :], table).then_inc(consts_in, 16)
            sp.dma_start(h[:, :], xT).then_inc(x_in, 16)
            sp.dma_start(par[:, :], params).then_inc(params_in, 16)

            def load(kind, row, u, it=0):
                n = OUT_UNIT if kind else UNIT
                src = (w_out_units if kind else w_units)[bass.ds(row + RAW * it, 1), :, :]
                if not isinstance(it, int) or u >= RAW:
                    sp.wait_ge(lo_made, 2 * (u - RAW) + 2 + 2 * RAW * it)
                sp.dma_start(raw_slot(u, 0, n), src.rearrange("a p n -> (a p) n")).then_inc(landed[u % RAW], 16)

            for kind, row, first, n in runs:
                head = RAW if first == 0 else 0
                for j in range(head):
                    load(kind, row + j, first + j)
                row, first, n = row + head, first + head, n - head
                with sp.Fori(0, n // RAW) as it:
                    for j in range(RAW):
                        load(kind, row + j, first + j, it)
                for j in range(n // RAW * RAW, n):
                    load(kind, row + j, first + j)

            sp.wait_ge(table_ready, 1)
            n_blocks = sp.value_load(meta_i[0:1, MAXB:MAXB + 1], min_val=1, max_val=MAXB)
            with sp.Fori(0, n_blocks) as b:
                e = sp.value_load(meta_i[0:1, bass.ds(b, 1)], min_val=0, max_val=NE - 1)
                for i in range(EXP_UNITS):
                    sp.wait_ge(exp_begun, b * EXP_UNITS + i + 2)
                    if i < 4:
                        src = w_gate_up[bass.ds(e, 1), 2 * P * i:2 * P * (i + 1), :]
                    else:
                        src = w_down[bass.ds(e, 1), 2 * P * (i - 4):2 * P * (i - 3), :]
                    sp.dma_start(ring[:, i * UNIT:(i + 1) * UNIT].rearrange("p (k n) -> p k n", k=2),
                                 src.rearrange("a (k p) n -> p (a k) n", p=P)).then_inc(e_landed[i], 16)

        @block.gpsimd
        def _(pool):
            pool.wait_ge(evac[plan["bias"].at(7)[0]], plan["bias"].at(7)[1] + 1)
            for i in range(8):
                pool.dma_start(bias_rows[i, :].rearrange("(p n) -> p n", p=P),
                               b_br[:, i * 384:(i + 1) * 384]).then_inc(bias_out, 16)
            pool.wait_ge(bias_out, 8 * 16)
            t = plan["stat11"].at(0)
            pool.wait_ge(full[t[0]], t[1] + 1)
            for i in range(8):
                src = bias_rows[i, 127:127 + P * 383].rearrange("(p n) -> p n", p=P)[:, 0:SEQ]
                pool.dma_start(b_bias[:, i * SEQ:(i + 1) * SEQ], src).then_inc(bias_in, 16)
            pool.dma_start(b_lv, levels).then_inc(levels_in, 16)
            pool.dma_start(b_rows, rows[:, 0:1024]).then_inc(rows_in, 16)
            t = plan["lnvar"].at(0)
            pool.wait_ge(full[t[0]], t[1] + 1)
            pool.dma_start(m_g, rows[:, 1024:2048]).then_inc(ln2_in, 16)
            pool.dma_start(m_b, rows[:, 2048:3072]).then_inc(ln2_in, 16)

        @block.tensor
        def _(pe):
            def mm(out_ap, lhsT, rhs, start, stop):
                return nc.tensor.matmul(out_ap, lhsT, rhs, start=start, stop=stop, skip_group_check=True)

            def turn(out_ap, in_ap):
                k = in_ap.shape[0]
                return nc.tensor.transpose(out_ap, in_ap, C("ident", 0, k, slice(0, k)))

            def free(t):
                if not isinstance(t[1], int) or t[1] > 0:
                    pe.wait_ge(evac[t[0]], t[1])
                return ps[t[0]]

            def taken(t):
                pe.wait_ge(evac[t[0]], t[1] + 1)

            def arrive(u, j, it=0):
                c = 2 * u + j
                pe.wait_ge(lo_made, c + 1 + 2 * RAW * it)
                return c

            def three(out_ap, hi, lo, moving_hi, moving_lo, start, stop):
                first = mm(out_ap, hi, moving_hi, start, False)
                mm(out_ap, hi, moving_lo, False, False)
                return first, mm(out_ap, lo, moving_hi, False, stop)

            def project(u, T, i, src, w, it=0, body=0, kt=KT, n_tiles=2, at=0):
                for j in range(n_tiles):
                    t = T.at(i + j, it, body)
                    if j % (n_tiles // 2) == 0:
                        c = arrive(u, j // (n_tiles // 2), it)
                    bank = free(t)
                    for k in range(kt):
                        a = (j % (n_tiles // 2) * kt + k) * P
                        x = slice((at + k) * TA, (at + k) * TA + w)
                        first, m = three(bank[:, 0:w], part(w_hi, c, a, P), part(w_lo, c, a, P),
                                         src[0][:, x], src[1][:, x], k == 0, k == kt - 1)
                        if j % (n_tiles // 2) == 0 and k == 0:
                            first.then_inc(half_begun, 1)
                    m.then_inc(full[t[0]], 1)

            def project_tokens(u, T, i, src, spans):
                for j, (a, n) in enumerate(spans):
                    t = T.at(i + j)
                    bank = free(t)
                    for k in range(KT):
                        if k % 4 == 0:
                            c = arrive(u, k // 4)
                        x = slice(k * TA + a, k * TA + a + n)
                        first, m = three(bank[0:n, 0:256], src[0][:, x], src[1][:, x],
                                         part(w_hi, c, k % 4 * 256, 256), part(w_lo, c, k % 4 * 256, 256),
                                         k == 0, k == KT - 1)
                        if (j, k) in ((0, 0), (len(spans) - 1, 4)):
                            first.then_inc(half_begun, 1)
                    m.then_inc(full[t[0]], 1)

            def stat(n, w):
                t = plan[f"stat{n}"].at(0)
                pe.wait_ge(sq_used, 8 * (n + 1))
                bank = free(t)
                mm(bank[:, 0:w], C("ones"), acc[:, 0:w], True, True).then_inc(full[t[0]], 1)

            X, HID = (x_hi, x_lo), (hid_hi, hid_lo)

            def ffn(n, x_count, w):
                pe.wait_ge(x_ready, x_count)
                u0, T = plan[f"in{n}"]
                with pe.Fori(0, FT // RAW) as it:
                    for j in range(RAW):
                        project(u0 + j, T, 2 * j, X, w, it, 2 * RAW)
                before, last = T.at(2 * FT - 3), T.at(2 * FT - 1)
                u1, T = plan[f"out{n}"]
                with pe.Fori(0, KT // 4) as it2:
                    for j in range(4):
                        t = T.at(j, it2, 4)
                        bank = free(t)
                        if j == 0:
                            taken(before)
                        for k in range(FT):
                            if j == 0 and k == FT - 1:
                                taken(last)
                            if k % (FT // 2) == 0:
                                c = arrive(u1 + j, k // (FT // 2), 2 * it2)
                            a = k % (FT // 2) * P
                            x = slice(k * TA, k * TA + w)
                            first, m = three(bank[:, 0:w], part(w_hi, c, a, P), part(w_lo, c, a, P),
                                             hid_hi[:, x], hid_lo[:, x], k == 0, k == FT - 1)
                            if k % (FT // 2) == 0:
                                first.then_inc(half_begun, 1)
                        m.then_inc(full[t[0]], 1)

            pe.wait_ge(consts_in, 16)
            pe.wait_ge(params_in, 16)
            for i in range(8):
                t = plan["bias"].at(i)
                bank = free(t)
                mm(bank[:, 0:384], W("rel_bias", i, i + 1, slice(0, 32)).to_broadcast([32, P]),
                   C("onehot", 0, 384, slice(0, 32)), True, True).then_inc(full[t[0]], 1)
            stat(0, TA)
            ffn(0, 8, TA)
            stat(1, TA)
            stat(2, TA)

            pe.wait_ge(x_ready, 16)
            t = plan["lr"].at(0)
            bank = free(t)
            for k in range(KT):
                m = mm(bank[0:RANK, 0:TA], W("w_lr", k * RANK, (k + 1) * RANK), zg[:, k * TA:(k + 1) * TA],
                       k == 0, k == KT - 1)
            m.then_inc(full[t[0]], 1)
            u0, T = plan["r"]
            project(u0, T, 0, X, TA)
            taken(plan["lr"].at(0))
            for i in range(GH):
                t = plan["gate"].at(i)
                bank = free(t)
                mm(bank[:, 0:TA], W("w_gate", i * GDK, (i + 1) * GDK, slice(0, RANK)), g_lr[0:RANK, :],
                   True, True).then_inc(full[t[0]], 1)
            for j in range(1, 4):
                project(u0 + j, T, 2 * j, X, TA)
            u0, T = plan["v"]
            for j in range(4):
                project_tokens(u0 + j, T, 3 * j, X, ((0, P), (P, P), (SEQ, META)))
            for name in ("k", "q"):
                u0, T = plan[name]
                for j in range(2):
                    project(u0 + j, T, 2 * j, X, TA)
            for i in range(GH):
                t = plan["att"].at(i)
                bank = free(t)
                taken(plan["q"][1].at(i))
                for a, n in ((0, P), (P, P), (SEQ, META)):
                    m = mm(bank[0:n, a:a + n], g_k[:, i * TA + a:i * TA + a + n], g_q[:, i * TA + a:i * TA + a + n],
                           True, True)
                m.then_inc(full[t[0]], 1)
            for i in range(GH):
                t = plan["kwT"].at(i)
                bank = free(t)
                turn(bank[:, 0:P], g_kw[:, i * TA:i * TA + P])
                turn(bank[:, P:2 * P], g_kw[:, i * TA + P:i * TA + 2 * P])
                turn(bank[0:META, 256:384], g_kw[:, i * TA + SEQ:(i + 1) * TA]).then_inc(full[t[0]], 1)
            for i in range(GH):
                taken(plan["kwT"].at(i))
                T = plan["kv"]
                kw = g_kwT[:, i * 384:(i + 1) * 384]
                v0, v1 = (g_v[:, t * D + i * GDV:t * D + (i + 1) * GDV] for t in (0, 1))
                bank = free(T.at(3 * i))
                mm(bank[:, 0:256], kw[0:META, 256:384], g_vm[0:META, i * GDV:(i + 1) * GDV], True, True)
                mm(bank[:, 256:512], kw[0:64, 0:128], v0[0:64, :], True, True).then_inc(full[T.at(3 * i)[0]], 1)
                bank = free(T.at(3 * i + 1))
                mm(bank[:, 0:256], kw[64:128, 0:128], v0[64:128, :], True, True).then_inc(full[T.at(3 * i + 1)[0]], 1)
                bank = free(T.at(3 * i + 2))
                mm(bank[:, 0:256], kw[0:64, 128:256], v1[0:64, :], True, True).then_inc(full[T.at(3 * i + 2)[0]], 1)
            for i in range(GH):
                taken(plan["att"].at(i))
                taken(plan["kv"].at(3 * i + 2))
                for half in range(2):
                    t = plan["o"].at(2 * i + half)
                    bank = free(t)
                    c0 = i * GDV + half * P
                    mm(bank[:, 0:P], g_v[:, c0:c0 + P], g_att[:, i * TA:i * TA + P], True, False)
                    mm(bank[:, P:2 * P], g_v[:, D + c0:D + c0 + P], g_att[:, i * TA + P:i * TA + 2 * P], False, False)
                    mm(bank[:, SEQ:TA], g_vm[0:META, c0:c0 + P], g_att[0:META, i * TA + SEQ:(i + 1) * TA], False, False)
                    for c in range(4):
                        st = g_s[:, (i * 4 + c) * GDV + half * P:(i * 4 + c) * GDV + (half + 1) * P]
                        m = mm(bank[:, c * CH:(c + 1) * CH], st, g_q[:, i * TA + c * CH:i * TA + (c + 1) * CH],
                               False, c == 3)
                    m.then_inc(full[t[0]], 1)
            for i in range(GH):
                taken(plan["o"].at(2 * i + 1))
                t = plan["gst"].at(i)
                bank = free(t)
                mm(bank[:, 0:TA], C("ones"), tile(g_sq, 2 * i, TA), True, False)
                mm(bank[:, 0:TA], C("ones"), tile(g_sq, 2 * i + 1, TA), False, True).then_inc(full[t[0]], 1)
            pe.wait_ge(x_ready, 24)
            u0, T = plan["gout"]
            for j in range(4):
                project(u0 + j, T, 2 * j, X, TA)
            stat(3, TA)
            stat(4, TA)
            ffn(1, 32, TA)
            stat(5, TA)
            stat(6, TA)

            pe.wait_ge(x_ready, 40)
            u0, T = plan["ks"]
            project(u0, T, 0, HID, TA)
            for i in range(2):
                taken(plan["ks"][1].at(i))
                t = plan["krot"].at(i)
                bank = free(t)
                mm(bank[:, 0:TA], C("rot"), tile(s_kraw, i, TA), True, True).then_inc(full[t[0]], 1)
            u0, T = plan["vs"]
            project_tokens(u0, T, 0, HID, ((0, P), (P, P), (SEQ, META)))
            ffn(2, 48, SEQ)
            stat(7, SEQ)
            stat(8, SEQ)

            pe.wait_ge(x_ready, 56)
            u0, T = plan["sq"]
            for j in range(4):
                project(u0 + j, T, 2 * j, X, SEQ)
                for i in (2 * j, 2 * j + 1):
                    taken(T.at(i))
                    t = plan["qrot"].at(i)
                    bank = free(t)
                    mm(bank[:, 0:SEQ], C("rot"), s_q[:, i * SEQ:(i + 1) * SEQ], True, True).then_inc(full[t[0]], 1)

            def attend(names, groups, first, pb, pitch, pT, q_of, k_of, v_of, segs, done):
                S, TT, V = (plan[x] for x in names)

                def scores(g):
                    done(g)
                    for u in range(4):
                        n, b = divmod(u, 2)
                        t = S.at(4 * g + u)
                        bank = free(t)
                        hs = slice(64 * b, 64 * b + 64)
                        for at, size, key in segs(n):
                            m = mm(bank[:, at:at + size], q_of(g, hs, n), k_of(g, hs, key, size), True, True)
                        m.then_inc(full[t[0]], 1)

                scores(0)
                for g in range(groups):
                    if g + 1 < groups:
                        scores(g + 1)
                    for u in range(4):
                        n, b = divmod(u, 2)
                        t = TT.at(4 * g + u)
                        bank = free(t)
                        pe.wait_ge(p_ready, first + 4 * g + u + 1)
                        for s, (at, size, key) in enumerate(segs(n)):
                            a = ((g % 2) * 4 + u) * pitch + at
                            p = pb[:, a:a + size]
                            m = turn(bank[0:size, s * P:(s + 1) * P], p)
                        m.then_inc(full[t[0]], 1)
                    t = V.at(g)
                    bank = free(t)
                    for u in range(4):
                        n, b = divmod(u, 2)
                        taken(TT.at(4 * g + u))
                        ss = segs(n)
                        for s, (at, size, key) in enumerate(ss):
                            m = mm(bank[64 * b:64 * b + 64, n * P:(n + 1) * P], v_of(g, b, key, size),
                                   pT[0:size, u * 384 + s * P:u * 384 + (s + 1) * P], s == 0, s == len(ss) - 1)
                    m.then_inc(full[t[0]], 1)
            swa_segs = (((0, P, 0), (P, META, SEQ)), ((0, P, 0), (P, P, P), (SEQ, META, SEQ)))
            attend(("ss", "sT", "sv"), 8, 0, a_p, TA, a_pT,
                   lambda g, hs, n: s_q[hs, g * SEQ + n * P:g * SEQ + (n + 1) * P],
                   lambda g, hs, key, size: kT[hs, g // 4, key:key + size],
                   lambda g, b, key, size: vs[0:size, key // P, (2 * (g // 4) + b) * 64:(2 * (g // 4) + b) * 64 + 64],
                   lambda n: swa_segs[n],
                   lambda g: pe.wait_ge(q_roped, g + 1))
            pe.wait_ge(x_ready, 64)
            u0, T = plan["sout"]
            for j in range(4):
                project(u0 + j, T, 2 * j, X, SEQ)
            stat(9, SEQ)
            stat(10, SEQ)
            ffn(3, 72, SEQ)
            stat(11, SEQ)

            pe.wait_ge(x_ready, 80)

            def level(n):
                if n == 0:
                    taken(plan["hq"][1].at(3))
                if LEVELS[n]:
                    pe.wait_ge(lvl_ready, n + 1)
                for p in range(2):
                    t = plan["lvl"].at(2 * n + p)
                    bank = free(t)
                    for i in range(4):
                        a = i * SEQ + p * P
                        left, right = (b_qk, b_qk) if LEVELS[n] else (b_kf, b_q)
                        m = mm(bank[:, i * P:(i + 1) * P], left[:, a:a + P], right[:, a:a + P], True, True)
                    m.then_inc(full[t[0]], 1)

            def section(name, js=None):
                u0, T = plan[name]
                for j in js if js is not None else range(4 if name in ("ga", "gb") else 2):
                    project(u0 + j, T, 2 * j, X, SEQ)

            section("z")
            section("hq")
            for j in range(4):
                section("ga", [j])
                if j >= 2:
                    level(j - 2)
            for j in range(4):
                section("gb", [j])
                level(j + 2)
            for j in range(2):
                section("hgate", [j])
                level(j + 6)
            section("mq")
            section("mk")
            pe.wait_ge(lvl_ready, len(LEVELS))
            t = plan["cross"].at(0)
            bank = free(t)
            for i in range(4):
                m = mm(bank[:, i * P:(i + 1) * P], b_qk[:, i * SEQ:i * SEQ + P], b_qk[:, i * SEQ + P:(i + 1) * SEQ], True, True)
            m.then_inc(full[t[0]], 1)
            for name in ("hi", "mv"):
                u0, T = plan[name]
                for j in range(2):
                    project_tokens(u0 + j, T, 2 * j, X, ((0, P), (P, P)))
            taken(plan["cross"].at(0))
            taken(plan["hi"][1].at(3))
            for i in range(4):
                t = plan["ho"].at(i)
                bank = free(t)
                v0, v1 = b_v[:, i * P:(i + 1) * P], b_v[:, 512 + i * P:512 + (i + 1) * P]
                mm(bank[:, 0:P], v0, b_att[:, i * P:(i + 1) * P], True, False)
                mm(bank[:, P:SEQ], v1, b_att[:, 512 + i * P:512 + (i + 1) * P], False, False)
                mm(bank[:, P:SEQ], v0, b_att[:, 1024 + i * P:1024 + (i + 1) * P], False, True).then_inc(full[t[0]], 1)
            for i in range(4):
                taken(plan["ho"].at(i))
                t = plan["hst"].at(i)
                bank = free(t)
                mm(bank[:, 0:SEQ], C("ones"), b_sq[:, i * SEQ:(i + 1) * SEQ], True, True).then_inc(full[t[0]], 1)
            moba_segs = (((0, P, 0),), ((0, P, 0), (P, P, P)))

            def moba_ready(g):
                if g == 0:
                    taken(plan["mk"][1].at(3))
                    taken(plan["mv"][1].at(3))

            attend(("bs", "bT", "bv"), 4, 32, b_p, SEQ, b_pT,
                   lambda g, hs, n: b_mq[hs, g * SEQ + n * P:g * SEQ + (n + 1) * P],
                   lambda g, hs, key, size: b_mk[hs, g * SEQ + key:g * SEQ + key + size],
                   lambda g, b, key, size: b_mv[0:size, key // P * 512 + (2 * g + b) * 64:key // P * 512 + (2 * g + b) * 64 + 64],
                   lambda n: moba_segs[n], moba_ready)
            for name, at in (("pa", 0), ("pb", 4)):
                pe.wait_ge(x_ready, 84 + at)
                u0, T = plan[name]
                for j in range(2):
                    project(u0 + j, T, 4 * j, X, SEQ, kt=4, n_tiles=4, at=at)
            pe.wait_ge(x_ready, 96)
            u0, T = plan["wo"]
            for j in range(4):
                project(u0 + j, T, 2 * j, X, SEQ)
            for name, k in (("mean", 1), ("lnvar", 2)):
                t = plan[name].at(0)
                pe.wait_ge(ln_in, k)
                bank = free(t)
                m = mm(bank[:, 0:SEQ], C("ones"), acc[:, 0:SEQ], True, True)
                m.then_inc(full[t[0]], 1)

            pe.wait_ge(x2_ready, 8)
            t = plan["route"].at(0)
            bank = free(t)
            for p in range(2):
                for k in range(KT):
                    m = mm(bank[:, p * 64:p * 64 + 36], h[:, k * TA + p * P:k * TA + (p + 1) * P],
                           W("w_route", k * 36, (k + 1) * 36), k == 0, k == KT - 1)
            m.then_inc(full[t[0]], 1)
            for i in range(4):
                t = plan["xtok"].at(i)
                bank = free(t)
                for k in range(4):
                    a = ((i % 2) * 4 + k) * TA + i // 2 * P
                    m = turn(bank[:, k * P:(k + 1) * P], h[:, a:a + P])
                    if i < 3 and k < 2:
                        m.then_inc(exp_begun, 1)
                m.then_inc(full[t[0]], 1)
            pe.wait_ge(m_ready, 1)
            t = plan["pos"].at(0)
            bank = free(t)
            M0, M1 = m_r[:, 0:32], m_r[:, 32:64]
            mm(bank[:, 0:32], C("upper"), M0, True, True)
            mm(bank[:, 32:64], C("upper"), M1, True, False)
            mm(bank[:, 32:64], C("ones"), M0, False, True).then_inc(full[t[0]], 1)
            t = plan["cnt"].at(0)
            bank = free(t)
            mm(bank[:, 0:32], C("ones"), M0, True, False)
            mm(bank[:, 0:32], C("ones"), M1, False, True).then_inc(full[t[0]], 1)

            pe.wait_ge(table_ready, 1)
            for i in range(4):
                taken(plan["xtok"].at(i))
                m = mm(ps[i][:, :], m_zero, m_x[:, 0:512], True, False)
            m.then_inc(y_zeroed, 1)
            n_blocks = pe.value_load(meta_i[0:1, MAXB:MAXB + 1], min_val=1, max_val=MAXB)
            taken(plan["cnt"].at(0))

            def gather():
                bank = ps[4]
                for kt in range(KT):
                    for p in range(2):
                        m = mm(bank[:, kt * 64:(kt + 1) * 64], m_x[:, p * D + kt * P:p * D + (kt + 1) * P],
                               m_P[:, p * 64:(p + 1) * 64], p == 0, p == 1)
                m.then_inc(full[4], 1)

            def combine():
                for p in range(2):
                    for n in range(2):
                        hs = slice(64 * n, 64 * n + 64)
                        m = mm(ps[2 * p + n][:, :], m_pwT[hs, p * P:(p + 1) * P], m_y[hs, :], False, False)
                return m

            pe.wait_ge(p_made, 1)
            t = plan["e_gather"].at(0)
            free(t)
            gather()
            with pe.Fori(0, n_blocks) as b:
                pe.wait_ge(evac[4], E_BASE[4] + b)
                pe.wait_ge(evac[5], E_BASE[5] + b)
                for i in range(4):
                    pe.wait_ge(e_landed[i], 16 * b + 16)
                    for kk in range(2):
                        k = 2 * i + kk
                        for j in range(2):
                            wt = ring[:, i * UNIT + kk * D:i * UNIT + (kk + 1) * D].rearrange(
                                "p (g n) -> p g n", g=2)[:, :, 256 * j:256 * j + 256]
                            m = mm(ps[5][64 * j:64 * j + 64, :].rearrange("p (g n) -> p g n", g=2),
                                   m_xT[:, k * 64:(k + 1) * 64], wt, k == 0, k == KT - 1)
                            if kk == 0 and j == 0:
                                m.then_inc(exp_begun, 1)
                m.then_inc(full[5], 1)
                pe.wait_ge(evac[7], E_BASE[7] + b)
                combine()
                pe.wait_ge(evac[6], E_BASE[6] + b)
                pe.wait_ge(pw_made, b + 1)
                for p in range(2):
                    m = turn(ps[6][:, 256 + p * P:256 + (p + 1) * P], m_PW[:, p * P:(p + 1) * P])
                m.then_inc(pw_turned, 1)
                pe.wait_ge(p_made, b + 2)
                gather()
                pe.wait_ge(evac[5], E_BASE[5] + b + 1)
                for c in range(2):
                    m = turn(ps[6][:, c * P:(c + 1) * P], m_h[:, c * P:(c + 1) * P])
                m.then_inc(full[6], 1)
                pe.wait_ge(evac[6], E_BASE[6] + b + 1)
                for i in range(2):
                    pe.wait_ge(e_landed[4 + i], 16 * b + 16)
                    for kk in range(2):
                        k = 2 * i + kk
                        for n in range(2):
                            m = mm(ps[7][64 * n:64 * n + 64, :], m_hT[:, kk * P + 64 * i:kk * P + 64 * i + 64],
                                   ring[:, (4 + i) * UNIT + kk * D + n * 512:(4 + i) * UNIT + kk * D + (n + 1) * 512],
                                   k == 0, k == 3)
                            if kk == 0 and n == 0:
                                m.then_inc(exp_begun, 1)
                m.then_inc(full[7], 1)
            pe.wait_ge(evac[7], E_BASE[7] + n_blocks)
            combine().then_inc(y_done, 1)

        @block.scalar
        def _(act):
            chain, ahead = [0], [0]

            def did(ins):
                ins.then_inc(act_chain, 1)
                chain[0] += 1

            def own():
                act.wait_ge(act_chain, chain[0])

            def filled(t):
                act.wait_ge(full[t[0]], t[1] + 1)
                return ps[t[0]]

            def split(u, it=0):
                n = half_size(u)
                act.wait_ge(landed[u % RAW], 16 * (u // RAW + 1) + 16 * it)
                for j in range(2):
                    c = 2 * u + j
                    if not isinstance(it, int) or c >= PARTS:
                        act.wait_ge(half_begun, c - PARTS + 2 + 2 * RAW * it)
                    nc.scalar.activation(part(w_hi, c, 0, n), raw_slot(u, j * n, n), ACT.Copy).then_inc(hi_made, 1)

            def split_to(u):
                while ahead[0] <= min(u, N_UNITS - 1):
                    split(ahead[0])
                    ahead[0] += 1

            def square(q, src, w):
                if q >= 2:
                    act.wait_ge(sq_used, q - 1)
                nc.scalar.activation(sq[:, q % 2, 0:w], src, ACT.Square).then_inc(sq_made, 1)

            def squares_of_h(n, w):
                for m in range(KT):
                    if n:
                        act.wait_ge(h_ready, 8 * ((n - 1) // 2) + m + 1)
                    square(8 * n + m, tile(h, m, w), w)

            def root(t, src, dst):
                act.wait_ge(evac[t[0]], t[1] + 1)
                nc.scalar.activation(dst, src, ACT.Sqrt).then_inc(std_made, 1)

            def root_stat(n, w):
                root(plan[f"stat{n}"].at(0), var[:, 0:w], std[:, 0:w])

            def branch_out(name, n, g, table, w, per=2):
                u0, T = plan[name]
                for m in range(KT):
                    split_to(u0 + m // per + 1)
                    t = T.at(m)
                    bank = filled(t)
                    square(8 * n + m, bank[:, 0:w], w)
                    nc.scalar.activation(tile(zg, m, w), bank[:, 0:w], ACT.Copy,
                                         scale=gain(g, m, table)).then_inc(evac[t[0]], 1)
                root_stat(n, w)

            def ffn(n, g, w):
                u0, T = plan[f"in{n}"]
                split_to(u0)

                def gate(j, it):
                    tg, tu = T.at(2 * j, it, 4), T.at(2 * j + 1, it, 4)
                    act.wait_ge(full[tg[0]], tg[1] + 1)
                    act.wait_ge(evac[tu[0]], tu[1])
                    nc.scalar.activation(tile(sg, j, w), ps[tg[0]][:, 0:w], ACT.Silu).then_inc(evac[tg[0]], 1)

                with act.Fori(0, FT // 2 - 1) as it:
                    for j in range(2):
                        split(u0 + j + 1, it)
                        gate(j, it)
                ahead[0] = u0 + FT - 1
                for j in range(2):
                    split_to(u0 + FT - 1 + j)
                    gate(j, FT // 2 - 1)
                branch_out(f"out{n}", 2 * g_index[n] + 1, g, halfg, w, 1)

            g_index = {0: 0, 1: 2, 2: 3, 3: 5}

            act.wait_ge(consts_in, 16)
            act.wait_ge(params_in, 16)
            act.wait_ge(lb_in, 1)
            nc.scalar.activation(small[:, 0:8], small[:, 0:8], ACT.Exp).then_inc(lb_exp, 1)
            for i in range(8):
                t = plan["bias"].at(i)
                nc.scalar.activation(b_br[:, i * 384:(i + 1) * 384], filled(t)[:, 0:384], ACT.Copy)\
                    .then_inc(evac[t[0]], 1)
            split_to(0)
            act.wait_ge(x_in, 16)
            squares_of_h(0, TA)
            root_stat(0, TA)
            act.wait_ge(lb_in, 2)
            ffn(0, 1, TA)
            squares_of_h(2, TA)
            root_stat(2, TA)

            t = plan["lr"].at(0)
            nc.scalar.activation(g_lr[0:RANK, :], filled(t)[0:RANK, 0:TA], ACT.Copy).then_inc(evac[t[0]], 1)
            for i in range(8):
                t = plan["r"][1].at(i)
                split_to(plan["r"][0] + i // 2 + 1)
                nc.scalar.activation(tile(g_r, i, TA), filled(t)[:, 0:TA], ACT.Silu).then_inc(evac[t[0]], 1)
            t = plan["gate"].at(3)
            act.wait_ge(evac[t[0]], t[1] + 1)
            did(nc.scalar.activation(g_e0, g_b, ACT.Abs))
            own()
            did(nc.scalar.activation(g_e1, g_e0, ACT.Exp, scale=-1.0))
            own()
            nc.scalar.activation(g_e2, g_e1, ACT.Ln, bias=C("ones", 0, 1)).then_inc(soft_made, 1)
            act.wait_ge(decay_in, 1)
            nc.scalar.activation(g_e0, g_b, ACT.Exp, scale=1.0 / 16).then_inc(decay_made, 1)
            nc.scalar.activation(g_e1, g_b, ACT.Exp, scale=-1.0 / 16).then_inc(decay_made, 1)
            act.wait_ge(decay_in, 2)
            nc.scalar.activation(g_e2, g_e2, ACT.Exp, scale=1.0 / 16).then_inc(decay_made, 1)
            split_to(plan["gout"][0])
            for i in range(GH):
                t = plan["kwT"].at(i)
                bank = filled(t)
                nc.scalar.activation(g_kwT[:, i * 384:i * 384 + 256], bank[:, 0:256], ACT.Copy)
                nc.scalar.activation(g_kwT[0:META, i * 384 + 256:(i + 1) * 384], bank[0:META, 256:384], ACT.Copy)\
                    .then_inc(evac[t[0]], 1)
            for i in range(8):
                t = plan["o"].at(i)
                bank = filled(t)
                nc.scalar.activation(tile(g_sq, i, TA), bank[:, 0:TA], ACT.Square)
                nc.scalar.activation(tile(g_o, i, TA), bank[:, 0:TA], ACT.Copy).then_inc(evac[t[0]], 1)
            for i in range(GH):
                root(plan["gst"].at(i), tile(g_kw, i, TA), tile(g_kw, i, TA))
            branch_out("gout", 3, 3, par, TA)
            squares_of_h(4, TA)
            root_stat(4, TA)
            ffn(1, 5, TA)
            squares_of_h(6, TA)
            root_stat(6, TA)

            for i in range(2):
                t = plan["ks"][1].at(i)
                split_to(plan["vs"][0])
                nc.scalar.activation(tile(s_kraw, i, TA), filled(t)[:, 0:TA], ACT.Copy).then_inc(evac[t[0]], 1)
            split_to(plan["in2"][0])
            for i, n in enumerate((P, P, META)):
                t = plan["vs"][1].at(i)
                nc.scalar.activation(vs[0:n, i, :], filled(t)[0:n, 0:256], ACT.Copy).then_inc(evac[t[0]], 1)
            ffn(2, 7, SEQ)
            squares_of_h(8, SEQ)
            root_stat(8, SEQ)

            for i in range(8):
                t = plan["sq"][1].at(i)
                split_to(plan["sq"][0] + i // 2 + 1)
                nc.scalar.activation(s_q[:, i * SEQ:(i + 1) * SEQ], filled(t)[:, 0:SEQ], ACT.Copy).then_inc(evac[t[0]], 1)

            def attend(names, groups, first, pb, pitch, pT, widths, n_full, meta, o, sinks):
                S, TT, V = (plan[x] for x in names)
                for g in range(groups):
                    at = 16 + (g % 2) * 16
                    act.wait_ge(neg_max, first + g + 1)
                    if sinks:
                        nc.scalar.activation(small[:, at + 4:at + 8], small[:, at + 4:at + 8], ACT.Exp)
                    for u in range(4):
                        a = ((g % 2) * 4 + u) * pitch
                        p = pb[:, a:a + widths[u // 2]]
                        e = nc.scalar.activation(p, p, ACT.Exp, bias=small[:, at + u:at + u + 1],
                                                 accum_out=small[:, at + 8 + u:at + 9 + u])
                        if u == 3:
                            e.then_inc(exp_made, 1)
                    for u in range(4):
                        t = TT.at(4 * g + u)
                        bank = filled(t)
                        if g:
                            act.wait_ge(full[V.at(g - 1)[0]], V.at(g - 1)[1] + 1)
                        n = n_full[u // 2] * P
                        c = nc.scalar.activation(pT[:, u * 384:u * 384 + n], bank[:, 0:n], ACT.Copy)
                        if meta:
                            c = nc.scalar.activation(pT[0:META, u * 384 + n:u * 384 + n + P], bank[0:META, n:n + P], ACT.Copy)
                        c.then_inc(evac[t[0]], 1)
                    t = V.at(g)
                    nc.scalar.activation(o[:, g * SEQ:(g + 1) * SEQ], filled(t)[:, 0:SEQ], ACT.Copy).then_inc(evac[t[0]], 1)

            attend(("ss", "sT", "sv"), 8, 0, a_p, TA, a_pT, (P + META, SEQ + META), (1, 2), True, s_o, True)
            branch_out("sout", 9, 9, par, SEQ)
            squares_of_h(10, SEQ)
            root_stat(10, SEQ)
            ffn(3, 11, SEQ)

            def b_in(i):
                return W("b_in", i, i + 1)

            def sect(name, i, dst, func, col):
                t = plan[name][1].at(i)
                split_to(plan[name][0] + i // 2 + 1)
                nc.scalar.activation(dst, filled(t)[:, 0:SEQ], func, bias=b_in(col)).then_inc(evac[t[0]], 1)

            for i in range(4):
                t = plan["z"][1].at(i)
                split_to(plan["z"][0] + i // 2 + 1)
                bank = filled(t)
                nc.scalar.activation(b_e[:, i * SEQ:(i + 1) * SEQ], bank[:, 0:SEQ], ACT.Sigmoid, bias=b_in(4 + i))
                nc.scalar.activation(b_kf[:, i * SEQ:(i + 1) * SEQ], bank[:, 0:SEQ], ACT.Sigmoid, scale=-1.0,
                                     bias=small[:, 12 + i:13 + i]).then_inc(evac[t[0]], 1)
            for i in range(4):
                sect("hq", i, b_q[:, i * SEQ:(i + 1) * SEQ], ACT.Silu, i)
            act.wait_ge(hg_arg, 1)
            nc.scalar.activation(b_b, b_e, ACT.Ln).then_inc(hg_ln, 1)
            for j in range(8):
                for i in range(2):
                    name, m = ("ga", 2 * j + i) if j < 4 else ("gb", 2 * (j - 4) + i)
                    dst = tile(b_sga, m, SEQ) if j < 4 else b_sgb[:, m * SEQ:(m + 1) * SEQ]
                    sect(name, m, dst, ACT.Sigmoid, (28 if j < 4 else 36) + m)
                act.wait_ge(lvl_in, j + 1)
                nc.scalar.activation(b_e, b_e, ACT.Exp).then_inc(lvl_exp, 1)
            for i in range(4):
                sect("hgate", i, b_sg[:, i * SEQ:(i + 1) * SEQ], ACT.Silu, 12 + i)
            for i in range(4):
                sect("mq", i, b_mq[:, i * SEQ:(i + 1) * SEQ], ACT.Identity, 16 + i)
            for i in range(4):
                sect("mk", i, b_mk[:, i * SEQ:(i + 1) * SEQ], ACT.Identity, 20 + i)
            split_to(plan["pa"][0])
            for i in range(4):
                t = plan["ho"].at(i)
                bank = filled(t)
                nc.scalar.activation(b_sq[:, i * SEQ:(i + 1) * SEQ], bank[:, 0:SEQ], ACT.Square)
                nc.scalar.activation(b_a[:, i * SEQ:(i + 1) * SEQ], bank[:, 0:SEQ], ACT.Copy).then_inc(evac[t[0]], 1)
            for i in range(4):
                root(plan["hst"].at(i), b_e[:, i * SEQ:(i + 1) * SEQ], b_e[:, i * SEQ:(i + 1) * SEQ])
            attend(("bs", "bT", "bv"), 4, 8, b_p, SEQ, b_pT, (P, SEQ), (1, 2), False, b_bo, False)
            split_to(N_UNITS)
            h3 = h[:, :].rearrange("p (m t) -> p m t", m=KT)[:, :, 0:SEQ]
            z3 = zg[:, :].rearrange("p (m t) -> p m t", m=KT)[:, :, 0:SEQ]
            act.wait_ge(centred, 1)
            nc.scalar.activation(z3, h3, ACT.Square).then_inc(ln_squared, 1)
            root(plan["lnvar"].at(0), var[:, 0:SEQ], std[:, 0:SEQ])
            for i in range(4):
                t = plan["xtok"].at(i)
                nc.scalar.activation(m_x[:, (i // 2) * D + (i % 2) * 512:(i // 2) * D + (i % 2) * 512 + 512],
                                     filled(t)[:, :], ACT.Copy).then_inc(evac[t[0]], 1)
            act.wait_ge(route_in, 1)
            nc.scalar.activation(r_["ge"], r_["ge"], ACT.Exp).then_inc(route_exp, 1)
            act.wait_ge(route_in, 2)
            nc.scalar.activation(r_["ev"], r_["ev"], ACT.Exp).then_inc(route_exp, 1)

            act.wait_ge(table_ready, 1)
            n_blocks = act.value_load(meta_i[0:1, MAXB:MAXB + 1], min_val=1, max_val=MAXB)
            t = plan["e_gather"].at(0)
            nc.scalar.activation(m_xT, filled(t)[:, :], ACT.Copy).then_inc(evac[4], 1)
            with act.Fori(0, n_blocks) as b:
                act.wait_ge(full[5], E_BASE[5] + b + 1)
                act.wait_ge(evac[5], E_BASE[5] + b)
                nc.scalar.activation(m_sg, ps[5][:, 0:256], ACT.Silu).then_inc(silu_made, 1)
                act.wait_ge(full[4], E_BASE[4] + b + 1)
                nc.scalar.activation(m_xT, ps[4][:, :], ACT.Copy).then_inc(evac[4], 1)
                act.wait_ge(full[6], E_BASE[6] + b + 1)
                nc.scalar.activation(m_turn, ps[6][:, :], ACT.Copy).then_inc(evac[6], 1)

            for p in range(2):
                act.wait_ge(fin_centred, p + 1)
                nc.scalar.activation(zg[:, p * D:(p + 1) * D], m_o[:, p * D:(p + 1) * D], ACT.Square,
                                     accum_out=small[:, 100 + p:101 + p]).then_inc(fin_squared, 1)
            act.wait_ge(fin_var, 1)
            nc.scalar.activation(small[:, 104:106], small[:, 102:104], ACT.Sqrt).then_inc(fin_std, 1)
            for p in range(2):
                act.wait_ge(out_ready, p + 1)
                act.dma_start(out[0, p * P:(p + 1) * P, :], m_o[:, p * D:(p + 1) * D]).then_inc(out_stored, 16)
            act.wait_ge(out_stored, 32)

        @block.vector
        def _(dve):
            chain, ahead, stds = [0], [0], [0]
            v = nc.vector

            def did(ins):
                ins.then_inc(dve_chain, 1)
                chain[0] += 1
                return chain[0]

            def own(c=None):
                dve.wait_ge(dve_chain, chain[0] if c is None else c)

            def then(ins):
                did(ins)
                own()

            def filled(t):
                dve.wait_ge(full[t[0]], t[1] + 1)
                return ps[t[0]]

            def mine(t):
                dve.wait_ge(evac[t[0]], t[1] + 1)

            def split(u, it=0):
                n = half_size(u)
                for j in range(2):
                    c = 2 * u + j
                    dve.wait_ge(hi_made, c + 1 + 2 * RAW * it)
                    v.tensor_tensor(part(w_lo, c, 0, n), raw_slot(u, j * n, n), part(w_hi, c, 0, n).bitcast(F32),
                                    ALU.subtract).then_inc(lo_made, 1)

            def split_to(u):
                while ahead[0] <= min(u, N_UNITS - 1):
                    split(ahead[0])
                    ahead[0] += 1

            def low_part(dst, src):
                return v.tensor_tensor(dst[1], src, dst[0].bitcast(F32), ALU.subtract)

            def to_x(m, src, w):
                dst = tile(x_hi, m, w), tile(x_lo, m, w)
                then(v.tensor_copy(dst[0], src))
                low_part(dst, src).then_inc(x_ready, 1)

            def add_square(n, m, w):
                q = 8 * n + m
                dve.wait_ge(sq_made, q + 1)
                if m == 0:
                    v.tensor_copy(acc[:, 0:w], sq[:, q % 2, 0:w]).then_inc(sq_used, 1)
                else:
                    dve.wait_ge(sq_used, q)
                    v.tensor_tensor(acc[:, 0:w], acc[:, 0:w], sq[:, q % 2, 0:w], ALU.add).then_inc(sq_used, 1)

            def inverse_root(t, w, mean_of, eps, mid, root, dst):
                bank = filled(t)
                v.tensor_scalar(mid, bank[:, 0:w], 1.0 / mean_of, eps, ALU.mult, ALU.add).then_inc(evac[t[0]], 1)
                stds[0] += 1
                dve.wait_ge(std_made, stds[0])
                then(v.reciprocal(dst, root))

            def inverse_rms(n, w):
                inverse_root(plan[f"stat{n}"].at(0), w, D, EPS, var[:, 0:w], std[:, 0:w], rs[:, 0:w])

            def normalise(g, w, col=None, dst=(x_hi, x_lo)):
                def whole(m, out):
                    gm = gain(g, m) if col is None else W(col, m, m + 1)
                    return v.scalar_tensor_tensor(out, tile(h, m, w), gm, rs[:, 0:w], ALU.mult, ALU.mult)

                steps = []
                for m in range(KT + 1):
                    if m < KT:
                        whole(m, tile(dst[0], m, w))
                        steps.append(did(whole(m, tile(zg, m, w))))
                    if m:
                        own(steps[m - 1])
                        low_part((tile(dst[0], m - 1, w), tile(dst[1], m - 1, w)), tile(zg, m - 1, w))\
                            .then_inc(x_ready, 1)

            def residual(name, n, w, follow=True, per=2):
                u0, T = plan[name]
                for m in range(KT):
                    split_to(u0 + m // per + 1)
                    add_square(n, m, w)
                inverse_rms(n, w)
                for m in range(KT):
                    mine(T.at(m))
                steps = [did(v.tensor_tensor(tile(zg, 0, w), tile(zg, 0, w), rs[:, 0:w], ALU.mult))]
                for m in range(KT):
                    if m + 1 < KT:
                        z = tile(zg, m + 1, w)
                        steps.append(did(v.tensor_tensor(z, z, rs[:, 0:w], ALU.mult)))
                    own(steps[m])
                    v.tensor_tensor(tile(h, m, w), tile(h, m, w), tile(zg, m, w), ALU.add).then_inc(h_ready, 1)
                    if follow and m:
                        add_square(n + 1, m - 1, w)
                if not follow:
                    dve.wait_ge(h_ready, 8 * ((n + 1) // 2))
                    for m in range(KT):
                        to_x(m, tile(h, m, w), w)
                if follow:
                    add_square(n + 1, KT - 1, w)
                    inverse_rms(n + 1, w)

            def ffn_in(n, w):
                u0, T = plan[f"in{n}"]
                split_to(u0)

                def hidden(j, it):
                    tg, tu = T.at(2 * j, it, 4), T.at(2 * j + 1, it, 4)
                    at = it * (2 * TA) + j * TA
                    cols = slice(at, at + w) if isinstance(it, int) else bass.ds(at, w)
                    dve.wait_ge(full[tu[0]], tu[1] + 1)
                    dve.wait_ge(evac[tg[0]], tg[1] + 1)
                    v.tensor_tensor(hid_hi[:, cols], ps[tu[0]][:, 0:w], tile(sg, j, w), ALU.mult)
                    v.tensor_tensor(tile(hw, j, w), ps[tu[0]][:, 0:w], tile(sg, j, w), ALU.mult).then_inc(hw_made, 1)
                    dve.wait_ge(hw_made, hw_base[0] + 2 * it + j + 1)
                    low_part((hid_hi[:, cols], hid_lo[:, cols]), tile(hw, j, w)).then_inc(evac[tu[0]], 1)

                with dve.Fori(0, FT // 2 - 1) as it:
                    for j in range(2):
                        split(u0 + j + 1, it)
                        hidden(j, it)
                ahead[0] = u0 + FT - 1
                for j in range(2):
                    split_to(u0 + FT - 1 + j)
                    hidden(j, FT // 2 - 1)
                hw_base[0] += FT

            hw_base = [0]
            dve.wait_ge(params_in, 16)
            l0, l1 = W("lb_logits", 0, 4), W("lb_logits", 4, 8)
            then(v.tensor_tensor(small[:, 8:12], l0, l1, ALU.max))
            did(v.tensor_tensor(small[:, 0:4], l0, small[:, 8:12], ALU.subtract))
            v.tensor_tensor(small[:, 4:8], l1, small[:, 8:12], ALU.subtract).then_inc(lb_in, 1)
            v.tensor_scalar(halfg[:, :], W("gains"), 0.5, None, ALU.mult).then_inc(lb_in, 1)
            then(v.tensor_scalar(small[:, 12:16], W("b_in", 4, 8), -1.0, None, ALU.mult))
            dve.wait_ge(lb_exp, 1)
            then(v.tensor_tensor(small[:, 8:12], small[:, 0:4], small[:, 4:8], ALU.add))
            then(v.reciprocal(small[:, 8:12], small[:, 8:12]))
            LB, LB1 = slice(240, 244), slice(244, 248)
            then(v.tensor_tensor(small[:, LB], small[:, 0:4], small[:, 8:12], ALU.mult))
            then(v.tensor_scalar(small[:, LB1], small[:, LB], -1.0, 1.0, ALU.mult, ALU.add))

            split_to(0)
            for m in range(KT):
                add_square(0, m, TA)
            inverse_rms(0, TA)
            dve.wait_ge(x_in, 16)
            normalise(0, TA)
            dve.wait_ge(bias_out, 8 * 16)
            ffn_in(0, TA)
            residual("out0", 1, TA, per=1)
            normalise(2, TA)
            split_to(plan["r"][0] + 1)

            for i in range(GH):
                t = plan["gate"].at(i)
                v.tensor_scalar(tile(g_b, i, TA), filled(t)[:, 0:TA], W("b_gate", i, i + 1), None, ALU.add)\
                    .then_inc(evac[t[0]], 1)
            mine(plan["gate"].at(3))
            split_to(plan["v"][0])
            dve.wait_ge(soft_made, 1)
            then(v.tensor_scalar(g_b, g_b, 0.0, None, ALU.min))
            then(v.tensor_tensor(g_e2, g_b, g_e2, ALU.subtract))
            for i in range(GH):
                s = v.tensor_tensor_scan(tile(g_b, i, TA), C("reset_g"), tile(g_e2, i, TA), 0.0, ALU.mult, ALU.add)
            s.then_inc(decay_in, 1)
            dve.wait_ge(decay_in, 1)
            b4 = g_b.rearrange("p (h t) -> p h t", h=GH)
            e4 = g_e2.rearrange("p (h t) -> p h t", h=GH)
            for i in range(GH):
                bx = g_b[:, i * TA:i * TA + SEQ].rearrange("p (c s) -> p c s", s=CH)
                ex = g_e2[:, i * TA:i * TA + SEQ].rearrange("p (c s) -> p c s", s=CH)
                v.tensor_tensor(ex, bx[:, :, CH - 1:CH].to_broadcast([P, 4, CH]), bx, ALU.subtract)
            v.tensor_tensor(e4[:, :, SEQ:TA], b4[:, :, TA - 1:TA].to_broadcast([P, GH, META]), b4[:, :, SEQ:TA],
                            ALU.subtract).then_inc(decay_in, 1)
            for j in range(4):
                split_to(plan["v"][0] + j + 1)
                for s, n in enumerate((P, P, META)):
                    t = plan["v"][1].at(3 * j + s)
                    dst = g_vm[0:n, j * 256:(j + 1) * 256] if s == 2 else g_v[:, s * D + j * 256:s * D + (j + 1) * 256]
                    v.tensor_copy(dst, filled(t)[0:n, 0:256]).then_inc(evac[t[0]], 1)
            dve.wait_ge(decay_made, 3)
            for i in range(GH):
                split_to(plan["k"][0] + i // 2 + 1)
                t = plan["k"][1].at(i)
                bank = filled(t)
                v.tensor_tensor(tile(g_k, i, TA), bank[:, 0:TA], tile(g_e1, i, TA), ALU.mult)
                v.tensor_tensor(tile(g_kw, i, TA), bank[:, 0:TA], tile(g_e2, i, TA), ALU.mult).then_inc(evac[t[0]], 1)
            for i in range(GH):
                split_to(plan["q"][0] + i // 2 + 1)
                t = plan["q"][1].at(i)
                v.scalar_tensor_tensor(tile(g_q, i, TA), filled(t)[:, 0:TA], float(GDK) ** -0.5, tile(g_e0, i, TA),
                                       ALU.mult, ALU.mult).then_inc(evac[t[0]], 1)
            decays = g_e0.rearrange("p (h t) -> p h t", h=GH)[:, :, CH - 1:SEQ:CH]
            did(v.tensor_copy(g_dec.rearrange("p (h c) -> p h c", h=GH), decays))
            for i in range(GH):
                t = plan["att"].at(i)
                bank = filled(t)
                v.tensor_tensor(g_att[:, i * TA:i * TA + SEQ].rearrange("p (a b) -> p a b", a=2),
                                bank[:, 0:SEQ].rearrange("p (a b) -> p a b", a=2),
                                C("pairmask").rearrange("p (a b) -> p a b", a=1).to_broadcast([P, 2, P]), ALU.mult)
                v.tensor_tensor(g_att[0:META, i * TA + SEQ:(i + 1) * TA], bank[0:META, SEQ:TA],
                                C("pairmask", 0, META, slice(0, META)), ALU.mult).then_inc(evac[t[0]], 1)
            for i in range(GH):
                def state(c):
                    return g_s[:, (i * 4 + c) * GDV:(i * 4 + c + 1) * GDV]

                def decay(c):
                    return g_dec[:, i * 4 + c:i * 4 + c + 1]

                ta, tb, tc = (plan["kv"].at(3 * i + c) for c in range(3))
                bank = filled(ta)
                then(v.tensor_copy(state(0), bank[:, 0:256]))
                v.scalar_tensor_tensor(state(1), state(0), decay(0), bank[:, 256:512], ALU.mult, ALU.add)\
                    .then_inc(evac[ta[0]], 1)
                mine(ta)
                v.scalar_tensor_tensor(state(2), state(1), decay(1), filled(tb)[:, 0:256], ALU.mult, ALU.add)\
                    .then_inc(evac[tb[0]], 1)
                mine(tb)
                v.scalar_tensor_tensor(state(3), state(2), decay(2), filled(tc)[:, 0:256], ALU.mult, ALU.add)\
                    .then_inc(evac[tc[0]], 1)
            for i in range(GH):
                r = tile(g_kw, i, TA)
                inverse_root(plan["gst"].at(i), TA, GDV, EPS, r, r, r)
                for half in range(2):
                    o = tile(g_o, 2 * i + half, TA)
                    then(v.scalar_tensor_tensor(o, o, W("gla_norm", half, half + 1), r, ALU.mult, ALU.mult))
                    then(v.tensor_tensor(o, o, tile(g_r, 2 * i + half, TA), ALU.mult))
                    to_x(2 * i + half, o, TA)
            residual("gout", 3, TA)
            normalise(4, TA)
            ffn_in(1, TA)
            residual("out1", 5, TA, per=1)
            normalise(None, TA, "kv_norm", (hid_hi, hid_lo))
            normalise(6, TA)
            split_to(plan["vs"][0])

            for i in range(2):
                t = plan["krot"].at(i)
                bank = filled(t)
                v.tensor_tensor(tile(s_krot, i, TA), bank[:, 0:TA], C("sin"), ALU.mult).then_inc(evac[t[0]], 1)
                mine(plan["ks"][1].at(i))
                then(v.tensor_tensor(kT[:, i, :], tile(s_kraw, i, TA), C("cos"), ALU.mult))
                then(v.tensor_tensor(kT[:, i, :], kT[:, i, :], tile(s_krot, i, TA), ALU.add))
            ffn_in(2, SEQ)
            residual("out2", 7, SEQ, per=1)
            normalise(8, SEQ)

            for i in range(8):
                split_to(plan["sq"][0] + i // 2 + 1)
                t = plan["qrot"].at(i)
                bank = filled(t)
                mine(plan["sq"][1].at(i))
                q = s_q[:, i * SEQ:(i + 1) * SEQ]
                x = s_t[:, (i % 2) * SEQ:(i % 2 + 1) * SEQ]
                did(v.tensor_tensor(q, q, C("cos", 0, SEQ), ALU.mult))
                v.tensor_tensor(x, bank[:, 0:SEQ], C("sin", 0, SEQ), ALU.mult).then_inc(evac[t[0]], 1)
                own()
                mine(t)
                v.tensor_tensor(q, q, x, ALU.add).then_inc(q_roped, 1)

            def attend(names, groups, first, pb, pitch, widths, mask_of, sinks):
                S = plan[names[0]]

                def maxima(g):
                    at = 16 + (g % 2) * 16
                    for u in range(4):
                        w = widths[u // 2]
                        t = S.at(4 * g + u)
                        p = pb[:, ((g % 2) * 4 + u) * pitch:((g % 2) * 4 + u) * pitch + w]
                        v.scalar_tensor_tensor(p, filled(t)[:, 0:w], 0.125, mask_of(g, u), ALU.mult, ALU.add)\
                            .then_inc(evac[t[0]], 1)
                    mine(t)
                    p4 = pb[:, (g % 2) * 4 * pitch:(g % 2 + 1) * 4 * pitch].rearrange("p (u t) -> p u t", u=4)
                    did(v.tensor_reduce(small[:, at:at + 2], p4[:, 0:2, 0:widths[0]], AX, ALU.max))
                    then(v.tensor_reduce(small[:, at + 2:at + 4], p4[:, 2:4, 0:widths[1]], AX, ALU.max))
                    if sinks:
                        sk = W("sinks", 4 * g, 4 * g + 4)
                        then(v.tensor_tensor(small[:, at:at + 4], small[:, at:at + 4], sk, ALU.max))
                        then(v.tensor_scalar(small[:, at:at + 4], small[:, at:at + 4], -1.0, None, ALU.mult))
                        v.tensor_tensor(small[:, at + 4:at + 8], small[:, at:at + 4], sk, ALU.add).then_inc(neg_max, 1)
                    else:
                        v.tensor_scalar(small[:, at:at + 4], small[:, at:at + 4], -1.0, None, ALU.mult)\
                            .then_inc(neg_max, 1)

                maxima(0)
                for g in range(groups):
                    if g + 1 < groups:
                        maxima(g + 1)
                    at = 16 + (g % 2) * 16
                    dve.wait_ge(exp_made, first + g + 1)
                    if sinks:
                        then(v.tensor_tensor(small[:, at + 8:at + 12], small[:, at + 8:at + 12],
                                             small[:, at + 4:at + 8], ALU.add))
                    then(v.reciprocal(small[:, at + 12:at + 16], small[:, at + 8:at + 12]))
                    for u in range(4):
                        p = pb[:, ((g % 2) * 4 + u) * pitch:((g % 2) * 4 + u) * pitch + widths[u // 2]]
                        v.tensor_scalar(p, p, small[:, at + 12 + u:at + 13 + u], None, ALU.mult).then_inc(p_ready, 1)

            attend(("ss",), 8, 0, a_p, TA, (P + META, SEQ + META), lambda g, u: C("swa0") if u < 2 else C("swa1"), True)
            for m in range(KT):
                mine(plan["sv"].at(m))
                to_x(m, s_o[:, m * SEQ:(m + 1) * SEQ], SEQ)
            residual("sout", 9, SEQ)
            normalise(10, SEQ)
            ffn_in(3, SEQ)
            residual("out3", 11, SEQ, follow=False, per=1)

            dve.wait_ge(bias_in, 8 * 16)
            for i in range(8):
                last = v.tensor_tensor(b_bias[:, i * SEQ:(i + 1) * SEQ], b_bias[:, i * SEQ:(i + 1) * SEQ], C("ninf"), ALU.add)
            did(last)
            did(v.memset(b_att[:, 0:1024], 0.0))
            for i in range(4):
                t = plan["z"][1].at(i)
                split_to(plan["z"][0] + i // 2 + 1)
                mine(t)
                e = b_e[:, i * SEQ:(i + 1) * SEQ]
                k = b_kf[:, i * SEQ:(i + 1) * SEQ]
                did(v.tensor_scalar(k, k, small[:, 244 + i:245 + i], None, ALU.mult))
                a = v.tensor_scalar(e, e, small[:, 244 + i:245 + i], small[:, 240 + i:241 + i], ALU.mult, ALU.add)
            a.then_inc(hg_arg, 1)
            split_to(plan["hq"][0] + 2)
            dve.wait_ge(hg_ln, 1)
            then(v.tensor_copy(b_e, b_b))
            for i in range(4):
                did(v.tensor_tensor_scan(b_b[:, i * SEQ:(i + 1) * SEQ], C("reset_h"), b_e[:, i * SEQ:(i + 1) * SEQ],
                                         0.0, ALU.mult, ALU.add))
            own()
            dve.wait_ge(levels_in, 16)

            def merge(n):
                for p in range(2):
                    t = plan["lvl"].at(2 * n + p)
                    bank = filled(t)
                    mask = b_lv[:, n * P:(n + 1) * P].bitcast(U32).rearrange("p (a s) -> p a s", a=1).to_broadcast([P, 4, P])
                    v.copy_predicated(b_att[:, p * 512:(p + 1) * 512].rearrange("p (a s) -> p a s", a=4), mask,
                                      bank[:, :].rearrange("p (a s) -> p a s", a=4)).then_inc(evac[t[0]], 1)

            for n in range(8):
                half = LEVELS[n] if n < 7 else P
                b3 = b_b.rearrange("p (g e s) -> p g e s", e=2, s=half)
                d3 = b_e.rearrange("p (g e s) -> p g e s", e=2, s=half)
                G = 4 * SEQ // (2 * half)
                ref = b3[:, :, 0, half - 1:half].to_broadcast([P, G, half])
                did(v.tensor_tensor(d3[:, :, 0, :], ref, b3[:, :, 0, :], ALU.subtract))
                if n < 7:
                    last = v.tensor_tensor(d3[:, :, 1, :], b3[:, :, 1, :], ref, ALU.subtract)
                else:
                    last = v.tensor_copy(d3[:, :, 1, :], b3[:, :, 1, :])
                last.then_inc(lvl_in, 1)
                split_to(plan["ga"][0] + n + 2)
                if n:
                    t = plan["lvl"].at(2 * (n - 1) + 1)
                    filled(t)
                dve.wait_ge(lvl_exp, n + 1)
                q3, k3, w3 = (x.rearrange("p (g e s) -> p g e s", e=2, s=half) for x in (b_q, b_kf, b_qk))
                if n == 0:
                    mine(plan["hq"][1].at(3))
                did(v.tensor_tensor(w3[:, :, 0, :], k3[:, :, 0, :], d3[:, :, 0, :], ALU.mult))
                v.tensor_tensor(w3[:, :, 1, :], q3[:, :, 1, :], d3[:, :, 1, :], ALU.mult).then_inc(lvl_ready, 1)
                dve.wait_ge(lvl_ready, n + 1)
                if n:
                    merge(n - 1)
                    mine(plan["lvl"].at(2 * (n - 1) + 1))
            split_to(plan["hgate"][0] + 2)
            merge(7)
            split_to(plan["hi"][0])
            t = plan["cross"].at(0)
            v.tensor_copy(b_att[:, 1024:1536], filled(t)[:, :]).then_inc(evac[t[0]], 1)
            dve.wait_ge(rows_in, 16)
            for name, dst, at in (("hi", b_v, 0), ("mv", b_mv, 512)):
                for j in range(2):
                    split_to(plan[name][0] + j + 1)
                    for p in range(2):
                        t = plan[name][1].at(2 * j + p)
                        v.tensor_tensor(dst[:, p * 512 + j * 256:p * 512 + (j + 1) * 256], filled(t)[:, 0:256],
                                        b_rows[:, at + j * 256:at + (j + 1) * 256], ALU.add).then_inc(evac[t[0]], 1)
            for i in range(4):
                r = b_e[:, i * SEQ:(i + 1) * SEQ]
                inverse_root(plan["hst"].at(i), SEQ, P, LN_EPS, r, r, r)
                mine(plan["hgate"][1].at(i))
                o = b_a[:, i * SEQ:(i + 1) * SEQ]
                then(v.scalar_tensor_tensor(o, o, W("hg_norm", i, i + 1), r, ALU.mult, ALU.mult))
                then(v.tensor_tensor(o, o, b_sg[:, i * SEQ:(i + 1) * SEQ], ALU.mult))
                to_x(i, o, SEQ)

            def moba_bias(g, u):
                head = 2 * g + u % 2
                return b_bias[:, head * SEQ + P:(head + 1) * SEQ] if u < 2 else b_bias[:, head * SEQ:(head + 1) * SEQ]

            attend(("bs",), 4, 8, b_p, SEQ, (P, SEQ), moba_bias, False)
            for m in range(4):
                mine(plan["bv"].at(m))
                to_x(4 + m, b_bo[:, m * SEQ:(m + 1) * SEQ], SEQ)

            for i in range(KT):
                split_to(plan["pa"][0] + i // 4 + 1)
                t = plan["pa"][1].at(i)
                v.tensor_tensor(tile(zg, i, SEQ), filled(t)[:, 0:SEQ], tile(b_sga, i, SEQ), ALU.mult)\
                    .then_inc(evac[t[0]], 1)
            for i in range(KT):
                split_to(plan["pb"][0] + i // 4 + 1)
                t = plan["pb"][1].at(i)
                gate = b_sgb[:, i * SEQ:(i + 1) * SEQ]
                v.tensor_tensor(gate, filled(t)[:, 0:SEQ], gate, ALU.mult).then_inc(evac[t[0]], 1)
                mine(t)
                did(v.tensor_tensor(tile(zg, i, SEQ), tile(zg, i, SEQ), gate, ALU.add))
            own()
            for i in range(KT):
                to_x(i, tile(zg, i, SEQ), SEQ)
            for i in range(KT):
                split_to(plan["wo"][0] + i // 2 + 1)
                t = plan["wo"][1].at(i)
                v.scalar_tensor_tensor(tile(h, i, SEQ), tile(h, i, SEQ), ALPHA, filled(t)[:, 0:SEQ], ALU.mult, ALU.add)\
                    .then_inc(evac[t[0]], 1)
            mine(t)
            h3 = h[:, :].rearrange("p (m t) -> p m t", m=KT)[:, :, 0:SEQ]
            ht = h[:, :].rearrange("p (m t) -> p t m", m=KT)[:, 0:SEQ, :]
            zt = zg[:, :].rearrange("p (m t) -> p t m", m=KT)[:, 0:SEQ, :]

            def over_tiles(x):
                return x.rearrange("p (a t) -> p a t", a=1).to_broadcast([P, KT, SEQ])

            v.tensor_reduce(acc[:, 0:SEQ], ht, AX, ALU.add).then_inc(ln_in, 1)
            t = plan["mean"].at(0)
            v.tensor_scalar(var[:, 0:SEQ], filled(t)[:, 0:SEQ], 1.0 / D, None, ALU.mult).then_inc(evac[t[0]], 1)
            mine(t)
            v.tensor_tensor(h3, h3, over_tiles(var[:, 0:SEQ]), ALU.subtract).then_inc(centred, 1)
            dve.wait_ge(centred, 1)
            dve.wait_ge(ln_squared, 1)
            v.tensor_reduce(acc[:, 0:SEQ], zt, AX, ALU.add).then_inc(ln_in, 1)
            inverse_root(plan["lnvar"].at(0), SEQ, D, LN_EPS, var[:, 0:SEQ], std[:, 0:SEQ], rs[:, 0:SEQ])
            then(v.tensor_tensor(h3, h3, over_tiles(rs[:, 0:SEQ]), ALU.mult))
            for m in range(KT):
                v.tensor_scalar(tile(h, m, SEQ), tile(h, m, SEQ), W("ln1_g", m, m + 1), W("ln1_b", m, m + 1),
                                ALU.mult, ALU.add).then_inc(x2_ready, 1)

            def two(x):
                return x.rearrange("p (a n) -> p a n", a=2)

            def spread(col, n):
                return col.rearrange("p (a n) -> p a n", n=1).to_broadcast([P, 2, n])

            def first_max(x, n, top, tmp, one):
                then(v.tensor_reduce(top, two(x), AX, ALU.max))
                then(v.tensor_tensor(two(tmp), two(x), spread(top, n), ALU.is_equal))
                places = C("iota32", 0, n).rearrange("p (a n) -> p a n", a=1).to_broadcast([P, 2, n])
                then(v.scalar_tensor_tensor(two(tmp), two(tmp), -64.0, places, ALU.mult, ALU.add))
                then(v.tensor_reduce(r_["place"], two(tmp), AX, ALU.min))
                then(v.tensor_tensor(two(one), two(tmp), spread(r_["place"], n), ALU.is_equal))

            t = plan["route"].at(0)
            bank = filled(t)
            lg = r_["lg"]
            v.tensor_tensor(two(lg), bank[:, 0:128].rearrange("p (a n) -> p a n", a=2)[:, :, 0:36],
                            W("b_route").rearrange("p (a n) -> p a n", a=1).to_broadcast([P, 2, 36]), ALU.add)\
                .then_inc(evac[t[0]], 1)
            mine(t)
            did(v.tensor_copy(two(r_["gl"]), two(lg)[:, :, 0:4]))
            then(v.tensor_copy(two(r_["em"]), two(lg)[:, :, 4:36]))
            first_max(r_["gl"], 4, r_["gtop"], r_["gt"], r_["g1"])
            v.tensor_tensor(two(r_["ge"]), two(r_["gl"]), spread(r_["gtop"], 4), ALU.subtract).then_inc(route_in, 1)
            then(v.tensor_scalar(r_["g1"], r_["g1"], -NEG, NEG, ALU.mult, ALU.add))
            e3 = r_["em"].rearrange("p (a n) -> p a n", n=8)
            then(v.tensor_tensor(e3, e3, r_["g1"].rearrange("p (a n) -> p a n", n=1).to_broadcast([P, 8, 8]), ALU.add))
            first_max(r_["em"], 32, r_["top1"], r_["tmp"], r_["o1"])
            then(v.scalar_tensor_tensor(r_["em"], r_["o1"], 3 * NEG, r_["em"], ALU.mult, ALU.add))
            first_max(r_["em"], 32, r_["top2"], r_["tmp"], r_["o2"])
            v.tensor_tensor(m_r[:, 0:64], r_["o1"], r_["o2"], ALU.add).then_inc(m_ready, 1)
            v.tensor_tensor(r_["ev"], r_["top2"], r_["top1"], ALU.subtract).then_inc(route_in, 1)
            dve.wait_ge(route_exp, 1)
            then(v.tensor_reduce(r_["pg"], two(r_["ge"]), AX, ALU.add))
            then(v.reciprocal(r_["pg"], r_["pg"]))
            dve.wait_ge(route_exp, 2)
            then(v.tensor_scalar(r_["w1"], r_["ev"], 1.0, None, ALU.add))
            then(v.reciprocal(r_["w1"], r_["w1"]))
            then(v.tensor_tensor(r_["w1"], r_["w1"], r_["pg"], ALU.mult))
            then(v.tensor_tensor(r_["w2"], r_["w1"], r_["ev"], ALU.mult))
            t = plan["cnt"].at(0)
            v.tensor_copy(r_["cnt"], filled(t)[:, 0:32]).then_inc(evac[t[0]], 1)
            mine(t)
            then(v.tensor_scalar(r_["nb"], r_["cnt"], 0.0, None, ALU.is_gt))
            for j in range(1, SEQ // SLOTS):
                then(v.scalar_tensor_tensor(r_["nb"], r_["cnt"], float(SLOTS * j), r_["nb"], ALU.is_gt, ALU.add))
            then(v.tensor_tensor_scan(r_["end"], C("ones", 0, 32), r_["nb"], 0.0, ALU.mult, ALU.add))
            then(v.tensor_tensor(r_["beg"], r_["end"], r_["nb"], ALU.subtract))
            then(v.tensor_scalar(r_["beg"], r_["beg"], float(SLOTS), None, ALU.mult))
            cmp3 = r_["cmp"][0:1, :].rearrange("p (b e) -> p b e", e=32)
            then(v.tensor_tensor(cmp3, r_["end"][0:1, :].rearrange("p (a e) -> p a e", a=1).to_broadcast([1, MAXB, 32]),
                                 C("iotab", 0, MAXB, slice(0, 1)).rearrange("p (b a) -> p b a", a=1).to_broadcast([1, MAXB, 32]),
                                 ALU.is_le))
            then(v.tensor_reduce(r_["eb"][0:1, :], cmp3, AX, ALU.add))
            then(v.tensor_scalar(meta_i[0:1, 0:MAXB], r_["eb"][0:1, :], float(NE - 1), None, ALU.min))
            then(v.tensor_copy(meta_i[0:1, MAXB:MAXB + 1], r_["end"][0:1, 31:32]))
            t = plan["pos"].at(0)
            bank = filled(t)
            v.tensor_tensor(two(r_["em"]), two(bank[:, 0:64]),
                            r_["beg"].rearrange("p (a n) -> p a n", a=1).to_broadcast([P, 2, 32]), ALU.add)\
                .then_inc(evac[t[0]], 1)
            mine(t)
            for k, one in ((0, "o1"), (1, "o2")):
                then(v.tensor_tensor(r_["tmp"], r_["em"], r_[one], ALU.mult))
                then(v.tensor_reduce(r_["dest"][:, 2 * k:2 * k + 2], two(r_["tmp"]), AX, ALU.add))
            did(v.memset(m_zero, 0.0))
            did(v.memset(m_y, 0.0))
            v.memset(m_turn, 0.0).then_inc(table_ready, 1)

            def col(x, i):
                return r_[x][:, i:i + 1]

            def choose():
                for p in range(2):
                    e = v.tensor_scalar(m_t[:, p * 64:(p + 1) * 64], C("iota"), col("dest", p), None, ALU.is_equal)
                return e

            def choose_2():
                for p in range(2):
                    e = v.scalar_tensor_tensor(m_P[:, p * 64:(p + 1) * 64], C("iota"), col("dest", 2 + p),
                                               m_t[:, p * 64:(p + 1) * 64], ALU.is_equal, ALU.add)
                return e

            def weigh():
                for p in range(2):
                    v.tensor_scalar(m_t[:, 128 + p * 64:192 + p * 64], C("iota"), col("dest", p), col("w1", p),
                                    ALU.is_equal, ALU.mult)
                    e = v.tensor_scalar(m_t[:, 256 + p * 64:320 + p * 64], C("iota"), col("dest", 2 + p), col("w2", p),
                                        ALU.is_equal, ALU.mult)
                return e

            def weigh_2():
                for p in range(2):
                    a, b = (m_t[:, x + p * 64:x + 64 + p * 64].rearrange("p (a s) -> p a s", a=1).to_broadcast([P, 2, 64])
                            for x in (128, 256))
                    e = v.tensor_tensor(m_PW[:, p * P:(p + 1) * P].rearrange("p (a s) -> p a s", a=2), a, b, ALU.add)
                return e

            def move_on():
                return v.tensor_scalar(r_["dest"], r_["dest"], -float(SLOTS), None, ALU.add)

            choose().then_inc(parts_made, 1)
            dve.wait_ge(parts_made, 1)
            choose_2().then_inc(p_made, 1)
            weigh().then_inc(parts_made, 1)
            dve.wait_ge(parts_made, 2)
            weigh_2().then_inc(pw_made, 1)
            dve.wait_ge(pw_made, 1)
            move_on().then_inc(moved, 1)
            n_blocks = dve.value_load(meta_i[0:1, MAXB:MAXB + 1], min_val=1, max_val=MAXB)
            with dve.Fori(0, n_blocks) as b:
                dve.wait_ge(moved, b + 1)
                choose().then_inc(parts_made, 1)
                dve.wait_ge(parts_made, 2 * b + 3)
                dve.wait_ge(full[4], E_BASE[4] + b)
                choose_2().then_inc(p_made, 1)
                dve.wait_ge(silu_made, b + 1)
                v.tensor_tensor(m_h, ps[5][:, 256:512], m_sg, ALU.mult).then_inc(evac[5], 1)
                weigh().then_inc(parts_made, 1)
                dve.wait_ge(parts_made, 2 * b + 4)
                dve.wait_ge(pw_turned, b + 1)
                weigh_2().then_inc(pw_made, 1)
                dve.wait_ge(pw_made, b + 2)
                move_on().then_inc(moved, 1)
                dve.wait_ge(full[7], E_BASE[7] + b + 1)
                v.tensor_copy(m_y, ps[7][:, :]).then_inc(evac[7], 1)

            dve.wait_ge(y_done, 1)
            for p in range(2):
                for n in range(2):
                    o = m_o[:, p * D + n * 512:p * D + (n + 1) * 512]
                    did(v.scalar_tensor_tensor(o, m_x[:, p * D + n * 512:p * D + (n + 1) * 512], ALPHA,
                                               ps[2 * p + n][:, :], ALU.mult, ALU.add))
            own()
            then(v.tensor_reduce(small[:, 96:98], two(m_o), AX, ALU.add))
            then(v.tensor_scalar(small[:, 96:98], small[:, 96:98], -1.0 / D, None, ALU.mult))
            for p in range(2):
                o = m_o[:, p * D:(p + 1) * D]
                v.tensor_scalar(o, o, small[:, 96 + p:97 + p], None, ALU.add).then_inc(fin_centred, 1)
            dve.wait_ge(fin_squared, 2)
            v.tensor_scalar(small[:, 102:104], small[:, 100:102], 1.0 / D, LN_EPS, ALU.mult, ALU.add).then_inc(fin_var, 1)
            dve.wait_ge(fin_std, 1)
            then(v.reciprocal(small[:, 106:108], small[:, 104:106]))
            dve.wait_ge(ln2_in, 32)
            dve.wait_ge(fin_centred, 2)
            for p in range(2):
                o = m_o[:, p * D:(p + 1) * D]
                then(v.scalar_tensor_tensor(o, o, small[:, 106 + p:107 + p], m_g, ALU.mult, ALU.mult))
                v.tensor_tensor(o, o, m_b, ALU.add).then_inc(out_ready, 1)


def kernel(x, meta_tokens, norm_gains, w_ffn_in, w_ffn_out, gla_w_in, gla_w_gate, gla_b_gate, gla_norm, gla_w_out,
           kv_norm, w_kv, swa_w_q, swa_sinks, swa_w_out, w_in_2, b_in_2, lb_logits_2, hg_norm_g_2, rel_bias_2,
           w_proj_a_2, w_proj_b_2, w_out_2, ln1_g_2, ln1_b_2, w_group_2, b_group_2, w_expert_2, b_expert_2,
           w_gate_up_2, w_down_2, ln2_g_2, ln2_b_2):
    import concourse.bacc as bacc
    from concourse.bass_utils import run_bass_kernel_spmd

    f = np.float32
    a = {k: np.asarray(v) for k, v in locals().items() if k not in ("bacc", "run_bass_kernel_spmd", "f")}

    def by_feature(w):
        n = w.shape[1] // 256
        return w.reshape(KT, P, n, 2, P).transpose(2, 1, 3, 0, 4).reshape(n, P, UNIT)

    def by_token(w):
        n = w.shape[1] // 256
        return w.reshape(KT, P, n, 256).transpose(2, 1, 0, 3).reshape(n, P, UNIT)

    def short(w):
        return w.reshape(4, P, 2, 4, P).transpose(2, 1, 3, 0, 4).reshape(2, P, UNIT)

    def ffn_in(w):
        return by_feature(np.stack([w[:, :FF].reshape(D, FT, P), w[:, FF:].reshape(D, FT, P)], axis=2).reshape(D, 2 * FF))

    order = np.array([(t * 8 + half * 4 + i) * 64 + d for t in range(2) for i in range(4) for half in range(2)
                      for d in range(64)])
    g = a["gla_w_in"][0]
    w2 = a["w_in_2"][0]
    kv = a["w_kv"]
    fi = a["w_ffn_in"]
    cut = {"q": (0, 512), "z": (512, 1024), "i": (1024, 1536), "g": (1536, 2048), "mq": (2048, 2560),
           "mk": (2560, 3072), "mv": (3072, 3584), "ga": (3584, 4608), "gb": (4608, 5632)}
    sec = {k: w2[:, s:e] for k, (s, e) in cut.items()}
    w_units = np.concatenate([
        ffn_in(fi[0, 0]), by_feature(g[:, 2048:3072]), by_token(g[:, 1024:2048]), by_feature(g[:, 512:1024]),
        by_feature(g[:, 0:512]), by_feature(a["gla_w_out"][0]), ffn_in(fi[0, 1]), by_feature(kv[:, :256]),
        by_token(kv[:, 256:]), ffn_in(fi[1, 0]), by_feature(a["swa_w_q"][0][:, order]),
        by_feature(a["swa_w_out"][0][order]), ffn_in(fi[1, 1]),
        by_feature(sec["z"]), by_feature(sec["q"]), by_feature(sec["ga"]), by_feature(sec["gb"]), by_feature(sec["g"]),
        by_feature(sec["mq"]), by_feature(sec["mk"]), by_token(sec["i"]), by_token(sec["mv"]),
        short(a["w_proj_a_2"][0]), short(a["w_proj_b_2"][0]), by_feature(a["w_out_2"][0])])
    w_out_units = a["w_ffn_out"].reshape(4, FT, P, KT, P).transpose(0, 3, 2, 1, 4).reshape(4 * KT, P, OUT_UNIT)
    tokens = np.concatenate([a["x"][0], a["meta_tokens"]])
    xT = tokens.reshape(TA, KT, P).transpose(2, 1, 0).reshape(P, KT * TA)

    def cols(vec):
        return vec.reshape(-1, P).T

    table, levels = constants()
    par = {k: np.zeros((P, n), f) for k, (_, n) in P_COLS.items()}
    par["gains"][:] = cols(a["norm_gains"].reshape(-1))
    par["kv_norm"][:] = cols(a["kv_norm"])
    par["b_gate"][:] = cols(a["gla_b_gate"][0])
    par["gla_norm"][:] = cols(a["gla_norm"][0])
    par["w_lr"][:] = g[:, 3072:].reshape(KT, P, RANK).transpose(1, 0, 2).reshape(P, -1)
    par["w_gate"][:RANK] = a["gla_w_gate"][0]
    par["b_in"][:] = cols(a["b_in_2"][0])
    par["lb_logits"][:] = cols(a["lb_logits_2"].reshape(-1))
    par["hg_norm"][:] = cols(a["hg_norm_g_2"][0])
    par["ln1_g"][:] = cols(a["ln1_g_2"][0])
    par["ln1_b"][:] = cols(a["ln1_b_2"][0])
    wr = np.concatenate([a["w_group_2"][0], a["w_expert_2"][0]], axis=1)
    par["w_route"][:] = wr.reshape(KT, P, 36).transpose(1, 0, 2).reshape(P, -1)
    par["b_route"][:] = np.concatenate([a["b_group_2"][0], a["b_expert_2"][0]])[None]
    par["rel_bias"][:32] = a["rel_bias_2"]
    heads = [t * 8 + half * 4 + i for t in range(2) for i in range(4) for _ in range(2) for half in range(2)]
    par["sinks"][:] = a["swa_sinks"][0][heads][None]
    params = np.concatenate([par[k] for k in P_COLS], axis=1)
    b2 = a["b_in_2"][0]
    rows = np.ascontiguousarray(np.broadcast_to(
        np.concatenate([b2[1024:1536], b2[3072:3584], a["ln2_g_2"][0], a["ln2_b_2"][0]]), (P, 3072)))

    nc = bacc.Bacc("TRN2", target_bir_lowering=False, num_devices=1)
    arrays = {"xT": xT, "w_units": w_units, "w_out_units": w_out_units, "w_gate_up": a["w_gate_up_2"][0],
              "w_down": a["w_down_2"][0], "table": table, "levels": levels, "params": params, "rows": rows}
    arrays = {k: np.ascontiguousarray(v) for k, v in arrays.items()}
    aps = [nc.dram_tensor(k, v.shape, mybir.dt.from_np(v.dtype), kind="ExternalInput").ap() for k, v in arrays.items()]
    out = nc.dram_tensor("out", (1, SEQ, D), F32, kind="ExternalOutput").ap()
    two_blocks(nc, *aps, out)
    r = run_bass_kernel_spmd(nc, [arrays], core_ids=[0])
    return r.results[0]["out"]
```

```python
from contextlib import ExitStack

import numpy as np

import concourse.bass as bass
from concourse import mybir

F32 = mybir.dt.float32
F32R = mybir.dt.float32r
I32 = mybir.dt.int32
U32 = mybir.dt.uint32
ALU = mybir.AluOpType
ACT = mybir.ActivationFunctionType
AX = mybir.AxisListType.X

P = 128
D = 1024
KT = D // P
SEQ = 256
META = 16
TA = SEQ + META
FF = 2816
FT = FF // P
EPS = 1e-6
LN_EPS = 1e-5
GH, GDK, GDV, CH = 4, 128, 256, 64
RANK = 16
NEG = -1e30
ALPHA = float(2.0 ** 0.25)
NE, EH = 32, 512
ARENA = 19008
SLOTS = 64
MAXB = NE + 2 * SEQ // SLOTS
RAW = 2
PARTS = 4
UNIT = 2 * KT * P
OUT_UNIT = FT * P
HALF = OUT_UNIT // 2
EXP_UNITS = 6

C_COLS = {}
for _name, _n in (("ident", P), ("ones", P), ("rot", P), ("pairmask", P), ("upper", P), ("iota", SLOTS),
                  ("iota32", 32), ("iotab", MAXB), ("reset_g", TA), ("reset_h", SEQ), ("cos", TA), ("sin", TA),
                  ("swa0", P + META), ("swa1", SEQ + META), ("ninf", SEQ), ("onehot", 384)):
    C_COLS[_name] = (sum(n for _, n in C_COLS.values()), _n)
NC_COLS = sum(n for _, n in C_COLS.values())
LEVELS = [64, 32, 16, 8, 4, 2, 1, 0]

P_COLS = {}
for _name, _n in (("gains", 96), ("kv_norm", KT), ("b_gate", GH), ("gla_norm", 2), ("w_lr", KT * RANK),
                  ("w_gate", GH * GDK), ("b_in", 44), ("lb_logits", 8), ("hg_norm", 4), ("ln1_g", KT), ("ln1_b", KT),
                  ("w_route", KT * 36), ("b_route", 36), ("rel_bias", 8), ("sinks", 32)):
    P_COLS[_name] = (sum(n for _, n in P_COLS.values()), _n)
NP_COLS = sum(n for _, n in P_COLS.values())


def constants():
    c = {k: np.zeros((P, n), np.float32) for k, (_, n) in C_COLS.items()}
    i = np.arange(P)
    c["ident"][i, i] = 1
    c["ones"][:] = 1
    d = i % 64
    part = np.where(d < 8, i + 8, i - 8)
    m = i[d < 16]
    c["rot"][part[m], m] = 1
    s, t = i[:, None], i[None, :]
    c["pairmask"][:] = (s // CH == t // CH) & (s <= t)
    c["upper"][:] = s < t
    c["iota"][:] = np.arange(SLOTS)
    c["iota32"][:] = np.arange(32)
    c["iotab"][:] = np.arange(MAXB)
    col = np.arange(TA)
    c["reset_g"][:] = col % CH != 0
    c["reset_h"][:] = np.arange(SEQ) % P != 0
    inv = np.float32(500000.0) ** (-np.arange(0, 16, 2, dtype=np.float32) / np.float32(16))
    pos = np.where(col < SEQ, col + META, col - SEQ).astype(np.float32)
    ang = pos[None, :] * inv[d % 8][:, None]
    c["cos"][:] = np.where((d < 16)[:, None], np.cos(ang), 1)
    c["sin"][:] = np.where((d < 8)[:, None], -np.sin(ang), np.where((d < 16)[:, None], np.sin(ang), 0))
    own = np.where(t <= s, 0, NEG)
    c["swa0"][:, :P] = own
    c["swa1"][:, :P] = np.where(t > s, 0, NEG)
    c["swa1"][:, P:2 * P] = own
    c["ninf"][:, :] = np.where(np.arange(SEQ)[None, :] <= P + s, 0, NEG)
    dist = 255 - np.arange(384)
    dd = np.maximum(dist, 1).astype(np.float32)
    log_part = 16 + (np.log(dd / np.float32(16)) / np.float32(np.log(8.0)) * np.float32(16)).astype(np.int32)
    bucket = np.where(dist < 16, dist, np.minimum(log_part, 31))
    c["onehot"][:32] = (bucket[None, :] == np.arange(32)[:, None]) & (dist >= 0)[None, :]
    table = np.concatenate([c[k] for k in C_COLS], axis=1)
    levels = np.zeros((P, len(LEVELS), P), np.float32)
    for n, h in enumerate(LEVELS):
        if h:
            levels[:, n] = (s // (2 * h) == t // (2 * h)) & (s % (2 * h) < h) & (t % (2 * h) >= h)
        else:
            levels[:, n] = s == t
    return table, levels.reshape(P, -1)


class Stream:

    def __init__(self):
        self.n = 0

    def take(self, n):
        first, self.n = self.n, self.n + n
        return first


class Tiles:

    def __init__(self, uses, banks, n):
        self.banks, self.base = banks, {b: uses[b] for b in banks}
        for i in range(n):
            uses[banks[i % len(banks)]] += 1

    def at(self, i, it=0, body=0):
        b = self.banks[i % len(self.banks)]
        return b, self.base[b] + i // len(self.banks) + it * (body // len(self.banks))


def two_blocks(nc, xT, w_units, w_out_units, w_gate_up, w_down, table, levels, params, rows, out):
    ctx = ExitStack()
    with ctx:
        def sb(name, shape, dt=F32):
            return ctx.enter_context(nc.sbuf_tensor(name, shape, dt))

        def sem(name):
            return ctx.enter_context(nc.semaphore(name))

        h = sb("h", [P, KT * TA])
        x_hi = sb("x_hi", [P, KT * TA], F32R)
        x_lo = sb("x_lo", [P, KT * TA], F32R)
        zg = sb("zg", [P, KT * TA])
        sq = sb("sq", [P, 2, TA])
        acc = sb("acc", [P, TA])
        var = sb("var", [P, TA])
        std = sb("std", [P, TA])
        rs = sb("rs", [P, TA])
        kT = sb("kT", [P, 2, TA])
        vs = sb("vs", [P, 3, 256])
        small = sb("small", [P, 320])
        cst = sb("cst", [P, NC_COLS])
        par = sb("par", [P, NP_COLS])
        halfg = sb("halfg", [P, 96])
        sg = sb("sg", [P, 2 * TA])
        hw = sb("hw", [P, 2 * TA])
        before_moe = ExitStack()
        with before_moe as early:
            def eb(name, shape, dt=F32):
                return early.enter_context(nc.sbuf_tensor(name, shape, dt))

            raw = eb("raw", [P, RAW * OUT_UNIT])
            w_hi = eb("w_hi", [P, PARTS * HALF], F32R)
            w_lo = eb("w_lo", [P, PARTS * HALF], F32R)
            with ExitStack() as ffn_only:
                hid_hi = ffn_only.enter_context(nc.sbuf_tensor("hid_hi", [P, FT * TA], F32R))
                hid_lo = ffn_only.enter_context(nc.sbuf_tensor("hid_lo", [P, FT * TA], F32R))
            arena = eb("arena", [P, ARENA])
        ring = sb("ring", [P, 2 * EXP_UNITS * UNIT])
        moe = sb("moe", [P, RAW * OUT_UNIT + 2 * PARTS * HALF + ARENA - 2 * EXP_UNITS * UNIT])
        meta_i = sb("meta_i", [1, MAXB + 8], I32)
        ps = [ctx.enter_context(nc.psum_tensor(f"ps{b}", [P, 512], F32)) for b in range(8)]
        bias_rows = nc.dram_tensor("bias_rows", [8, P * 384], F32, kind="Internal").ap()

        def C(name, a=0, b=None, parts=slice(0, P)):
            at, n = C_COLS[name]
            return cst[parts, at + a:at + (n if b is None else b)]

        def W(name, a=0, b=None, parts=slice(0, P)):
            at, n = P_COLS[name]
            return par[parts, at + a:at + (n if b is None else b)]

        def gain(g, m, table=par):
            at = P_COLS["gains"][0] if table is par else 0
            return table[:, at + g * KT + m:at + g * KT + m + 1]

        place = [0]

        def room(n):
            at = place[0]
            place[0] += n
            assert place[0] <= ARENA, place[0]
            return arena[:, at:at + n]

        def tile(buf, m, t, w=TA):
            return buf[:, m * w:m * w + t]

        s_kraw = arena[:, 2 * FT * TA:2 * FT * TA + 2 * TA]
        s_krot = arena[:, 2 * FT * TA + 2 * TA:2 * FT * TA + 4 * TA]
        g_v = room(2 * D)
        g_vm = room(D)
        g_r = zg
        g_b = room(GH * TA)
        g_att = g_b
        g_sq = room(2 * GH * TA)
        g_e1, g_e2 = g_sq[:, 0:GH * TA], g_sq[:, GH * TA:2 * GH * TA]
        g_o = room(KT * TA)
        g_e0, g_k = g_o[:, 0:GH * TA], g_o[:, GH * TA:2 * GH * TA]
        g_kw, g_q = room(GH * TA), room(GH * TA)
        g_kwT = room(GH * 384)
        g_s = room(GH * 4 * GDV)
        g_dec = room(GH * 4)
        g_lr = room(TA)
        place[0] = 0
        s_q = room(KT * SEQ)
        s_t = room(2 * SEQ)
        s_o = room(KT * SEQ)
        a_p = room(2 * 4 * TA)
        a_pT = room(2 * 4 * 384)
        place[0] = 0
        b_sga, b_sgb = zg, room(KT * SEQ)
        b_sg = room(4 * SEQ)
        b_p = room(8 * SEQ)
        b_kf, b_q = b_p[:, 0:4 * SEQ], b_p[:, 4 * SEQ:8 * SEQ]
        b_b, b_e, b_qk = (room(4 * SEQ) for _ in range(3))
        b_bo, b_sq = b_b, b_qk
        b_v, b_mv = room(2 * 512), room(2 * 512)
        b_mq, b_mk = room(4 * SEQ), room(4 * SEQ)
        b_bias = room(8 * SEQ)
        b_att = room(3 * 512)
        b_a = room(4 * SEQ)
        b_lv = room(len(LEVELS) * P)
        b_rows = room(2 * 512)
        b_pT = arena[:, place[0] - 2 * 1024:place[0] - 2 * 1024 + 4 * 384]
        place[0] = 0
        def moe_room(n):
            at = place[0]
            place[0] += n
            assert place[0] <= moe.shape[1], place[0]
            return moe[:, at:at + n]

        m_x = moe_room(2 * D)
        m_g, m_b = moe_room(D), moe_room(D)
        m_r = moe_room(2200)
        r_, at_ = {}, 64
        for name, n in (("lg", 72), ("gl", 8), ("gt", 8), ("g1", 8), ("ge", 8), ("em", 64), ("tmp", 64), ("o1", 64),
                        ("o2", 64), ("gtop", 2), ("top1", 2), ("top2", 2), ("place", 2), ("ev", 2), ("pg", 2),
                        ("w1", 2), ("w2", 2), ("dest", 4), ("cnt", 32), ("nb", 32), ("end", 32), ("beg", 32),
                        ("eb", MAXB), ("cmp", MAXB * 32)):
            r_[name] = m_r[:, at_:at_ + n]
            at_ += n
        assert at_ <= 2200, at_
        m_P = moe_room(2 * 64)
        m_PW = moe_room(2 * P)
        m_PP = moe_room(2 * P)
        m_w = moe_room(4)
        m_t = moe_room(6 * 64)
        m_zero = moe_room(P)
        m_xT = moe_room(512)
        m_h = moe_room(256)
        m_sg = moe_room(256)
        m_turn = moe_room(256)
        m_hT = m_turn
        m_y, m_pT = (x_hi[:, 0:512], x_lo[:, 0:512]), x_hi[:, 512:512 + 2 * P]
        m_o = moe_room(2 * D)
        b_br = arena[:, 2 * FT * TA:2 * FT * TA + 8 * 384]

        consts_in, params_in, x_in, levels_in, rows_in, ln2_in = (
            sem(n) for n in ("consts_in", "params_in", "x_in", "levels_in", "rows_in", "ln2_in"))
        bias_out, bias_in, out_stored = sem("bias_out"), sem("bias_in"), sem("out_stored")
        full = [sem(f"full{b}") for b in range(8)]
        evac = [sem(f"evac{b}") for b in range(8)]
        landed = [sem(f"landed{s}") for s in range(RAW)]
        hi_made, lo_made, hw_made = sem("hi_made"), sem("lo_made"), sem("hw_made")
        e_landed = [sem(f"e_landed{s}") for s in range(2 * EXP_UNITS)]
        half_begun = sem("half_begun")
        exp_begun = sem("exp_begun")
        ht_made, w_taken, yhi_made = sem("ht_made"), sem("w_taken"), sem("yhi_made")
        sq_made, sq_used, std_made = sem("sq_made"), sem("sq_used"), sem("std_made")
        squared, sums_made = sem("squared"), sem("sums_made")
        xhi_made, scaled = sem("xhi_made"), sem("scaled")
        gate_silu, hid_made = sem("gate_silu"), sem("hid_made")
        x_ready, h_ready = sem("x_ready"), sem("h_ready")
        act_chain, dve_chain = sem("act_chain"), sem("dve_chain")
        soft_made, decay_in, decay_made = (sem(n) for n in ("soft_made", "decay_in", "decay_made"))
        q_roped, neg_max, exp_made, p_ready = (sem(n) for n in ("q_roped", "neg_max", "exp_made", "p_ready"))
        lb_in, lb_exp = sem("lb_in"), sem("lb_exp")
        hg_arg, hg_ln, lvl_in, lvl_exp, lvl_ready = (
            sem(n) for n in ("hg_arg", "hg_ln", "lvl_in", "lvl_exp", "lvl_ready"))
        ln_in, centred, ln_squared, x2_ready = (sem(n) for n in ("ln_in", "centred", "ln_squared", "x2_ready"))
        route_in, route_exp, m_ready, table_ready = (
            sem(n) for n in ("route_in", "route_exp", "m_ready", "table_ready"))
        p_made, pw_made, pw_turned, parts_made, moved = (
            sem(n) for n in ("p_made", "pw_made", "pw_turned", "parts_made", "moved"))
        y_zeroed, silu_made, y_done = (sem(n) for n in ("y_zeroed", "silu_made", "y_done"))
        fin_centred, fin_squared, fin_var, fin_std, out_ready = (
            sem(n) for n in ("fin_centred", "fin_squared", "fin_var", "fin_std", "out_ready"))

        units, uses = Stream(), [0] * 8
        MAIN = [0, 1, 2, 3]
        plan = {}

        def ffn_plan(n):
            plan[f"in{n}"] = (units.take(FT), Tiles(uses, MAIN, 2 * FT))
            plan[f"out{n}"] = (units.take(KT), Tiles(uses, MAIN, KT))

        def tiles(name, banks, n):
            plan[name] = Tiles(uses, banks, n)

        tiles("stat0", [7], 1)
        tiles("bias", [4, 5, 6], 8)
        ffn_plan(0)
        tiles("stat1", [7], 1)
        tiles("stat2", [7], 1)
        tiles("lr", [4], 1)
        plan["r"] = (units.take(4), Tiles(uses, MAIN, 8))
        tiles("gate", [4, 5, 6, 7], 4)
        plan["v"] = (units.take(4), Tiles(uses, MAIN, 12))
        plan["k"] = (units.take(2), Tiles(uses, MAIN, 4))
        plan["q"] = (units.take(2), Tiles(uses, MAIN, 4))
        tiles("att", [0, 1, 2, 3], 4)
        tiles("kwT", [4, 5, 6, 7], 4)
        tiles("kv", list(range(8)), 12)
        tiles("o", list(range(8)), 8)
        tiles("gst", MAIN, 4)
        plan["gout"] = (units.take(4), Tiles(uses, MAIN, 8))
        tiles("stat3", [7], 1)
        tiles("stat4", [7], 1)
        ffn_plan(1)
        tiles("stat5", [7], 1)
        tiles("stat6", [7], 1)
        plan["ks"] = (units.take(1), Tiles(uses, MAIN, 2))
        tiles("krot", [4, 5], 2)
        plan["vs"] = (units.take(1), Tiles(uses, MAIN, 3))
        ffn_plan(2)
        tiles("stat7", [7], 1)
        tiles("stat8", [7], 1)
        plan["sq"] = (units.take(4), Tiles(uses, MAIN, 8))
        tiles("qrot", [4, 5], 8)
        tiles("ss", MAIN, 32)
        tiles("sT", [4, 5, 6], 32)
        tiles("sv", [7], 8)
        plan["sout"] = (units.take(4), Tiles(uses, MAIN, 8))
        tiles("stat9", [7], 1)
        tiles("stat10", [7], 1)
        ffn_plan(3)
        tiles("stat11", [7], 1)
        SECTIONS = ["z", "hq", "ga", "gb", "hgate", "mq", "mk", "hi", "mv"]
        for name in SECTIONS:
            n_units = 4 if name in ("ga", "gb") else 2
            plan[name] = (units.take(n_units), Tiles(uses, MAIN, 2 * n_units))
        tiles("lvl", [4, 5, 6, 7], 16)
        tiles("cross", [4], 1)
        tiles("ho", [0, 1, 2, 3], 4)
        tiles("hst", [4, 5, 6, 7], 4)
        tiles("bs", MAIN, 16)
        tiles("bT", [4, 5, 6], 16)
        tiles("bv", [7], 4)
        plan["pa"] = (units.take(2), Tiles(uses, MAIN, 8))
        plan["pb"] = (units.take(2), Tiles(uses, MAIN, 8))
        plan["wo"] = (units.take(4), Tiles(uses, MAIN, 8))
        tiles("mean", [7], 1)
        tiles("lnvar", [7], 1)
        tiles("xtok", [0, 1, 2, 3], 4)
        tiles("route", [4], 1)
        tiles("pos", [5], 1)
        tiles("cnt", [6], 1)
        N_UNITS = units.n
        tiles("e_gather", [4], 1)
        E_BASE = {b: uses[b] for b in range(4, 8)}


        block = ctx.enter_context(nc.Block())

        runs = []
        u, row, orow = 0, 0, 0
        for key, val in plan.items():
            if not isinstance(val, tuple):
                continue
            n = {"out": KT, "in": FT}.get(key.rstrip("0123"), None)
            first = val[0]
            nxt = min([v[0] for v in plan.values() if isinstance(v, tuple) and v[0] > first] + [N_UNITS])
            n = nxt - first
            if key.startswith("out"):
                runs.append((1, orow, first, n))
                orow += n
            elif runs and runs[-1][0] == 0 and runs[-1][2] + runs[-1][3] == first:
                runs[-1] = (0, runs[-1][1], runs[-1][2], runs[-1][3] + n)
                row += n
            else:
                runs.append((0, row, first, n))
                row += n

        is_out = [False] * N_UNITS
        for kind, _, first, n in runs:
            for u in range(first, first + n):
                is_out[u] = bool(kind)

        def half_size(u):
            return HALF if is_out[u] else UNIT // 2

        def raw_slot(u, a, n):
            return raw[:, (u % RAW) * OUT_UNIT + a:(u % RAW) * OUT_UNIT + a + n]

        def part(w, c, a, n):
            return w[:, (c % PARTS) * HALF + a:(c % PARTS) * HALF + a + n]

        @block.sync
        def _(sp):
            sp.dma_start(h[:, :], xT).then_inc(x_in, 16)
            sp.dma_start(par[:, :], params).then_inc(params_in, 16)

            def load(kind, row, u, it=0):
                n = OUT_UNIT if kind else UNIT
                src = (w_out_units if kind else w_units)[bass.ds(row + RAW * it, 1), :, :]
                if not isinstance(it, int) or u >= RAW:
                    sp.wait_ge(lo_made, 2 * (u - RAW) + 2 + 2 * RAW * it)
                sp.dma_start(raw_slot(u, 0, n), src.rearrange("a p n -> (a p) n")).then_inc(landed[u % RAW], 16)

            for kind, row, first, n in runs:
                head = RAW if first == 0 else 0
                for j in range(head):
                    load(kind, row + j, first + j)
                if head:
                    sp.dma_start(cst[:, :], table).then_inc(consts_in, 16)
                row, first, n = row + head, first + head, n - head
                with sp.Fori(0, n // RAW) as it:
                    for j in range(RAW):
                        load(kind, row + j, first + j, it)
                for j in range(n // RAW * RAW, n):
                    load(kind, row + j, first + j)

            def load_expert(e, slot, wait=None):
                for i in range(EXP_UNITS):
                    if wait is not None:
                        sp.wait_ge(exp_begun, wait + i)
                    if i < 4:
                        src = w_gate_up[bass.ds(e, 1), 2 * P * i:2 * P * (i + 1), :]
                    else:
                        src = w_down[bass.ds(e, 1), 2 * P * (i - 4):2 * P * (i - 3), :]
                    at = slot * EXP_UNITS + i
                    sp.dma_start(ring[:, at * UNIT:(at + 1) * UNIT].rearrange("p (k n) -> p k n", k=2),
                                 src.rearrange("a (k p) n -> p (a k) n", p=P)).then_inc(e_landed[at], 16)

            t = plan["wo"][1].at(7)
            sp.wait_ge(full[t[0]], t[1] + 1)
            load_expert(0, 0)
            load_expert(1, 1)
            sp.wait_ge(table_ready, 1)
            n_pairs = sp.value_load(meta_i[0:1, MAXB:MAXB + 1], min_val=4, max_val=MAXB // 2)
            with sp.Fori(1, n_pairs) as pair:
                for j in range(2):
                    e = sp.value_load(meta_i[0:1, bass.ds(2 * pair + j, 1)], min_val=0, max_val=NE - 1)
                    load_expert(e, j, 2 * EXP_UNITS * pair + EXP_UNITS * (j - 2) + 2)

        @block.gpsimd
        def _(pool):
            for i in (5, 6, 7):
                pool.wait_ge(evac[plan["bias"].at(i)[0]], plan["bias"].at(i)[1] + 1)
            for i in range(8):
                pool.dma_start(bias_rows[i, :].rearrange("(p n) -> p n", p=P),
                               b_br[:, i * 384:(i + 1) * 384]).then_inc(bias_out, 16)
            pool.wait_ge(bias_out, 8 * 16)
            t = plan["stat11"].at(0)
            pool.wait_ge(full[t[0]], t[1] + 1)
            for i in range(8):
                src = bias_rows[i, 127:127 + P * 383].rearrange("(p n) -> p n", p=P)[:, 0:SEQ]
                pool.dma_start(b_bias[:, i * SEQ:(i + 1) * SEQ], src).then_inc(bias_in, 16)
            pool.dma_start(b_lv, levels).then_inc(levels_in, 16)
            pool.dma_start(b_rows, rows[:, 0:1024]).then_inc(rows_in, 16)
            t = plan["lnvar"].at(0)
            pool.wait_ge(full[t[0]], t[1] + 1)
            pool.dma_start(m_g, rows[:, 1024:2048]).then_inc(ln2_in, 16)
            pool.dma_start(m_b, rows[:, 2048:3072]).then_inc(ln2_in, 16)

        @block.tensor
        def _(pe):
            def mm(out_ap, lhsT, rhs, start, stop):
                return nc.tensor.matmul(out_ap, lhsT, rhs, start=start, stop=stop, skip_group_check=True)

            def turn(out_ap, in_ap):
                k = in_ap.shape[0]
                return nc.tensor.transpose(out_ap, in_ap, C("ident", 0, k, slice(0, k)))

            def free(t):
                if not isinstance(t[1], int) or t[1] > 0:
                    pe.wait_ge(evac[t[0]], t[1])
                return ps[t[0]]

            def taken(t):
                pe.wait_ge(evac[t[0]], t[1] + 1)

            def arrive(u, j, it=0):
                c = 2 * u + j
                pe.wait_ge(lo_made, c + 1 + 2 * RAW * it)
                return c

            def three(out_ap, hi, lo, moving_hi, moving_lo, start, stop):
                first = mm(out_ap, hi, moving_hi, start, False)
                mm(out_ap, hi, moving_lo, False, False)
                return first, mm(out_ap, lo, moving_hi, False, stop)

            def project(u, T, i, src, w, it=0, body=0, kt=KT, n_tiles=2, at=0, x_base=None):
                for j in range(n_tiles):
                    t = T.at(i + j, it, body)
                    if j % (n_tiles // 2) == 0:
                        c = arrive(u, j // (n_tiles // 2), it)
                    bank = free(t)
                    for k in range(kt):
                        a = (j % (n_tiles // 2) * kt + k) * P
                        x = slice((at + k) * TA, (at + k) * TA + w)
                        if x_base is not None and j == 0:
                            pe.wait_ge(x_ready, x_base + k + 1)
                        first, m = three(bank[:, 0:w], part(w_hi, c, a, P), part(w_lo, c, a, P),
                                         src[0][:, x], src[1][:, x], k == 0, k == kt - 1)
                        if j % (n_tiles // 2) == 0 and k == 0:
                            first.then_inc(half_begun, 1)
                    m.then_inc(full[t[0]], 1)

            def project_tokens(u, T, i, src, spans):
                for j, (a, n) in enumerate(spans):
                    t = T.at(i + j)
                    bank = free(t)
                    for k in range(KT):
                        if k % 4 == 0:
                            c = arrive(u, k // 4)
                        x = slice(k * TA + a, k * TA + a + n)
                        first, m = three(bank[0:n, 0:256], src[0][:, x], src[1][:, x],
                                         part(w_hi, c, k % 4 * 256, 256), part(w_lo, c, k % 4 * 256, 256),
                                         k == 0, k == KT - 1)
                        if (j, k) in ((0, 0), (len(spans) - 1, 4)):
                            first.then_inc(half_begun, 1)
                    m.then_inc(full[t[0]], 1)

            def stat(n, w, columns=False):
                t = plan[f"stat{n}"].at(0)
                if n % 2:
                    pe.wait_ge(sq_used, 8 * (n // 2 + 1))
                else:
                    pe.wait_ge(sums_made, n // 2 + 1)
                bank = free(t)
                m = mm(bank[:, 0:w], C("ones"), acc[:, 0:w], True, True)
                if columns:
                    for s, (a, size) in enumerate(((0, P), (P, P), (SEQ, META))):
                        m = mm(bank[0:size, 300 + s:301 + s], acc[:, a:a + size], C("ones", 0, 1), True, True)
                m.then_inc(full[t[0]], 1)

            X, HID = (x_hi, x_lo), (hid_hi, hid_lo)

            def ffn(n, x_base, w, between=None):
                u0, T = plan[f"in{n}"]
                project(u0, T, 0, X, w, x_base=x_base)
                if between is not None:
                    between()
                project(u0 + 1, T, 2, X, w)
                with pe.Fori(1, FT // RAW) as it:
                    for j in range(RAW):
                        project(u0 + j, T, 2 * j, X, w, it, 2 * RAW)
                u1, T = plan[f"out{n}"]
                with pe.Fori(0, KT // 4) as it2:
                    for j in range(4):
                        t = T.at(j, it2, 4)
                        bank = free(t)
                        if j == 0:
                            pe.wait_ge(hid_made, FT * (n + 1) - 1)
                        for k in range(FT):
                            if j == 0 and k == FT - 1:
                                pe.wait_ge(hid_made, FT * (n + 1))
                            if k % (FT // 2) == 0:
                                c = arrive(u1 + j, k // (FT // 2), 2 * it2)
                            a = k % (FT // 2) * P
                            x = slice(k * TA, k * TA + w)
                            first, m = three(bank[:, 0:w], part(w_hi, c, a, P), part(w_lo, c, a, P),
                                             hid_hi[:, x], hid_lo[:, x], k == 0, k == FT - 1)
                            if k % (FT // 2) == 0:
                                first.then_inc(half_begun, 1)
                        m.then_inc(full[t[0]], 1)

            def first_stat():
                pe.wait_ge(consts_in, 16)
                pe.wait_ge(params_in, 16)
                stat(0, TA)
                for i in range(8):
                    t = plan["bias"].at(i)
                    bank = free(t)
                    mm(bank[:, 0:384], W("rel_bias", i, i + 1, slice(0, 32)).to_broadcast([32, P]),
                       C("onehot", 0, 384, slice(0, 32)), True, True).then_inc(full[t[0]], 1)

            ffn(0, 0, TA, first_stat)
            stat(1, TA)

            u0, T = plan["r"]
            project(u0, T, 0, X, TA, x_base=8)
            stat(2, TA, True)
            t = plan["lr"].at(0)
            bank = free(t)
            for k in range(KT):
                m = mm(bank[0:RANK, 0:TA], W("w_lr", k * RANK, (k + 1) * RANK), h[:, k * TA:(k + 1) * TA],
                       k == 0, k == KT - 1)
            m.then_inc(full[t[0]], 1)
            project(u0 + 1, T, 2, X, TA)
            taken(plan["lr"].at(0))
            for i in range(GH):
                t = plan["gate"].at(i)
                bank = free(t)
                mm(bank[:, 0:TA], W("w_gate", i * GDK, (i + 1) * GDK, slice(0, RANK)), g_lr[0:RANK, :],
                   True, True).then_inc(full[t[0]], 1)
            for j in (2, 3):
                project(u0 + j, T, 2 * j, X, TA)
            u0, T = plan["v"]
            for j in range(4):
                project_tokens(u0 + j, T, 3 * j, X, ((0, P), (P, P), (SEQ, META)))
            for name in ("k", "q"):
                u0, T = plan[name]
                for j in range(2):
                    project(u0 + j, T, 2 * j, X, TA)
            for i in range(GH):
                t = plan["att"].at(i)
                bank = free(t)
                taken(plan["q"][1].at(i))
                for a, n in ((0, P), (P, P), (SEQ, META)):
                    m = mm(bank[0:n, a:a + n], g_k[:, i * TA + a:i * TA + a + n], g_q[:, i * TA + a:i * TA + a + n],
                           True, True)
                m.then_inc(full[t[0]], 1)
            for i in range(GH):
                t = plan["kwT"].at(i)
                bank = free(t)
                turn(bank[:, 0:P], g_kw[:, i * TA:i * TA + P])
                turn(bank[:, P:2 * P], g_kw[:, i * TA + P:i * TA + 2 * P])
                turn(bank[0:META, 256:384], g_kw[:, i * TA + SEQ:(i + 1) * TA]).then_inc(full[t[0]], 1)
            for i in range(GH):
                taken(plan["kwT"].at(i))
                T = plan["kv"]
                kw = g_kwT[:, i * 384:(i + 1) * 384]
                v0, v1 = (g_v[:, t * D + i * GDV:t * D + (i + 1) * GDV] for t in (0, 1))
                bank = free(T.at(3 * i))
                mm(bank[:, 0:256], kw[0:META, 256:384], g_vm[0:META, i * GDV:(i + 1) * GDV], True, True)
                mm(bank[:, 256:512], kw[0:64, 0:128], v0[0:64, :], True, True).then_inc(full[T.at(3 * i)[0]], 1)
                bank = free(T.at(3 * i + 1))
                mm(bank[:, 0:256], kw[64:128, 0:128], v0[64:128, :], True, True).then_inc(full[T.at(3 * i + 1)[0]], 1)
                bank = free(T.at(3 * i + 2))
                mm(bank[:, 0:256], kw[0:64, 128:256], v1[0:64, :], True, True).then_inc(full[T.at(3 * i + 2)[0]], 1)
            for i in range(GH):
                taken(plan["att"].at(i))
                taken(plan["kv"].at(3 * i + 2))
                for half in range(2):
                    t = plan["o"].at(2 * i + half)
                    bank = free(t)
                    c0 = i * GDV + half * P
                    mm(bank[:, 0:P], g_v[:, c0:c0 + P], g_att[:, i * TA:i * TA + P], True, False)
                    mm(bank[:, P:2 * P], g_v[:, D + c0:D + c0 + P], g_att[:, i * TA + P:i * TA + 2 * P], False, False)
                    mm(bank[:, SEQ:TA], g_vm[0:META, c0:c0 + P], g_att[0:META, i * TA + SEQ:(i + 1) * TA], False, False)
                    for c in range(4):
                        st = g_s[:, (i * 4 + c) * GDV + half * P:(i * 4 + c) * GDV + (half + 1) * P]
                        m = mm(bank[:, c * CH:(c + 1) * CH], st, g_q[:, i * TA + c * CH:i * TA + (c + 1) * CH],
                               False, c == 3)
                    m.then_inc(full[t[0]], 1)
            for i in range(GH):
                taken(plan["o"].at(2 * i + 1))
                t = plan["gst"].at(i)
                bank = free(t)
                mm(bank[:, 0:TA], C("ones"), tile(g_sq, 2 * i, TA), True, False)
                mm(bank[:, 0:TA], C("ones"), tile(g_sq, 2 * i + 1, TA), False, True).then_inc(full[t[0]], 1)
            u0, T = plan["gout"]
            for j in range(4):
                project(u0 + j, T, 2 * j, X, TA, x_base=None if j else 16)
            stat(3, TA)
            ffn(1, 24, TA, lambda: stat(4, TA))
            stat(5, TA)

            u0, T = plan["ks"]
            project(u0, T, 0, HID, TA, x_base=32)
            stat(6, TA, True)
            u0, T = plan["vs"]
            project_tokens(u0, T, 0, HID, ((0, P), (P, P), (SEQ, META)))
            for i in range(2):
                taken(plan["ks"][1].at(i))
                t = plan["krot"].at(i)
                bank = free(t)
                mm(bank[:, 0:TA], C("rot"), tile(s_kraw, i, TA), True, True).then_inc(full[t[0]], 1)
            ffn(2, 40, SEQ)
            stat(7, SEQ)

            u0, T = plan["sq"]

            def rotate(j):
                for i in (2 * j, 2 * j + 1):
                    taken(plan["sq"][1].at(i))
                    t = plan["qrot"].at(i)
                    bank = free(t)
                    mm(bank[:, 0:SEQ], C("rot"), s_q[:, i * SEQ:(i + 1) * SEQ], True, True).then_inc(full[t[0]], 1)

            for j in range(4):
                project(u0 + j, T, 2 * j, X, SEQ, x_base=None if j else 48)
                if j == 0:
                    stat(8, SEQ)
                else:
                    rotate(j - 1)
            rotate(3)

            def attend(names, groups, first, pb, pitch, pT, q_of, k_of, v_of, segs, done, lag=0):
                S, TT, V = (plan[x] for x in names)

                def scores(g):
                    done(g)
                    for u in range(4):
                        n, b = divmod(u, 2)
                        t = S.at(4 * g + u)
                        bank = free(t)
                        hs = slice(64 * b, 64 * b + 64)
                        for at, size, key in segs(n):
                            m = mm(bank[:, at:at + size], q_of(g, hs, n), k_of(g, hs, key, size), True, True)
                        m.then_inc(full[t[0]], 1)

                def outputs(g):
                    t = V.at(g)
                    bank = free(t)
                    for u in range(4):
                        n, b = divmod(u, 2)
                        taken(TT.at(4 * g + u))
                        ss = segs(n)
                        for s, (at, size, key) in enumerate(ss):
                            a = (g % (1 + lag) * 4 + u) * 384 + s * P
                            m = mm(bank[64 * b:64 * b + 64, n * P:(n + 1) * P], v_of(g, b, key, size),
                                   pT[0:size, a:a + P], s == 0, s == len(ss) - 1)
                    m.then_inc(full[t[0]], 1)

                scores(0)
                for g in range(groups):
                    if g + 1 < groups:
                        scores(g + 1)
                    for u in range(4):
                        n, b = divmod(u, 2)
                        t = TT.at(4 * g + u)
                        bank = free(t)
                        pe.wait_ge(p_ready, first + 4 * g + u + 1)
                        for s, (at, size, key) in enumerate(segs(n)):
                            a = ((g % 2) * 4 + u) * pitch + at
                            p = pb[:, a:a + size]
                            m = turn(bank[0:size, s * P:(s + 1) * P], p)
                        m.then_inc(full[t[0]], 1)
                    if g >= lag:
                        outputs(g - lag)
                if lag:
                    outputs(groups - 1)

            swa_segs = (((0, P, 0), (P, META, SEQ)), ((0, P, 0), (P, P, P), (SEQ, META, SEQ)))
            attend(("ss", "sT", "sv"), 8, 0, a_p, TA, a_pT,
                   lambda g, hs, n: s_q[hs, g * SEQ + n * P:g * SEQ + (n + 1) * P],
                   lambda g, hs, key, size: kT[hs, g // 4, key:key + size],
                   lambda g, b, key, size: vs[0:size, key // P, (2 * (g // 4) + b) * 64:(2 * (g // 4) + b) * 64 + 64],
                   lambda n: swa_segs[n],
                   lambda g: pe.wait_ge(q_roped, g + 1), lag=1)
            u0, T = plan["sout"]
            for j in range(4):
                project(u0 + j, T, 2 * j, X, SEQ, x_base=None if j else 56)
            stat(9, SEQ)
            ffn(3, 64, SEQ, lambda: stat(10, SEQ))
            stat(11, SEQ)

            def level(n):
                if n == 0:
                    taken(plan["hq"][1].at(3))
                if LEVELS[n]:
                    pe.wait_ge(lvl_ready, n + 1)
                for p in range(2):
                    t = plan["lvl"].at(2 * n + p)
                    bank = free(t)
                    for i in range(4):
                        a = i * SEQ + p * P
                        left, right = (b_qk, b_qk) if LEVELS[n] else (b_kf, b_q)
                        m = mm(bank[:, i * P:(i + 1) * P], left[:, a:a + P], right[:, a:a + P], True, True)
                    m.then_inc(full[t[0]], 1)

            def section(name, js=None):
                u0, T = plan[name]
                for j in js if js is not None else range(4 if name in ("ga", "gb") else 2):
                    project(u0 + j, T, 2 * j, X, SEQ, x_base=72 if (name, j) == ("z", 0) else None)

            section("z")
            section("hq")
            for j in range(4):
                section("ga", [j])
                if j >= 2:
                    level(j - 2)
            for j in range(4):
                section("gb", [j])
                level(j + 2)
            for j in range(2):
                section("hgate", [j])
                level(j + 6)
            section("mq")
            section("mk")
            pe.wait_ge(lvl_ready, len(LEVELS))
            t = plan["cross"].at(0)
            bank = free(t)
            for i in range(4):
                m = mm(bank[:, i * P:(i + 1) * P], b_qk[:, i * SEQ:i * SEQ + P], b_qk[:, i * SEQ + P:(i + 1) * SEQ], True, True)
            m.then_inc(full[t[0]], 1)
            for name in ("hi", "mv"):
                u0, T = plan[name]
                for j in range(2):
                    project_tokens(u0 + j, T, 2 * j, X, ((0, P), (P, P)))
            taken(plan["cross"].at(0))
            taken(plan["hi"][1].at(3))
            for i in range(4):
                t = plan["ho"].at(i)
                bank = free(t)
                v0, v1 = b_v[:, i * P:(i + 1) * P], b_v[:, 512 + i * P:512 + (i + 1) * P]
                mm(bank[:, 0:P], v0, b_att[:, i * P:(i + 1) * P], True, False)
                mm(bank[:, P:SEQ], v1, b_att[:, 512 + i * P:512 + (i + 1) * P], False, False)
                mm(bank[:, P:SEQ], v0, b_att[:, 1024 + i * P:1024 + (i + 1) * P], False, True).then_inc(full[t[0]], 1)
            for i in range(4):
                taken(plan["ho"].at(i))
                t = plan["hst"].at(i)
                bank = free(t)
                mm(bank[:, 0:SEQ], C("ones"), b_sq[:, i * SEQ:(i + 1) * SEQ], True, True).then_inc(full[t[0]], 1)
            moba_segs = (((0, P, 0),), ((0, P, 0), (P, P, P)))

            def moba_ready(g):
                if g == 0:
                    taken(plan["mk"][1].at(3))
                    taken(plan["mv"][1].at(3))

            attend(("bs", "bT", "bv"), 4, 32, b_p, SEQ, b_pT,
                   lambda g, hs, n: b_mq[hs, g * SEQ + n * P:g * SEQ + (n + 1) * P],
                   lambda g, hs, key, size: b_mk[hs, g * SEQ + key:g * SEQ + key + size],
                   lambda g, b, key, size: b_mv[0:size, key // P * 512 + (2 * g + b) * 64:key // P * 512 + (2 * g + b) * 64 + 64],
                   lambda n: moba_segs[n], moba_ready)
            for name, at in (("pa", 0), ("pb", 4)):
                u0, T = plan[name]
                for j in range(2):
                    project(u0 + j, T, 4 * j, X, SEQ, kt=4, n_tiles=4, at=at, x_base=None if j else 80 + at)
            u0, T = plan["wo"]
            for j in range(4):
                project(u0 + j, T, 2 * j, X, SEQ, x_base=None if j else 88)
            for name, k in (("mean", 1), ("lnvar", 2)):
                t = plan[name].at(0)
                pe.wait_ge(ln_in, k)
                bank = free(t)
                m = mm(bank[:, 0:SEQ], C("ones"), acc[:, 0:SEQ], True, True)
                m.then_inc(full[t[0]], 1)

            pe.wait_ge(x2_ready, 8)
            t = plan["route"].at(0)
            bank = free(t)
            for p in range(2):
                for k in range(KT):
                    m = mm(bank[:, p * 64:p * 64 + 36], h[:, k * TA + p * P:k * TA + (p + 1) * P],
                           W("w_route", k * 36, (k + 1) * 36), k == 0, k == KT - 1)
            m.then_inc(full[t[0]], 1)
            for i in range(4):
                t = plan["xtok"].at(i)
                bank = free(t)
                for k in range(4):
                    a = ((i % 2) * 4 + k) * TA + i // 2 * P
                    m = turn(bank[:, k * P:(k + 1) * P], h[:, a:a + P])
                m.then_inc(full[t[0]], 1)
            pe.wait_ge(m_ready, 1)
            t = plan["pos"].at(0)
            bank = free(t)
            M0, M1 = m_r[:, 0:32], m_r[:, 32:64]
            mm(bank[:, 0:32], C("upper"), M0, True, True)
            mm(bank[:, 32:64], C("upper"), M1, True, False)
            mm(bank[:, 32:64], C("ones"), M0, False, True).then_inc(full[t[0]], 1)
            t = plan["cnt"].at(0)
            bank = free(t)
            mm(bank[:, 0:32], C("ones"), M0, True, False)
            mm(bank[:, 0:32], C("ones"), M1, False, True).then_inc(full[t[0]], 1)

            pe.wait_ge(table_ready, 1)
            for i in range(4):
                taken(plan["xtok"].at(i))
                m = mm(ps[i][:, :], m_zero, m_x[:, 0:512], True, False)
            m.then_inc(y_zeroed, 1)
            n_pairs = pe.value_load(meta_i[0:1, MAXB:MAXB + 1], min_val=4, max_val=MAXB // 2)
            taken(plan["cnt"].at(0))

            def gather():
                bank = ps[4]
                for kt in range(KT):
                    for p in range(2):
                        m = mm(bank[:, kt * 64:(kt + 1) * 64], m_x[:, p * D + kt * P:p * D + (kt + 1) * P],
                               m_P[:, p * 64:(p + 1) * 64], p == 0, p == 1)
                m.then_inc(full[4], 1)

            def combine():
                for p in range(2):
                    for n in range(2):
                        hs = slice(64 * n, 64 * n + 64)
                        for y in m_y:
                            m = mm(ps[2 * p + n][:, :], m_pT[hs, p * P:(p + 1) * P], y[hs, :], False, False)
                return m

            def expert(b, s):
                pe.wait_ge(evac[4], E_BASE[4] + b)
                pe.wait_ge(evac[5], E_BASE[5] + b)
                for i in range(4):
                    pe.wait_ge(e_landed[s * EXP_UNITS + i], 8 * (b - s) + 16)
                    for kk in range(2):
                        k = 2 * i + kk
                        for j in range(2):
                            a = (s * EXP_UNITS + i) * UNIT + kk * D
                            wt = ring[:, a:a + D].rearrange("p (g n) -> p g n", g=2)[:, :, 256 * j:256 * j + 256]
                            m = mm(ps[5][64 * j:64 * j + 64, :].rearrange("p (g n) -> p g n", g=2),
                                   m_xT[:, k * 64:(k + 1) * 64], wt, k == 0, k == KT - 1)
                            if kk == 0 and j == 0:
                                m.then_inc(exp_begun, 1)
                m.then_inc(full[5], 1)
                pe.wait_ge(evac[6], E_BASE[6] + b)
                pe.wait_ge(evac[7], E_BASE[7] + b)
                combine()
                pe.wait_ge(pw_made, b + 1)
                for p in range(2):
                    turn(ps[6][:, 256 + p * P:256 + (p + 1) * P], m_PP[:, p * P:(p + 1) * P])
                for p in range(2):
                    m = mm(ps[7][:, 0:1], m_PW[:, p * P:(p + 1) * P], C("ones", 0, 1), p == 0, p == 1)
                m.then_inc(pw_turned, 1)
                pe.wait_ge(evac[5], E_BASE[5] + b + 1)
                for c in range(2):
                    m = turn(ps[6][:, c * P:(c + 1) * P], m_h[:, c * P:(c + 1) * P])
                m.then_inc(full[6], 1)
                pe.wait_ge(p_made, b + 2)
                gather()
                pe.wait_ge(ht_made, b + 1)
                pe.wait_ge(w_taken, b + 1)
                for i in range(2):
                    pe.wait_ge(e_landed[s * EXP_UNITS + 4 + i], 8 * (b - s) + 16)
                    for kk in range(2):
                        k = 2 * i + kk
                        for n in range(2):
                            a = (s * EXP_UNITS + 4 + i) * UNIT + kk * D + n * 512
                            m = mm(ps[7][64 * n:64 * n + 64, :], m_hT[:, kk * P + 64 * i:kk * P + 64 * i + 64],
                                   ring[:, a:a + 512], k == 0, k == 3)
                            if kk == 0 and n == 0:
                                m.then_inc(exp_begun, 1)
                m.then_inc(full[7], 1)

            pe.wait_ge(p_made, 1)
            t = plan["e_gather"].at(0)
            free(t)
            gather()
            with pe.Fori(0, n_pairs) as pair:
                for s in range(2):
                    expert(2 * pair + s, s)
            pe.wait_ge(evac[7], E_BASE[7] + 2 * n_pairs)
            pe.wait_ge(evac[6], E_BASE[6] + 2 * n_pairs)
            combine().then_inc(y_done, 1)

        @block.scalar
        def _(act):
            chain, ahead = [0], [0]

            def did(ins):
                ins.then_inc(act_chain, 1)
                chain[0] += 1

            def own():
                act.wait_ge(act_chain, chain[0])

            def filled(t):
                act.wait_ge(full[t[0]], t[1] + 1)
                return ps[t[0]]

            def split(u, it=0):
                n = half_size(u)
                act.wait_ge(landed[u % RAW], 16 * (u // RAW + 1) + 16 * it)
                for j in range(2):
                    c = 2 * u + j
                    if not isinstance(it, int) or c >= PARTS:
                        act.wait_ge(half_begun, c - PARTS + 2 + 2 * RAW * it)
                    nc.scalar.activation(part(w_hi, c, 0, n), raw_slot(u, j * n, n), ACT.Copy).then_inc(hi_made, 1)

            def split_to(u):
                while ahead[0] <= min(u, N_UNITS - 1):
                    split(ahead[0])
                    ahead[0] += 1

            def square(q, src, w):
                if q >= 2:
                    act.wait_ge(sq_used, q - 1)
                nc.scalar.activation(sq[:, q % 2, 0:w], src, ACT.Square).then_inc(sq_made, 1)

            def high(m, src, w, dst=x_hi, **scale):
                nc.scalar.activation(tile(dst, m, w), src, ACT.Copy, **scale).then_inc(xhi_made, 1)

            def operands(n, w, gain_of, also=None):
                for m in range(KT):
                    if n:
                        act.wait_ge(h_ready, 8 * (n // 2 - 1) + m + 1)
                    if also is not None:
                        high(m, tile(h, m, w), w, hid_hi, scale=also(m))
                    else:
                        high(m, tile(h, m, w), w, scale=gain_of(m))
                    nc.scalar.activation(tile(zg, m, w), tile(h, m, w), ACT.Square).then_inc(squared, 1)
                if also is not None:
                    for m in range(KT):
                        high(m, tile(h, m, w), w, scale=gain_of(m))

            def root(t, src, dst):
                act.wait_ge(evac[t[0]], t[1] + 1)
                nc.scalar.activation(dst, src, ACT.Sqrt).then_inc(std_made, 1)

            def root_stat(n, w, columns=False):
                t = plan[f"stat{n}"].at(0)
                if columns:
                    act.wait_ge(evac[t[0]], t[1] + 1)
                    nc.scalar.activation(small[:, 252:255], small[:, 248:251], ACT.Sqrt)
                root(t, var[:, 0:w], std[:, 0:w])

            def branch_out(name, n, g, table, w, per=2):
                u0, T = plan[name]
                for m in range(KT):
                    split_to(u0 + m // per + 1)
                    t = T.at(m)
                    bank = filled(t)
                    square(8 * (n // 2) + m, bank[:, 0:w], w)
                    nc.scalar.activation(tile(zg, m, w), bank[:, 0:w], ACT.Copy,
                                         scale=gain(g, m, table)).then_inc(evac[t[0]], 1)
                root_stat(n, w)

            def ffn(n, g, w):
                u0, T = plan[f"in{n}"]

                def gate(j, it):
                    tg = T.at(2 * j, it, 4)
                    act.wait_ge(evac[tg[0]], tg[1] + 1)
                    nc.scalar.activation(tile(sg, j, w), tile(sg, j, w), ACT.Silu).then_inc(gate_silu, 1)

                with act.Fori(0, FT // 2 - 1) as it:
                    for j in range(2):
                        gate(j, it)
                        split(u0 + j + 2, it)
                ahead[0] = u0 + FT
                for j in range(2):
                    gate(j, FT // 2 - 1)
                    split_to(u0 + FT + j)
                branch_out(f"out{n}", 2 * g_index[n] + 1, g, halfg, w, 1)

            g_index = {0: 0, 1: 2, 2: 3, 3: 5}

            act.wait_ge(params_in, 16)
            act.wait_ge(x_in, 16)
            operands(0, TA, lambda m: gain(0, m))
            split_to(plan["in0"][0] + 1)
            act.wait_ge(lb_in, 2)
            nc.scalar.activation(small[:, 0:8], small[:, 0:8], ACT.Exp).then_inc(lb_exp, 1)
            root_stat(0, TA)
            for i in range(8):
                t = plan["bias"].at(i)
                nc.scalar.activation(b_br[:, i * 384:(i + 1) * 384], filled(t)[:, 0:384], ACT.Copy)\
                    .then_inc(evac[t[0]], 1)
            ffn(0, 1, TA)
            act.wait_ge(bias_out, 8 * 16)
            operands(2, TA, lambda m: gain(2, m))
            split_to(plan["r"][0] + 1)
            root_stat(2, TA, True)

            for i in range(8):
                t = plan["r"][1].at(i)
                split_to(plan["r"][0] + i // 2 + 1)
                act.wait_ge(evac[t[0]], t[1] + 1)
                nc.scalar.activation(tile(g_r, i, TA), tile(g_r, i, TA), ACT.Silu)
            t = plan["gate"].at(3)
            act.wait_ge(evac[t[0]], t[1] + 1)
            did(nc.scalar.activation(g_e0, g_b, ACT.Abs))
            own()
            did(nc.scalar.activation(g_e1, g_e0, ACT.Exp, scale=-1.0))
            own()
            nc.scalar.activation(g_e2, g_e1, ACT.Ln, bias=C("ones", 0, 1)).then_inc(soft_made, 1)
            act.wait_ge(decay_in, 1)
            nc.scalar.activation(g_e0, g_b, ACT.Exp, scale=1.0 / 16).then_inc(decay_made, 1)
            nc.scalar.activation(g_e1, g_b, ACT.Exp, scale=-1.0 / 16).then_inc(decay_made, 1)
            act.wait_ge(decay_in, 2)
            nc.scalar.activation(g_e2, g_e2, ACT.Exp, scale=1.0 / 16).then_inc(decay_made, 1)
            split_to(plan["gout"][0])
            for i in range(GH):
                t = plan["kwT"].at(i)
                bank = filled(t)
                nc.scalar.activation(g_kwT[:, i * 384:i * 384 + 256], bank[:, 0:256], ACT.Copy)
                nc.scalar.activation(g_kwT[0:META, i * 384 + 256:(i + 1) * 384], bank[0:META, 256:384], ACT.Copy)\
                    .then_inc(evac[t[0]], 1)
            for i in range(8):
                t = plan["o"].at(i)
                bank = filled(t)
                nc.scalar.activation(tile(g_sq, i, TA), bank[:, 0:TA], ACT.Square)
                nc.scalar.activation(tile(g_o, i, TA), bank[:, 0:TA], ACT.Copy, scale=W("gla_norm", i % 2, i % 2 + 1))\
                    .then_inc(evac[t[0]], 1)
            for i in range(GH):
                root(plan["gst"].at(i), tile(g_kw, i, TA), tile(g_kw, i, TA))
            for i in range(8):
                act.wait_ge(scaled, i + 1)
                high(i, tile(g_o, i, TA), TA)
            branch_out("gout", 3, 3, par, TA)
            operands(4, TA, lambda m: gain(4, m))
            split_to(plan["in1"][0] + 1)
            root_stat(4, TA)
            ffn(1, 5, TA)
            operands(6, TA, lambda m: gain(6, m), lambda m: W("kv_norm", m, m + 1))
            split_to(plan["vs"][0])
            root_stat(6, TA, True)

            split_to(plan["in2"][0])
            t = plan["ks"][1].at(0)
            act.wait_ge(evac[t[0]], t[1] + 1)
            for i, n in enumerate((P, P, META)):
                t = plan["vs"][1].at(i)
                nc.scalar.activation(vs[0:n, i, :], filled(t)[0:n, 0:256], ACT.Copy, scale=small[0:n, 256 + i:257 + i])\
                    .then_inc(evac[t[0]], 1)
            split_to(plan["in2"][0] + 1)
            ffn(2, 7, SEQ)
            operands(8, SEQ, lambda m: gain(8, m))
            split_to(plan["sq"][0] + 1)
            root_stat(8, SEQ)

            split_to(plan["sq"][0] + 4)

            def attend(names, groups, first, pb, pitch, pT, widths, n_full, meta, o, sinks, lag=0):
                S, TT, V = (plan[x] for x in names)

                def outputs(g):
                    t = V.at(g)
                    nc.scalar.activation(o[:, g * SEQ:(g + 1) * SEQ], filled(t)[:, 0:SEQ], ACT.Copy).then_inc(evac[t[0]], 1)

                for g in range(groups):
                    at = 16 + (g % 2) * 16
                    act.wait_ge(neg_max, first + g + 1)
                    if sinks:
                        nc.scalar.activation(small[:, at + 4:at + 8], small[:, at + 4:at + 8], ACT.Exp)
                    for u in range(4):
                        a = ((g % 2) * 4 + u) * pitch
                        p = pb[:, a:a + widths[u // 2]]
                        e = nc.scalar.activation(p, p, ACT.Exp, bias=small[:, at + u:at + u + 1],
                                                 accum_out=small[:, at + 8 + u:at + 9 + u])
                        if u == 3:
                            e.then_inc(exp_made, 1)
                    for u in range(4):
                        t = TT.at(4 * g + u)
                        bank = filled(t)
                        if g > lag:
                            act.wait_ge(full[V.at(g - 1 - lag)[0]], V.at(g - 1 - lag)[1] + 1)
                        n = n_full[u // 2] * P
                        a = (g % (1 + lag) * 4 + u) * 384
                        c = nc.scalar.activation(pT[:, a:a + n], bank[:, 0:n], ACT.Copy)
                        if meta:
                            c = nc.scalar.activation(pT[0:META, a + n:a + n + P], bank[0:META, n:n + P], ACT.Copy)
                        c.then_inc(evac[t[0]], 1)
                    if g >= lag:
                        outputs(g - lag)
                if lag:
                    outputs(groups - 1)

            attend(("ss", "sT", "sv"), 8, 0, a_p, TA, a_pT, (P + META, SEQ + META), (1, 2), True, s_o, True,
                   lag=1)
            branch_out("sout", 9, 9, par, SEQ)
            operands(10, SEQ, lambda m: gain(10, m))
            split_to(plan["in3"][0] + 1)
            root_stat(10, SEQ)
            ffn(3, 11, SEQ)
            for m in range(KT):
                act.wait_ge(h_ready, 8 * 5 + m + 1)
                high(m, tile(h, m, SEQ), SEQ)

            def b_in(i):
                return W("b_in", i, i + 1)

            def sect(name, i, dst, func, col):
                t = plan[name][1].at(i)
                split_to(plan[name][0] + i // 2 + 1)
                nc.scalar.activation(dst, filled(t)[:, 0:SEQ], func, bias=b_in(col)).then_inc(evac[t[0]], 1)

            for i in range(4):
                t = plan["z"][1].at(i)
                split_to(plan["z"][0] + i // 2 + 1)
                bank = filled(t)
                nc.scalar.activation(b_e[:, i * SEQ:(i + 1) * SEQ], bank[:, 0:SEQ], ACT.Sigmoid, bias=b_in(4 + i))
                nc.scalar.activation(b_kf[:, i * SEQ:(i + 1) * SEQ], bank[:, 0:SEQ], ACT.Sigmoid, scale=-1.0,
                                     bias=small[:, 12 + i:13 + i]).then_inc(evac[t[0]], 1)
            for i in range(4):
                sect("hq", i, b_q[:, i * SEQ:(i + 1) * SEQ], ACT.Silu, i)
            act.wait_ge(hg_arg, 1)
            nc.scalar.activation(b_b, b_e, ACT.Ln).then_inc(hg_ln, 1)
            for j in range(8):
                for i in range(2):
                    name, m = ("ga", 2 * j + i) if j < 4 else ("gb", 2 * (j - 4) + i)
                    dst = tile(b_sga, m, SEQ) if j < 4 else b_sgb[:, m * SEQ:(m + 1) * SEQ]
                    sect(name, m, dst, ACT.Sigmoid, (28 if j < 4 else 36) + m)
                act.wait_ge(lvl_in, j + 1)
                nc.scalar.activation(b_e, b_e, ACT.Exp).then_inc(lvl_exp, 1)
            for i in range(4):
                sect("hgate", i, b_sg[:, i * SEQ:(i + 1) * SEQ], ACT.Silu, 12 + i)
            for i in range(4):
                sect("mq", i, b_mq[:, i * SEQ:(i + 1) * SEQ], ACT.Identity, 16 + i)
            for i in range(4):
                sect("mk", i, b_mk[:, i * SEQ:(i + 1) * SEQ], ACT.Identity, 20 + i)
            split_to(plan["pa"][0])
            for i in range(4):
                t = plan["ho"].at(i)
                bank = filled(t)
                nc.scalar.activation(b_sq[:, i * SEQ:(i + 1) * SEQ], bank[:, 0:SEQ], ACT.Square)
                nc.scalar.activation(b_a[:, i * SEQ:(i + 1) * SEQ], bank[:, 0:SEQ], ACT.Copy).then_inc(evac[t[0]], 1)
            for i in range(4):
                root(plan["hst"].at(i), b_e[:, i * SEQ:(i + 1) * SEQ], b_e[:, i * SEQ:(i + 1) * SEQ])
            attend(("bs", "bT", "bv"), 4, 8, b_p, SEQ, b_pT, (P, SEQ), (1, 2), False, b_bo, False)
            split_to(N_UNITS)
            h3 = h[:, :].rearrange("p (m t) -> p m t", m=KT)[:, :, 0:SEQ]
            z3 = zg[:, :].rearrange("p (m t) -> p m t", m=KT)[:, :, 0:SEQ]
            act.wait_ge(centred, 1)
            nc.scalar.activation(z3, h3, ACT.Square).then_inc(ln_squared, 1)
            root(plan["lnvar"].at(0), var[:, 0:SEQ], std[:, 0:SEQ])
            for i in range(4):
                t = plan["xtok"].at(i)
                nc.scalar.activation(m_x[:, (i // 2) * D + (i % 2) * 512:(i // 2) * D + (i % 2) * 512 + 512],
                                     filled(t)[:, :], ACT.Copy).then_inc(evac[t[0]], 1)
            act.wait_ge(route_in, 1)
            nc.scalar.activation(r_["ge"], r_["ge"], ACT.Exp).then_inc(route_exp, 1)
            act.wait_ge(route_in, 2)
            nc.scalar.activation(r_["ev"], r_["ev"], ACT.Exp).then_inc(route_exp, 1)

            act.wait_ge(table_ready, 1)
            n_pairs = act.value_load(meta_i[0:1, MAXB:MAXB + 1], min_val=4, max_val=MAXB // 2)
            t = plan["e_gather"].at(0)
            nc.scalar.activation(m_xT, filled(t)[:, :], ACT.Copy).then_inc(evac[4], 1)
            with act.Fori(0, n_pairs) as pair:
                for s in range(2):
                    b = 2 * pair + s
                    act.wait_ge(full[5], E_BASE[5] + b + 1)
                    act.wait_ge(evac[5], E_BASE[5] + b)
                    nc.scalar.activation(m_sg, ps[5][:, 0:256], ACT.Silu).then_inc(silu_made, 1)
                    act.wait_ge(full[6], E_BASE[6] + b + 1)
                    nc.scalar.activation(m_hT, ps[6][:, 0:256], ACT.Copy).then_inc(ht_made, 1)
                    nc.scalar.activation(m_pT, ps[6][:, 256:512], ACT.Copy).then_inc(evac[6], 1)
                    act.wait_ge(full[4], E_BASE[4] + b + 1)
                    nc.scalar.activation(m_xT, ps[4][:, :], ACT.Copy).then_inc(evac[4], 1)

            for p in range(2):
                act.wait_ge(fin_centred, p + 1)
                nc.scalar.activation(zg[:, p * D:(p + 1) * D], m_o[:, p * D:(p + 1) * D], ACT.Square,
                                     accum_out=small[:, 100 + p:101 + p]).then_inc(fin_squared, 1)
            act.wait_ge(fin_var, 1)
            nc.scalar.activation(small[:, 104:106], small[:, 102:104], ACT.Sqrt).then_inc(fin_std, 1)
            for p in range(2):
                act.wait_ge(out_ready, p + 1)
                act.dma_start(out[0, p * P:(p + 1) * P, :], m_o[:, p * D:(p + 1) * D]).then_inc(out_stored, 16)
            act.wait_ge(out_stored, 32)

        @block.vector
        def _(dve):
            chain, ahead, stds, highs, sums = [0], [0], [0], [0], [0]
            v = nc.vector

            def did(ins):
                ins.then_inc(dve_chain, 1)
                chain[0] += 1
                return chain[0]

            def own(c=None):
                dve.wait_ge(dve_chain, chain[0] if c is None else c)

            def then(ins):
                did(ins)
                own()

            def filled(t):
                dve.wait_ge(full[t[0]], t[1] + 1)
                return ps[t[0]]

            def mine(t):
                dve.wait_ge(evac[t[0]], t[1] + 1)

            def split(u, it=0):
                n = half_size(u)
                for j in range(2):
                    c = 2 * u + j
                    dve.wait_ge(hi_made, c + 1 + 2 * RAW * it)
                    v.tensor_tensor(part(w_lo, c, 0, n), raw_slot(u, j * n, n), part(w_hi, c, 0, n).bitcast(F32),
                                    ALU.subtract).then_inc(lo_made, 1)

            def split_to(u):
                while ahead[0] <= min(u, N_UNITS - 1):
                    split(ahead[0])
                    ahead[0] += 1

            def low_part(dst, src):
                return v.tensor_tensor(dst[1], src, dst[0].bitcast(F32), ALU.subtract)

            def to_x(m, src, w):
                dst = tile(x_hi, m, w), tile(x_lo, m, w)
                then(v.tensor_copy(dst[0], src))
                low_part(dst, src).then_inc(x_ready, 1)

            def add_square(n, m, w):
                q = 8 * (n // 2) + m
                dve.wait_ge(sq_made, q + 1)
                if m == 0:
                    v.tensor_copy(acc[:, 0:w], sq[:, q % 2, 0:w]).then_inc(sq_used, 1)
                else:
                    dve.wait_ge(sq_used, q)
                    v.tensor_tensor(acc[:, 0:w], acc[:, 0:w], sq[:, q % 2, 0:w], ALU.add).then_inc(sq_used, 1)

            def inverse_root(t, w, mean_of, eps, mid, root, dst):
                bank = filled(t)
                v.tensor_scalar(mid, bank[:, 0:w], 1.0 / mean_of, eps, ALU.mult, ALU.add).then_inc(evac[t[0]], 1)
                stds[0] += 1
                dve.wait_ge(std_made, stds[0])
                then(v.reciprocal(dst, root))

            def inverse_rms(n, w):
                inverse_root(plan[f"stat{n}"].at(0), w, D, EPS, var[:, 0:w], std[:, 0:w], rs[:, 0:w])

            def low(m, w, factor=None, dst=(x_hi, x_lo), src=None):
                highs[0] += 1
                dve.wait_ge(xhi_made, highs[0])
                src = tile(h, m, w) if src is None else src
                hi = tile(dst[0], m, w).bitcast(F32)
                if factor is None:
                    e = v.tensor_tensor(tile(dst[1], m, w), src, hi, ALU.subtract)
                else:
                    e = v.scalar_tensor_tensor(tile(dst[1], m, w), src, factor, hi, ALU.mult, ALU.subtract)
                e.then_inc(x_ready, 1)

            def sum_squares(w):
                sums[0] += 1
                dve.wait_ge(squared, 8 * sums[0])
                squares = zg[:, :].rearrange("p (m t) -> p t m", m=KT)[:, 0:w, :]
                v.tensor_reduce(acc[:, 0:w], squares, AX, ALU.add).then_inc(sums_made, 1)

            def inverse_rms_columns(n, w):
                t = plan[f"stat{n}"].at(0)
                bank = filled(t)
                v.tensor_scalar(small[:, 248:250], bank[:, 300:302], 1.0 / D, EPS, ALU.mult, ALU.add)
                v.tensor_scalar(small[0:META, 250:251], bank[0:META, 302:303], 1.0 / D, EPS, ALU.mult, ALU.add)
                inverse_rms(n, w)
                then(v.reciprocal(small[:, 256:259], small[:, 252:255]))

            def residual(name, n, w, factor_of=None, dst=(x_hi, x_lo), per=2):
                u0, T = plan[name]
                for m in range(KT):
                    split_to(u0 + m // per + 1)
                    add_square(n, m, w)
                inverse_rms(n, w)
                for m in range(KT):
                    mine(T.at(m))
                steps = []
                for m in range(KT + 2):
                    if m < KT:
                        z = tile(zg, m, w)
                        steps.append(did(v.tensor_tensor(z, z, rs[:, 0:w], ALU.mult)))
                    if 1 <= m <= KT:
                        own(steps[m - 1])
                        v.tensor_tensor(tile(h, m - 1, w), tile(h, m - 1, w), tile(zg, m - 1, w), ALU.add)\
                            .then_inc(h_ready, 1)
                    if m >= 2:
                        low(m - 2, w, factor_of and factor_of(m - 2), dst)

            def ffn_in(n, w):
                u0, T = plan[f"in{n}"]

                def hidden(j, it):
                    tg, tu = T.at(2 * j, it, 4), T.at(2 * j + 1, it, 4)
                    at = it * (2 * TA) + j * TA
                    cols = slice(at, at + w) if isinstance(it, int) else bass.ds(at, w)
                    g, x = tile(sg, j, w), tile(hw, j, w)
                    dve.wait_ge(full[tg[0]], tg[1] + 1)
                    v.tensor_tensor(g, ps[tg[0]][:, 0:w], rs[:, 0:w], ALU.mult).then_inc(evac[tg[0]], 1)
                    dve.wait_ge(full[tu[0]], tu[1] + 1)
                    v.tensor_tensor(x, ps[tu[0]][:, 0:w], rs[:, 0:w], ALU.mult).then_inc(evac[tu[0]], 1)
                    mine(tu)
                    dve.wait_ge(gate_silu, FT * n + 2 * it + j + 1)
                    v.tensor_tensor(hid_hi[:, cols], x, g, ALU.mult)
                    v.tensor_tensor(x, x, g, ALU.mult).then_inc(hw_made, 1)
                    dve.wait_ge(hw_made, FT * n + 2 * it + j + 1)
                    low_part((hid_hi[:, cols], hid_lo[:, cols]), x).then_inc(hid_made, 1)

                with dve.Fori(0, FT // 2 - 1) as it:
                    for j in range(2):
                        hidden(j, it)
                        split(u0 + j + 2, it)
                ahead[0] = u0 + FT
                for j in range(2):
                    hidden(j, FT // 2 - 1)
                    split_to(u0 + FT + j)

            dve.wait_ge(params_in, 16)
            l0, l1 = W("lb_logits", 0, 4), W("lb_logits", 4, 8)
            then(v.tensor_tensor(small[:, 8:12], l0, l1, ALU.max))
            did(v.tensor_tensor(small[:, 0:4], l0, small[:, 8:12], ALU.subtract))
            v.tensor_tensor(small[:, 4:8], l1, small[:, 8:12], ALU.subtract).then_inc(lb_in, 1)
            v.tensor_scalar(halfg[:, :], W("gains"), 0.5, None, ALU.mult).then_inc(lb_in, 1)
            then(v.tensor_scalar(small[:, 12:16], W("b_in", 4, 8), -1.0, None, ALU.mult))

            lr3, gn3 = (x.rearrange("p (k n) -> p k n", k=KT) for x in (W("w_lr"), W("gains", 2 * KT, 3 * KT)))
            did(v.tensor_tensor(lr3, lr3, gn3.to_broadcast([P, KT, RANK]), ALU.mult))
            did(v.memset(small[:, 248:251], 1.0))
            dve.wait_ge(x_in, 16)
            for m in range(KT):
                low(m, TA, gain(0, m))
            sum_squares(TA)
            split_to(plan["in0"][0] + 1)
            inverse_rms(0, TA)
            dve.wait_ge(lb_exp, 1)
            then(v.tensor_tensor(small[:, 8:12], small[:, 0:4], small[:, 4:8], ALU.add))
            then(v.reciprocal(small[:, 8:12], small[:, 8:12]))
            LB, LB1 = slice(240, 244), slice(244, 248)
            then(v.tensor_tensor(small[:, LB], small[:, 0:4], small[:, 8:12], ALU.mult))
            then(v.tensor_scalar(small[:, LB1], small[:, LB], -1.0, 1.0, ALU.mult, ALU.add))
            ffn_in(0, TA)
            residual("out0", 1, TA, lambda m: gain(2, m), per=1)
            dve.wait_ge(bias_out, 8 * 16)
            sum_squares(TA)
            split_to(plan["r"][0] + 1)
            inverse_rms_columns(2, TA)

            for i in range(8):
                t = plan["r"][1].at(i)
                split_to(plan["r"][0] + i // 2 + 1)
                v.tensor_tensor(tile(g_r, i, TA), filled(t)[:, 0:TA], rs[:, :], ALU.mult).then_inc(evac[t[0]], 1)
                if i == 1:
                    t = plan["lr"].at(0)
                    v.tensor_tensor(g_lr[0:RANK, :], filled(t)[0:RANK, 0:TA], rs[0:RANK, :], ALU.mult)\
                        .then_inc(evac[t[0]], 1)
                if i == 3:
                    for n in range(GH):
                        t = plan["gate"].at(n)
                        v.tensor_scalar(tile(g_b, n, TA), filled(t)[:, 0:TA], W("b_gate", n, n + 1), None, ALU.add)\
                            .then_inc(evac[t[0]], 1)
            mine(plan["gate"].at(3))
            dve.wait_ge(soft_made, 1)
            then(v.tensor_scalar(g_b, g_b, 0.0, None, ALU.min))
            then(v.tensor_tensor(g_e2, g_b, g_e2, ALU.subtract))
            for i in range(GH):
                s = v.tensor_tensor_scan(tile(g_b, i, TA), C("reset_g"), tile(g_e2, i, TA), 0.0, ALU.mult, ALU.add)
            s.then_inc(decay_in, 1)
            dve.wait_ge(decay_in, 1)
            b4 = g_b.rearrange("p (h t) -> p h t", h=GH)
            e4 = g_e2.rearrange("p (h t) -> p h t", h=GH)
            for i in range(GH):
                bx = g_b[:, i * TA:i * TA + SEQ].rearrange("p (c s) -> p c s", s=CH)
                ex = g_e2[:, i * TA:i * TA + SEQ].rearrange("p (c s) -> p c s", s=CH)
                v.tensor_tensor(ex, bx[:, :, CH - 1:CH].to_broadcast([P, 4, CH]), bx, ALU.subtract)
            v.tensor_tensor(e4[:, :, SEQ:TA], b4[:, :, TA - 1:TA].to_broadcast([P, GH, META]), b4[:, :, SEQ:TA],
                            ALU.subtract).then_inc(decay_in, 1)
            for j in range(4):
                split_to(plan["v"][0] + j + 1)
                for s, n in enumerate((P, P, META)):
                    t = plan["v"][1].at(3 * j + s)
                    dst = g_vm[0:n, j * 256:(j + 1) * 256] if s == 2 else g_v[:, s * D + j * 256:s * D + (j + 1) * 256]
                    v.tensor_scalar(dst, filled(t)[0:n, 0:256], small[0:n, 256 + s:257 + s], None, ALU.mult)\
                        .then_inc(evac[t[0]], 1)
            dve.wait_ge(decay_made, 3)
            decays = g_e0.rearrange("p (h t) -> p h t", h=GH)[:, :, CH - 1:SEQ:CH]
            did(v.tensor_copy(g_dec.rearrange("p (h c) -> p h c", h=GH), decays))
            own()
            for e in (g_e1, g_e2, g_e0):
                e = e.rearrange("p (h t) -> p h t", h=GH)
                did(v.tensor_tensor(e, e, rs[:, :].rearrange("p (a t) -> p a t", a=1).to_broadcast([P, GH, TA]), ALU.mult))
            own()
            for i in range(GH):
                split_to(plan["k"][0] + i // 2 + 1)
                t = plan["k"][1].at(i)
                bank = filled(t)
                v.tensor_tensor(tile(g_k, i, TA), bank[:, 0:TA], tile(g_e1, i, TA), ALU.mult)
                v.tensor_tensor(tile(g_kw, i, TA), bank[:, 0:TA], tile(g_e2, i, TA), ALU.mult).then_inc(evac[t[0]], 1)
            for i in range(GH):
                split_to(plan["q"][0] + i // 2 + 1)
                t = plan["q"][1].at(i)
                v.scalar_tensor_tensor(tile(g_q, i, TA), filled(t)[:, 0:TA], float(GDK) ** -0.5, tile(g_e0, i, TA),
                                       ALU.mult, ALU.mult).then_inc(evac[t[0]], 1)
            for i in range(GH):
                t = plan["att"].at(i)
                bank = filled(t)
                v.tensor_tensor(g_att[:, i * TA:i * TA + SEQ].rearrange("p (a b) -> p a b", a=2),
                                bank[:, 0:SEQ].rearrange("p (a b) -> p a b", a=2),
                                C("pairmask").rearrange("p (a b) -> p a b", a=1).to_broadcast([P, 2, P]), ALU.mult)
                v.tensor_tensor(g_att[0:META, i * TA + SEQ:(i + 1) * TA], bank[0:META, SEQ:TA],
                                C("pairmask", 0, META, slice(0, META)), ALU.mult).then_inc(evac[t[0]], 1)
            for i in range(GH):
                def state(c):
                    return g_s[:, (i * 4 + c) * GDV:(i * 4 + c + 1) * GDV]

                def decay(c):
                    return g_dec[:, i * 4 + c:i * 4 + c + 1]

                ta, tb, tc = (plan["kv"].at(3 * i + c) for c in range(3))
                bank = filled(ta)
                then(v.tensor_copy(state(0), bank[:, 0:256]))
                v.scalar_tensor_tensor(state(1), state(0), decay(0), bank[:, 256:512], ALU.mult, ALU.add)\
                    .then_inc(evac[ta[0]], 1)
                mine(ta)
                v.scalar_tensor_tensor(state(2), state(1), decay(1), filled(tb)[:, 0:256], ALU.mult, ALU.add)\
                    .then_inc(evac[tb[0]], 1)
                mine(tb)
                v.scalar_tensor_tensor(state(3), state(2), decay(2), filled(tc)[:, 0:256], ALU.mult, ALU.add)\
                    .then_inc(evac[tc[0]], 1)
            for i in range(8):
                o = tile(g_o, i, TA)
                mine(plan["o"].at(i))
                did(v.tensor_tensor(o, o, tile(g_r, i, TA), ALU.mult))
            for i in range(GH):
                t = plan["gst"].at(i)
                v.tensor_scalar(tile(g_kw, i, TA), filled(t)[:, 0:TA], 1.0 / GDV, EPS, ALU.mult, ALU.add)\
                    .then_inc(evac[t[0]], 1)
            own()
            for i in range(GH):
                r = tile(g_kw, i, TA)
                stds[0] += 1
                dve.wait_ge(std_made, stds[0])
                then(v.reciprocal(r, r))
                for half in range(2):
                    o = tile(g_o, 2 * i + half, TA)
                    v.tensor_tensor(o, o, r, ALU.mult).then_inc(scaled, 1)
                    if i or half:
                        low(2 * i + half - 1, TA, src=tile(g_o, 2 * i + half - 1, TA))
            low(7, TA, src=tile(g_o, 7, TA))
            residual("gout", 3, TA, lambda m: gain(4, m))
            sum_squares(TA)
            split_to(plan["in1"][0] + 1)
            inverse_rms(4, TA)
            ffn_in(1, TA)
            residual("out1", 5, TA, lambda m: W("kv_norm", m, m + 1), (hid_hi, hid_lo), per=1)
            sum_squares(TA)
            for m in range(KT):
                low(m, TA, gain(6, m))
            split_to(plan["vs"][0])
            inverse_rms_columns(6, TA)

            for i in range(2):
                t = plan["ks"][1].at(i)
                v.tensor_tensor(tile(s_kraw, i, TA), filled(t)[:, 0:TA], rs[:, :], ALU.mult).then_inc(evac[t[0]], 1)
            split_to(plan["in2"][0])
            for i in range(2):
                t = plan["krot"].at(i)
                bank = filled(t)
                v.tensor_tensor(tile(s_krot, i, TA), bank[:, 0:TA], C("sin"), ALU.mult).then_inc(evac[t[0]], 1)
                mine(t)
                mine(plan["ks"][1].at(i))
                then(v.tensor_tensor(kT[:, i, :], tile(s_kraw, i, TA), C("cos"), ALU.mult))
                then(v.tensor_tensor(kT[:, i, :], kT[:, i, :], tile(s_krot, i, TA), ALU.add))
            split_to(plan["in2"][0] + 1)
            ffn_in(2, SEQ)
            residual("out2", 7, SEQ, lambda m: gain(8, m), per=1)
            sum_squares(SEQ)
            split_to(plan["sq"][0] + 1)
            inverse_rms(8, SEQ)

            def rotate(i):
                t = plan["qrot"].at(i)
                bank = filled(t)
                mine(plan["sq"][1].at(i))
                q = s_q[:, i * SEQ:(i + 1) * SEQ]
                x = s_t[:, (i % 2) * SEQ:(i % 2 + 1) * SEQ]
                did(v.tensor_tensor(q, q, C("cos", 0, SEQ), ALU.mult))
                v.tensor_tensor(x, bank[:, 0:SEQ], C("sin", 0, SEQ), ALU.mult).then_inc(evac[t[0]], 1)
                own()
                mine(t)
                v.tensor_tensor(q, q, x, ALU.add).then_inc(q_roped, 1)

            for j in range(4):
                split_to(plan["sq"][0] + j + 1)
                for i in (2 * j, 2 * j + 1):
                    t = plan["sq"][1].at(i)
                    v.tensor_tensor(s_q[:, i * SEQ:(i + 1) * SEQ], filled(t)[:, 0:SEQ], rs[:, 0:SEQ], ALU.mult)\
                        .then_inc(evac[t[0]], 1)
                if j:
                    rotate(2 * j - 2)
                    rotate(2 * j - 1)
            rotate(6)
            rotate(7)

            def attend(names, groups, first, pb, pitch, widths, mask_of, sinks, between=None):
                S = plan[names[0]]

                def maxima(g):
                    at = 16 + (g % 2) * 16
                    for u in range(4):
                        w = widths[u // 2]
                        t = S.at(4 * g + u)
                        p = pb[:, ((g % 2) * 4 + u) * pitch:((g % 2) * 4 + u) * pitch + w]
                        v.scalar_tensor_tensor(p, filled(t)[:, 0:w], 0.125, mask_of(g, u), ALU.mult, ALU.add)\
                            .then_inc(evac[t[0]], 1)
                    mine(t)
                    p4 = pb[:, (g % 2) * 4 * pitch:(g % 2 + 1) * 4 * pitch].rearrange("p (u t) -> p u t", u=4)
                    did(v.tensor_reduce(small[:, at:at + 2], p4[:, 0:2, 0:widths[0]], AX, ALU.max))
                    then(v.tensor_reduce(small[:, at + 2:at + 4], p4[:, 2:4, 0:widths[1]], AX, ALU.max))
                    if sinks:
                        sk = W("sinks", 4 * g, 4 * g + 4)
                        then(v.tensor_tensor(small[:, at:at + 4], small[:, at:at + 4], sk, ALU.max))
                        then(v.tensor_scalar(small[:, at:at + 4], small[:, at:at + 4], -1.0, None, ALU.mult))
                        v.tensor_tensor(small[:, at + 4:at + 8], small[:, at:at + 4], sk, ALU.add).then_inc(neg_max, 1)
                    else:
                        v.tensor_scalar(small[:, at:at + 4], small[:, at:at + 4], -1.0, None, ALU.mult)\
                            .then_inc(neg_max, 1)

                maxima(0)
                for g in range(groups):
                    if g + 1 < groups:
                        maxima(g + 1)
                    at = 16 + (g % 2) * 16
                    dve.wait_ge(exp_made, first + g + 1)
                    if sinks:
                        then(v.tensor_tensor(small[:, at + 8:at + 12], small[:, at + 8:at + 12],
                                             small[:, at + 4:at + 8], ALU.add))
                    then(v.reciprocal(small[:, at + 12:at + 16], small[:, at + 8:at + 12]))
                    for u in range(4):
                        p = pb[:, ((g % 2) * 4 + u) * pitch:((g % 2) * 4 + u) * pitch + widths[u // 2]]
                        v.tensor_scalar(p, p, small[:, at + 12 + u:at + 13 + u], None, ALU.mult).then_inc(p_ready, 1)
                    if between is not None:
                        between(g)

            attend(("ss",), 8, 0, a_p, TA, (P + META, SEQ + META), lambda g, u: C("swa0") if u < 2 else C("swa1"), True)
            for m in range(KT):
                mine(plan["sv"].at(m))
                to_x(m, s_o[:, m * SEQ:(m + 1) * SEQ], SEQ)
            residual("sout", 9, SEQ, lambda m: gain(10, m))
            sum_squares(SEQ)
            split_to(plan["in3"][0] + 1)
            inverse_rms(10, SEQ)
            ffn_in(3, SEQ)
            residual("out3", 11, SEQ, per=1)

            dve.wait_ge(bias_in, 8 * 16)
            for i in range(8):
                last = v.tensor_tensor(b_bias[:, i * SEQ:(i + 1) * SEQ], b_bias[:, i * SEQ:(i + 1) * SEQ], C("ninf"), ALU.add)
            did(last)
            did(v.memset(b_att[:, 0:1024], 0.0))
            for i in range(4):
                t = plan["z"][1].at(i)
                split_to(plan["z"][0] + i // 2 + 1)
                mine(t)
                e = b_e[:, i * SEQ:(i + 1) * SEQ]
                k = b_kf[:, i * SEQ:(i + 1) * SEQ]
                did(v.tensor_scalar(k, k, small[:, 244 + i:245 + i], None, ALU.mult))
                a = v.tensor_scalar(e, e, small[:, 244 + i:245 + i], small[:, 240 + i:241 + i], ALU.mult, ALU.add)
            a.then_inc(hg_arg, 1)
            split_to(plan["hq"][0] + 2)
            dve.wait_ge(hg_ln, 1)
            then(v.tensor_copy(b_e, b_b))
            for i in range(4):
                did(v.tensor_tensor_scan(b_b[:, i * SEQ:(i + 1) * SEQ], C("reset_h"), b_e[:, i * SEQ:(i + 1) * SEQ],
                                         0.0, ALU.mult, ALU.add))
            own()
            dve.wait_ge(levels_in, 16)

            def merge(n):
                for p in range(2):
                    t = plan["lvl"].at(2 * n + p)
                    bank = filled(t)
                    mask = b_lv[:, n * P:(n + 1) * P].bitcast(U32).rearrange("p (a s) -> p a s", a=1).to_broadcast([P, 4, P])
                    v.copy_predicated(b_att[:, p * 512:(p + 1) * 512].rearrange("p (a s) -> p a s", a=4), mask,
                                      bank[:, :].rearrange("p (a s) -> p a s", a=4)).then_inc(evac[t[0]], 1)

            for n in range(8):
                half = LEVELS[n] if n < 7 else P
                b3 = b_b.rearrange("p (g e s) -> p g e s", e=2, s=half)
                d3 = b_e.rearrange("p (g e s) -> p g e s", e=2, s=half)
                G = 4 * SEQ // (2 * half)
                ref = b3[:, :, 0, half - 1:half].to_broadcast([P, G, half])
                did(v.tensor_tensor(d3[:, :, 0, :], ref, b3[:, :, 0, :], ALU.subtract))
                if n < 7:
                    last = v.tensor_tensor(d3[:, :, 1, :], b3[:, :, 1, :], ref, ALU.subtract)
                else:
                    last = v.tensor_copy(d3[:, :, 1, :], b3[:, :, 1, :])
                last.then_inc(lvl_in, 1)
                split_to(plan["ga"][0] + n + 2)
                if n:
                    t = plan["lvl"].at(2 * (n - 1) + 1)
                    filled(t)
                dve.wait_ge(lvl_exp, n + 1)
                q3, k3, w3 = (x.rearrange("p (g e s) -> p g e s", e=2, s=half) for x in (b_q, b_kf, b_qk))
                if n == 0:
                    mine(plan["hq"][1].at(3))
                did(v.tensor_tensor(w3[:, :, 0, :], k3[:, :, 0, :], d3[:, :, 0, :], ALU.mult))
                v.tensor_tensor(w3[:, :, 1, :], q3[:, :, 1, :], d3[:, :, 1, :], ALU.mult).then_inc(lvl_ready, 1)
                dve.wait_ge(lvl_ready, n + 1)
                if n:
                    merge(n - 1)
                    mine(plan["lvl"].at(2 * (n - 1) + 1))
            split_to(plan["hgate"][0] + 2)
            merge(7)
            split_to(plan["hi"][0])
            t = plan["cross"].at(0)
            v.tensor_copy(b_att[:, 1024:1536], filled(t)[:, :]).then_inc(evac[t[0]], 1)
            dve.wait_ge(rows_in, 16)
            for name, dst, at in (("hi", b_v, 0), ("mv", b_mv, 512)):
                for j in range(2):
                    split_to(plan[name][0] + j + 1)
                    for p in range(2):
                        t = plan[name][1].at(2 * j + p)
                        v.tensor_tensor(dst[:, p * 512 + j * 256:p * 512 + (j + 1) * 256], filled(t)[:, 0:256],
                                        b_rows[:, at + j * 256:at + (j + 1) * 256], ALU.add).then_inc(evac[t[0]], 1)
            for i in range(4):
                t = plan["hst"].at(i)
                v.tensor_scalar(b_e[:, i * SEQ:(i + 1) * SEQ], filled(t)[:, 0:SEQ], 1.0 / P, LN_EPS, ALU.mult, ALU.add)\
                    .then_inc(evac[t[0]], 1)

            def finish_head(i):
                r = b_e[:, i * SEQ:(i + 1) * SEQ]
                stds[0] += 1
                dve.wait_ge(std_made, stds[0])
                then(v.reciprocal(r, r))
                mine(plan["hgate"][1].at(i))
                o = b_a[:, i * SEQ:(i + 1) * SEQ]
                then(v.scalar_tensor_tensor(o, o, W("hg_norm", i, i + 1), r, ALU.mult, ALU.mult))
                then(v.tensor_tensor(o, o, b_sg[:, i * SEQ:(i + 1) * SEQ], ALU.mult))
                to_x(i, o, SEQ)

            def moba_bias(g, u):
                head = 2 * g + u % 2
                return b_bias[:, head * SEQ + P:(head + 1) * SEQ] if u < 2 else b_bias[:, head * SEQ:(head + 1) * SEQ]

            attend(("bs",), 4, 8, b_p, SEQ, (P, SEQ), moba_bias, False, finish_head)
            for m in range(4):
                mine(plan["bv"].at(m))
                to_x(4 + m, b_bo[:, m * SEQ:(m + 1) * SEQ], SEQ)

            for i in range(KT):
                split_to(plan["pa"][0] + i // 4 + 1)
                t = plan["pa"][1].at(i)
                v.tensor_tensor(tile(zg, i, SEQ), filled(t)[:, 0:SEQ], tile(b_sga, i, SEQ), ALU.mult)\
                    .then_inc(evac[t[0]], 1)
            for i in range(KT):
                split_to(plan["pb"][0] + i // 4 + 1)
                t = plan["pb"][1].at(i)
                gate = b_sgb[:, i * SEQ:(i + 1) * SEQ]
                v.tensor_tensor(gate, filled(t)[:, 0:SEQ], gate, ALU.mult).then_inc(evac[t[0]], 1)
                mine(t)
                did(v.tensor_tensor(tile(zg, i, SEQ), tile(zg, i, SEQ), gate, ALU.add))
            own()
            for i in range(KT):
                to_x(i, tile(zg, i, SEQ), SEQ)
            for i in range(KT):
                split_to(plan["wo"][0] + i // 2 + 1)
                t = plan["wo"][1].at(i)
                v.scalar_tensor_tensor(tile(h, i, SEQ), tile(h, i, SEQ), ALPHA, filled(t)[:, 0:SEQ], ALU.mult, ALU.add)\
                    .then_inc(evac[t[0]], 1)
            mine(t)
            h3 = h[:, :].rearrange("p (m t) -> p m t", m=KT)[:, :, 0:SEQ]
            ht = h[:, :].rearrange("p (m t) -> p t m", m=KT)[:, 0:SEQ, :]
            zt = zg[:, :].rearrange("p (m t) -> p t m", m=KT)[:, 0:SEQ, :]

            def over_tiles(x):
                return x.rearrange("p (a t) -> p a t", a=1).to_broadcast([P, KT, SEQ])

            v.tensor_reduce(acc[:, 0:SEQ], ht, AX, ALU.add).then_inc(ln_in, 1)
            t = plan["mean"].at(0)
            v.tensor_scalar(var[:, 0:SEQ], filled(t)[:, 0:SEQ], 1.0 / D, None, ALU.mult).then_inc(evac[t[0]], 1)
            mine(t)
            v.tensor_tensor(h3, h3, over_tiles(var[:, 0:SEQ]), ALU.subtract).then_inc(centred, 1)
            dve.wait_ge(centred, 1)
            dve.wait_ge(ln_squared, 1)
            v.tensor_reduce(acc[:, 0:SEQ], zt, AX, ALU.add).then_inc(ln_in, 1)
            inverse_root(plan["lnvar"].at(0), SEQ, D, LN_EPS, var[:, 0:SEQ], std[:, 0:SEQ], rs[:, 0:SEQ])
            then(v.tensor_tensor(h3, h3, over_tiles(rs[:, 0:SEQ]), ALU.mult))
            for m in range(KT):
                v.tensor_scalar(tile(h, m, SEQ), tile(h, m, SEQ), W("ln1_g", m, m + 1), W("ln1_b", m, m + 1),
                                ALU.mult, ALU.add).then_inc(x2_ready, 1)

            def two(x):
                return x.rearrange("p (a n) -> p a n", a=2)

            def spread(col, n):
                return col.rearrange("p (a n) -> p a n", n=1).to_broadcast([P, 2, n])

            def first_max(x, n, top, tmp, one):
                then(v.tensor_reduce(top, two(x), AX, ALU.max))
                then(v.tensor_tensor(two(tmp), two(x), spread(top, n), ALU.is_equal))
                places = C("iota32", 0, n).rearrange("p (a n) -> p a n", a=1).to_broadcast([P, 2, n])
                then(v.scalar_tensor_tensor(two(tmp), two(tmp), -64.0, places, ALU.mult, ALU.add))
                then(v.tensor_reduce(r_["place"], two(tmp), AX, ALU.min))
                then(v.tensor_tensor(two(one), two(tmp), spread(r_["place"], n), ALU.is_equal))

            t = plan["route"].at(0)
            bank = filled(t)
            lg = r_["lg"]
            v.tensor_tensor(two(lg), bank[:, 0:128].rearrange("p (a n) -> p a n", a=2)[:, :, 0:36],
                            W("b_route").rearrange("p (a n) -> p a n", a=1).to_broadcast([P, 2, 36]), ALU.add)\
                .then_inc(evac[t[0]], 1)
            mine(t)
            did(v.tensor_copy(two(r_["gl"]), two(lg)[:, :, 0:4]))
            then(v.tensor_copy(two(r_["em"]), two(lg)[:, :, 4:36]))
            first_max(r_["gl"], 4, r_["gtop"], r_["gt"], r_["g1"])
            v.tensor_tensor(two(r_["ge"]), two(r_["gl"]), spread(r_["gtop"], 4), ALU.subtract).then_inc(route_in, 1)
            then(v.tensor_scalar(r_["g1"], r_["g1"], -NEG, NEG, ALU.mult, ALU.add))
            e3 = r_["em"].rearrange("p (a n) -> p a n", n=8)
            then(v.tensor_tensor(e3, e3, r_["g1"].rearrange("p (a n) -> p a n", n=1).to_broadcast([P, 8, 8]), ALU.add))
            first_max(r_["em"], 32, r_["top1"], r_["tmp"], r_["o1"])
            then(v.scalar_tensor_tensor(r_["em"], r_["o1"], 3 * NEG, r_["em"], ALU.mult, ALU.add))
            first_max(r_["em"], 32, r_["top2"], r_["tmp"], r_["o2"])
            v.tensor_tensor(m_r[:, 0:64], r_["o1"], r_["o2"], ALU.add).then_inc(m_ready, 1)
            v.tensor_tensor(r_["ev"], r_["top2"], r_["top1"], ALU.subtract).then_inc(route_in, 1)
            dve.wait_ge(route_exp, 1)
            then(v.tensor_reduce(r_["pg"], two(r_["ge"]), AX, ALU.add))
            then(v.reciprocal(r_["pg"], r_["pg"]))
            dve.wait_ge(route_exp, 2)
            then(v.tensor_scalar(r_["w1"], r_["ev"], 1.0, None, ALU.add))
            then(v.reciprocal(r_["w1"], r_["w1"]))
            then(v.tensor_tensor(r_["w1"], r_["w1"], r_["pg"], ALU.mult))
            then(v.tensor_tensor(r_["w2"], r_["w1"], r_["ev"], ALU.mult))
            t = plan["cnt"].at(0)
            v.tensor_copy(r_["cnt"], filled(t)[:, 0:32]).then_inc(evac[t[0]], 1)
            mine(t)
            then(v.tensor_scalar(r_["nb"], r_["cnt"], 0.0, None, ALU.is_gt))
            for j in range(1, SEQ // SLOTS):
                then(v.scalar_tensor_tensor(r_["nb"], r_["cnt"], float(SLOTS * j), r_["nb"], ALU.is_gt, ALU.add))
            then(v.scalar_tensor_tensor(r_["nb"], C("iota32"), 2.0, r_["nb"], ALU.is_lt, ALU.max))
            then(v.tensor_tensor_scan(r_["end"], C("ones", 0, 32), r_["nb"], 0.0, ALU.mult, ALU.add))
            then(v.tensor_tensor(r_["beg"], r_["end"], r_["nb"], ALU.subtract))
            then(v.tensor_scalar(r_["beg"], r_["beg"], float(SLOTS), None, ALU.mult))
            cmp3 = r_["cmp"][0:1, :].rearrange("p (b e) -> p b e", e=32)
            then(v.tensor_tensor(cmp3, r_["end"][0:1, :].rearrange("p (a e) -> p a e", a=1).to_broadcast([1, MAXB, 32]),
                                 C("iotab", 0, MAXB, slice(0, 1)).rearrange("p (b a) -> p b a", a=1).to_broadcast([1, MAXB, 32]),
                                 ALU.is_le))
            then(v.tensor_reduce(r_["eb"][0:1, :], cmp3, AX, ALU.add))
            then(v.tensor_scalar(meta_i[0:1, 0:MAXB], r_["eb"][0:1, :], float(NE - 1), None, ALU.min))
            pairs = r_["cmp"][0:1, 0:MAXB]
            then(v.tensor_scalar(pairs, C("iotab", 0, MAXB, slice(0, 1)), 2.0, None, ALU.mult))
            then(v.tensor_tensor(pairs, pairs, r_["end"][0:1, 31:32].to_broadcast([1, MAXB]), ALU.is_lt))
            then(v.tensor_reduce(r_["place"][0:1, 0:1], pairs, AX, ALU.add))
            then(v.tensor_copy(meta_i[0:1, MAXB:MAXB + 1], r_["place"][0:1, 0:1]))
            t = plan["pos"].at(0)
            bank = filled(t)
            v.tensor_tensor(two(r_["em"]), two(bank[:, 0:64]),
                            r_["beg"].rearrange("p (a n) -> p a n", a=1).to_broadcast([P, 2, 32]), ALU.add)\
                .then_inc(evac[t[0]], 1)
            mine(t)
            for k, one in ((0, "o1"), (1, "o2")):
                then(v.tensor_tensor(r_["tmp"], r_["em"], r_[one], ALU.mult))
                then(v.tensor_reduce(r_["dest"][:, 2 * k:2 * k + 2], two(r_["tmp"]), AX, ALU.add))
            did(v.memset(m_zero, 0.0))
            did(v.tensor_scalar(m_pT, cst[:, 0:2 * P], 0.0, None, ALU.mult))
            did(v.tensor_scalar(m_y[0], cst[:, 0:512], 0.0, None, ALU.mult))
            v.tensor_scalar(m_y[1], cst[:, 0:512], 0.0, None, ALU.mult).then_inc(table_ready, 1)

            def col(x, i):
                return r_[x][:, i:i + 1]

            def choose():
                for p in range(2):
                    e = v.tensor_scalar(m_t[:, p * 64:(p + 1) * 64], C("iota"), col("dest", p), None, ALU.is_equal)
                return e

            def choose_2():
                for p in range(2):
                    e = v.scalar_tensor_tensor(m_P[:, p * 64:(p + 1) * 64], C("iota"), col("dest", 2 + p),
                                               m_t[:, p * 64:(p + 1) * 64], ALU.is_equal, ALU.add)
                return e

            def weigh():
                for p in range(2):
                    v.tensor_scalar(m_t[:, 128 + p * 64:192 + p * 64], C("iota"), col("dest", p), col("w1", p),
                                    ALU.is_equal, ALU.mult)
                    e = v.tensor_scalar(m_t[:, 256 + p * 64:320 + p * 64], C("iota"), col("dest", 2 + p), col("w2", p),
                                        ALU.is_equal, ALU.mult)
                return e

            def weigh_2():
                for p in range(2):
                    a, b = (m_t[:, x + p * 64:x + 64 + p * 64].rearrange("p (a s) -> p a s", a=1).to_broadcast([P, 2, 64])
                            for x in (128, 256))
                    v.tensor_tensor(m_PW[:, p * P:(p + 1) * P].rearrange("p (a s) -> p a s", a=2), a, b, ALU.add)
                    chosen = m_P[:, p * 64:(p + 1) * 64].rearrange("p (a s) -> p a s", a=1).to_broadcast([P, 2, 64])
                    e = v.tensor_copy(m_PP[:, p * P:(p + 1) * P].rearrange("p (a s) -> p a s", a=2), chosen)
                return e

            def move_on():
                return v.tensor_scalar(r_["dest"], r_["dest"], -float(SLOTS), None, ALU.add)

            choose().then_inc(parts_made, 1)
            dve.wait_ge(parts_made, 1)
            choose_2().then_inc(p_made, 1)
            weigh().then_inc(parts_made, 1)
            dve.wait_ge(parts_made, 2)
            weigh_2().then_inc(pw_made, 1)
            dve.wait_ge(pw_made, 1)
            move_on().then_inc(moved, 1)
            n_pairs = dve.value_load(meta_i[0:1, MAXB:MAXB + 1], min_val=4, max_val=MAXB // 2)
            with dve.Fori(0, n_pairs) as pair:
                for s in range(2):
                    b = 2 * pair + s
                    dve.wait_ge(moved, b + 1)
                    choose().then_inc(parts_made, 1)
                    dve.wait_ge(parts_made, 2 * b + 3)
                    dve.wait_ge(full[4], E_BASE[4] + b)
                    choose_2().then_inc(p_made, 1)
                    weigh().then_inc(parts_made, 1)
                    dve.wait_ge(silu_made, b + 1)
                    v.tensor_tensor(m_h, ps[5][:, 256:512], m_sg, ALU.mult).then_inc(evac[5], 1)
                    dve.wait_ge(pw_turned, b + 1)
                    v.tensor_copy(m_w[:, 0:1], ps[7][:, 0:1]).then_inc(w_taken, 1)
                    dve.wait_ge(parts_made, 2 * b + 4)
                    dve.wait_ge(p_made, b + 2)
                    weigh_2().then_inc(pw_made, 1)
                    dve.wait_ge(pw_made, b + 2)
                    move_on().then_inc(moved, 1)
                    dve.wait_ge(w_taken, b + 1)
                    dve.wait_ge(full[7], E_BASE[7] + b + 1)
                    v.tensor_scalar(m_y[0], ps[7][:, :], m_w[:, 0:1], None, ALU.mult).then_inc(yhi_made, 1)
                    dve.wait_ge(yhi_made, b + 1)
                    v.scalar_tensor_tensor(m_y[1], ps[7][:, :], m_w[:, 0:1], m_y[0].bitcast(F32), ALU.mult, ALU.subtract)\
                        .then_inc(evac[7], 1)

            dve.wait_ge(y_done, 1)
            for p in range(2):
                for n in range(2):
                    o = m_o[:, p * D + n * 512:p * D + (n + 1) * 512]
                    did(v.scalar_tensor_tensor(o, m_x[:, p * D + n * 512:p * D + (n + 1) * 512], ALPHA,
                                               ps[2 * p + n][:, :], ALU.mult, ALU.add))
            own()
            then(v.tensor_reduce(small[:, 96:98], two(m_o), AX, ALU.add))
            then(v.tensor_scalar(small[:, 96:98], small[:, 96:98], -1.0 / D, None, ALU.mult))
            for p in range(2):
                o = m_o[:, p * D:(p + 1) * D]
                v.tensor_scalar(o, o, small[:, 96 + p:97 + p], None, ALU.add).then_inc(fin_centred, 1)
            dve.wait_ge(fin_squared, 2)
            v.tensor_scalar(small[:, 102:104], small[:, 100:102], 1.0 / D, LN_EPS, ALU.mult, ALU.add).then_inc(fin_var, 1)
            dve.wait_ge(fin_std, 1)
            then(v.reciprocal(small[:, 106:108], small[:, 104:106]))
            dve.wait_ge(ln2_in, 32)
            dve.wait_ge(fin_centred, 2)
            for p in range(2):
                o = m_o[:, p * D:(p + 1) * D]
                then(v.scalar_tensor_tensor(o, o, small[:, 106 + p:107 + p], m_g, ALU.mult, ALU.mult))
                v.tensor_tensor(o, o, m_b, ALU.add).then_inc(out_ready, 1)


def kernel(x, meta_tokens, norm_gains, w_ffn_in, w_ffn_out, gla_w_in, gla_w_gate, gla_b_gate, gla_norm, gla_w_out,
           kv_norm, w_kv, swa_w_q, swa_sinks, swa_w_out, w_in_2, b_in_2, lb_logits_2, hg_norm_g_2, rel_bias_2,
           w_proj_a_2, w_proj_b_2, w_out_2, ln1_g_2, ln1_b_2, w_group_2, b_group_2, w_expert_2, b_expert_2,
           w_gate_up_2, w_down_2, ln2_g_2, ln2_b_2):
    import concourse.bacc as bacc
    from concourse.bass_utils import run_bass_kernel_spmd

    f = np.float32
    a = {k: np.asarray(v) for k, v in locals().items() if k not in ("bacc", "run_bass_kernel_spmd", "f")}

    def by_feature(w):
        n = w.shape[1] // 256
        return w.reshape(KT, P, n, 2, P).transpose(2, 1, 3, 0, 4).reshape(n, P, UNIT)

    def by_token(w):
        n = w.shape[1] // 256
        return w.reshape(KT, P, n, 256).transpose(2, 1, 0, 3).reshape(n, P, UNIT)

    def short(w):
        return w.reshape(4, P, 2, 4, P).transpose(2, 1, 3, 0, 4).reshape(2, P, UNIT)

    def ffn_in(w):
        return by_feature(np.stack([w[:, :FF].reshape(D, FT, P), w[:, FF:].reshape(D, FT, P)], axis=2).reshape(D, 2 * FF))

    order = np.array([(t * 8 + half * 4 + i) * 64 + d for t in range(2) for i in range(4) for half in range(2)
                      for d in range(64)])
    g = a["gla_w_in"][0]
    w2 = a["w_in_2"][0]
    kv = a["w_kv"]
    fi = a["w_ffn_in"]
    cut = {"q": (0, 512), "z": (512, 1024), "i": (1024, 1536), "g": (1536, 2048), "mq": (2048, 2560),
           "mk": (2560, 3072), "mv": (3072, 3584), "ga": (3584, 4608), "gb": (4608, 5632)}
    sec = {k: w2[:, s:e] for k, (s, e) in cut.items()}
    w_units = np.concatenate([
        ffn_in(fi[0, 0]), by_feature(g[:, 2048:3072]), by_token(g[:, 1024:2048]), by_feature(g[:, 512:1024]),
        by_feature(g[:, 0:512]), by_feature(a["gla_w_out"][0]), ffn_in(fi[0, 1]), by_feature(kv[:, :256]),
        by_token(kv[:, 256:]), ffn_in(fi[1, 0]), by_feature(a["swa_w_q"][0][:, order]),
        by_feature(a["swa_w_out"][0][order]), ffn_in(fi[1, 1]),
        by_feature(sec["z"]), by_feature(sec["q"]), by_feature(sec["ga"]), by_feature(sec["gb"]), by_feature(sec["g"]),
        by_feature(sec["mq"]), by_feature(sec["mk"]), by_token(sec["i"]), by_token(sec["mv"]),
        short(a["w_proj_a_2"][0]), short(a["w_proj_b_2"][0]), by_feature(a["w_out_2"][0])])
    w_out_units = a["w_ffn_out"].reshape(4, FT, P, KT, P).transpose(0, 3, 2, 1, 4).reshape(4 * KT, P, OUT_UNIT)
    tokens = np.concatenate([a["x"][0], a["meta_tokens"]])
    xT = tokens.reshape(TA, KT, P).transpose(2, 1, 0).reshape(P, KT * TA)

    def cols(vec):
        return vec.reshape(-1, P).T

    table, levels = constants()
    par = {k: np.zeros((P, n), f) for k, (_, n) in P_COLS.items()}
    par["gains"][:] = cols(a["norm_gains"].reshape(-1))
    par["kv_norm"][:] = cols(a["kv_norm"])
    par["b_gate"][:] = cols(a["gla_b_gate"][0])
    par["gla_norm"][:] = cols(a["gla_norm"][0])
    par["w_lr"][:] = g[:, 3072:].reshape(KT, P, RANK).transpose(1, 0, 2).reshape(P, -1)
    par["w_gate"][:RANK] = a["gla_w_gate"][0]
    par["b_in"][:] = cols(a["b_in_2"][0])
    par["lb_logits"][:] = cols(a["lb_logits_2"].reshape(-1))
    par["hg_norm"][:] = cols(a["hg_norm_g_2"][0])
    par["ln1_g"][:] = cols(a["ln1_g_2"][0])
    par["ln1_b"][:] = cols(a["ln1_b_2"][0])
    wr = np.concatenate([a["w_group_2"][0], a["w_expert_2"][0]], axis=1)
    par["w_route"][:] = wr.reshape(KT, P, 36).transpose(1, 0, 2).reshape(P, -1)
    par["b_route"][:] = np.concatenate([a["b_group_2"][0], a["b_expert_2"][0]])[None]
    par["rel_bias"][:32] = a["rel_bias_2"]
    heads = [t * 8 + half * 4 + i for t in range(2) for i in range(4) for _ in range(2) for half in range(2)]
    par["sinks"][:] = a["swa_sinks"][0][heads][None]
    params = np.concatenate([par[k] for k in P_COLS], axis=1)
    b2 = a["b_in_2"][0]
    rows = np.ascontiguousarray(np.broadcast_to(
        np.concatenate([b2[1024:1536], b2[3072:3584], a["ln2_g_2"][0], a["ln2_b_2"][0]]), (P, 3072)))

    nc = bacc.Bacc("TRN2", target_bir_lowering=False, num_devices=1)
    arrays = {"xT": xT, "w_units": w_units, "w_out_units": w_out_units, "w_gate_up": a["w_gate_up_2"][0],
              "w_down": a["w_down_2"][0], "table": table, "levels": levels, "params": params, "rows": rows}
    arrays = {k: np.ascontiguousarray(v) for k, v in arrays.items()}
    aps = [nc.dram_tensor(k, v.shape, mybir.dt.from_np(v.dtype), kind="ExternalInput").ap() for k, v in arrays.items()]
    out = nc.dram_tensor("out", (1, SEQ, D), F32, kind="ExternalOutput").ap()
    two_blocks(nc, *aps, out)
    r = run_bass_kernel_spmd(nc, [arrays], core_ids=[0])
    return r.results[0]["out"]
```
